# Optimizing a Trainium2 kernel written in Bass

```python
import jax
import jax.numpy as jnp
from jax import lax
import numpy as np

D_MODEL = 1024
BATCH = 1
SEQ = 512
DEPTH = 1

MIX_WIDTH = D_MODEL
ATTN_WIDTH = MIX_WIDTH // 2
ATTN_HEAD_DIM = 64
ATTN_HEADS = ATTN_WIDTH // ATTN_HEAD_DIM
DILATED_PATTERNS = ((128, 1), (512, 4), (2048, 16))
MLSTM_WIDTH = MIX_WIDTH - ATTN_WIDTH
MLSTM_HEADS = 4
MLSTM_HEAD_DIM = MLSTM_WIDTH // MLSTM_HEADS
MLSTM_CONV = 4
MLSTM_CHUNK = 128
PEER_HEADS = 8
PEER_N_KEYS = 128
PEER_N_EXPERTS = PEER_N_KEYS * PEER_N_KEYS
PEER_KEY_DIM = 256
PEER_TOPK = 16
PEER_TOKEN_BLOCK = 128
DEEPNORM_ALPHA = (2.0 * DEPTH) ** 0.25
DEEPNORM_BETA = (8.0 * DEPTH) ** -0.25
LN_EPS = 1e-5
IN_SIZES = (ATTN_WIDTH, ATTN_WIDTH, ATTN_WIDTH, MLSTM_WIDTH, MLSTM_WIDTH, MLSTM_WIDTH, 2 * MLSTM_HEADS)
IN_COLS = sum(IN_SIZES)
SPLIT_POINTS = tuple(int(s) for s in np.cumsum(IN_SIZES)[:-1])

kernel_name = "hymba_dilated_mlstm_peer_deepnorm"

def _layer_norm(x, g, b):
    xf = x.astype(jnp.float32)
    mu = jnp.mean(xf, axis=-1, keepdims=True)
    var = jnp.mean(jnp.square(xf - mu), axis=-1, keepdims=True)
    y = (xf - mu) * lax.rsqrt(var + LN_EPS)
    return (y * g.astype(jnp.float32) + b.astype(jnp.float32)).astype(x.dtype)

def _dilated_branch(q, k, v, window, dilation):
    B, S, H, E = q.shape
    steps = window // dilation
    L = S // dilation
    n_blk = -(-L // steps)
    pad = n_blk * steps - L

    def to_sub(t):
        return t.reshape(B, L, dilation, H, E).transpose(0, 2, 3, 1, 4)

    qb = jnp.pad(to_sub(q), ((0, 0), (0, 0), (0, 0), (0, pad), (0, 0))).reshape(B, dilation, H, n_blk, steps, E)
    kp = jnp.pad(to_sub(k), ((0, 0), (0, 0), (0, 0), (steps, pad), (0, 0))).reshape(B, dilation, H, n_blk + 1, steps, E)
    vp = jnp.pad(to_sub(v), ((0, 0), (0, 0), (0, 0), (steps, pad), (0, 0))).reshape(B, dilation, H, n_blk + 1, steps, E)
    kb = jnp.concatenate([kp[:, :, :, :-1], kp[:, :, :, 1:]], axis=4)
    vb = jnp.concatenate([vp[:, :, :, :-1], vp[:, :, :, 1:]], axis=4)
    s = jnp.einsum('bghnqe,bghnke->bghnqk', qb, kb) * (E ** -0.5)
    qpos = jnp.arange(n_blk)[:, None] * steps + jnp.arange(steps)[None, :]
    kpos = jnp.arange(n_blk)[:, None] * steps - steps + jnp.arange(2 * steps)[None, :]
    dist = qpos[:, :, None] - kpos[:, None, :]
    mask = (dist >= 0) & (dist <= steps) & (kpos[:, None, :] >= 0)
    s = jnp.where(mask, s, -jnp.inf)
    m = jnp.max(s, axis=-1)
    p = jnp.exp(s - m[..., None])
    l = jnp.sum(p, axis=-1)
    acc = jnp.einsum('bghnqk,bghnke->bghnqe', p, vb)

    def from_sub(t):
        rest = t.shape[5:]
        t = t.reshape((B, dilation, H, n_blk * steps) + rest)[:, :, :, :L]
        perm = (0, 3, 1, 2) + tuple(range(4, 4 + len(rest)))
        return t.transpose(perm).reshape((B, S, H) + rest)

    return from_sub(acc), from_sub(m), from_sub(l)

def _dilated_attention(q, k, v):
    branches = [_dilated_branch(q, k, v, w, d) for (w, d) in DILATED_PATTERNS]
    m_all = jnp.max(jnp.stack([b[1] for b in branches]), axis=0)
    num = 0.0
    den = 0.0
    for acc, m, l in branches:
        e = jnp.exp(m - m_all)
        num = num + acc * e[..., None]
        den = den + l * e
    return num / den[..., None]

def _mlstm_chunkwise(q, k, v, i_pre, logf):
    B, S, H, E = q.shape
    NC = S // MLSTM_CHUNK
    CH = MLSTM_CHUNK

    def chunks(t):
        return t.reshape(B, NC, CH, H, E).transpose(1, 0, 3, 2, 4)

    def gchunks(t):
        return t.reshape(B, NC, CH, H).transpose(1, 0, 3, 2)

    bcum = jnp.cumsum(gchunks(logf), axis=-1)
    tril = jnp.tril(jnp.ones((CH, CH), dtype=bool))

    def step(carry, xs):
        C, n, m = carry
        qc, kc, vc, ic, bc = xs
        dlog = jnp.where(tril, bc[..., :, None] - bc[..., None, :] + ic[..., None, :], -jnp.inf)
        m_inter = bc + m[..., None]
        m_t = jnp.maximum(m_inter, jnp.max(dlog, axis=-1))
        w_inter = jnp.exp(m_inter - m_t)
        P = jnp.exp(dlog - m_t[..., None]) * jnp.einsum('bhte,bhse->bhts', qc, kc)
        num = w_inter[..., None] * jnp.einsum('bhvk,bhtk->bhtv', C, qc) + jnp.einsum('bhts,bhsv->bhtv', P, vc)
        den = w_inter * jnp.einsum('bhtk,bhk->bht', qc, n) + jnp.sum(P, axis=-1)
        h = num / jnp.maximum(jnp.abs(den), jnp.exp(-m_t))[..., None]
        bL = bc[..., -1]
        g = bL[..., None] - bc + ic
        m_new = jnp.maximum(bL + m, jnp.max(g, axis=-1))
        a = jnp.exp(bL + m - m_new)
        wk = jnp.exp(g - m_new[..., None])
        C_new = a[..., None, None] * C + jnp.einsum('bhs,bhsv,bhsk->bhvk', wk, vc, kc)
        n_new = a[..., None] * n + jnp.einsum('bhs,bhsk->bhk', wk, kc)
        return (C_new, n_new, m_new), h

    init = (jnp.zeros((B, H, E, E), jnp.float32), jnp.zeros((B, H, E), jnp.float32), jnp.zeros((B, H), jnp.float32))
    _, hs = lax.scan(step, init, (chunks(q), chunks(k), chunks(v), gchunks(i_pre), bcum))
    return hs.transpose(1, 0, 3, 2, 4).reshape(B, S, H, E)

def _mlstm_mixer(x_m, v_m, o_m, gates, conv_w, conv_b, w_mq, w_mk, b_igate, b_fgate, mh_norm_g):
    B, S, _ = x_m.shape
    H, E = MLSTM_HEADS, MLSTM_HEAD_DIM
    xc = lax.conv_general_dilated(x_m, conv_w[:, None, :], window_strides=(1,), padding=((MLSTM_CONV - 1, 0),),
                                  dimension_numbers=('NWC', 'WIO', 'NWC'), feature_group_count=MLSTM_WIDTH) + conv_b
    xc = jax.nn.silu(xc).reshape(B, S, H, E)
    q = jnp.einsum('bshe,hef->bshf', xc, w_mq).astype(jnp.float32) * (E ** -0.5)
    k = jnp.einsum('bshe,hef->bshf', xc, w_mk).astype(jnp.float32)
    v = v_m.reshape(B, S, H, E).astype(jnp.float32)
    g = gates.astype(jnp.float32)
    i_pre = g[..., :H] + b_igate.astype(jnp.float32)
    logf = jax.nn.log_sigmoid(g[..., H:] + b_fgate.astype(jnp.float32))
    ht = _mlstm_chunkwise(q, k, v, i_pre, logf)
    mu = jnp.mean(ht, axis=-1, keepdims=True)
    var = jnp.mean(jnp.square(ht - mu), axis=-1, keepdims=True)
    hn = ((ht - mu) * lax.rsqrt(var + LN_EPS)).reshape(B, S, MLSTM_WIDTH) * mh_norm_g.astype(jnp.float32)
    out = jax.nn.sigmoid(o_m.astype(jnp.float32)) * hn
    return out.astype(x_m.dtype)

def _token_mixing(h, w_in, conv_w, conv_b, w_mq, w_mk, b_igate, b_fgate, mh_norm_g, w_out):
    B, S, _ = h.shape
    proj = h @ w_in
    q_a, k_a, v_a, x_m, v_m, o_m, gates = jnp.split(proj, SPLIT_POINTS, axis=-1)
    shp = (B, S, ATTN_HEADS, ATTN_HEAD_DIM)
    attn = _dilated_attention(q_a.reshape(shp).astype(jnp.float32), k_a.reshape(shp).astype(jnp.float32),
                              v_a.reshape(shp).astype(jnp.float32))
    attn = attn.reshape(B, S, ATTN_WIDTH).astype(h.dtype)
    mlstm = _mlstm_mixer(x_m, v_m, o_m, gates, conv_w, conv_b, w_mq, w_mk, b_igate, b_fgate, mh_norm_g)
    return jnp.concatenate([attn, mlstm], axis=-1) @ w_out

def _peer(h, w_query, sub_keys, w_down, w_up):
    B, S, D = h.shape
    T = B * S
    xt = h.reshape(T, D)
    qry = (xt @ w_query).reshape(T, PEER_HEADS, 2, PEER_KEY_DIM // 2).astype(jnp.float32)
    sc = jnp.einsum('thpc,hpkc->thpk', qry, sub_keys.astype(jnp.float32))
    v1, i1 = lax.top_k(sc[:, :, 0], PEER_TOPK)
    v2, i2 = lax.top_k(sc[:, :, 1], PEER_TOPK)
    cand = (v1[..., :, None] + v2[..., None, :]).reshape(T, PEER_HEADS, PEER_TOPK * PEER_TOPK)
    cidx = (i1[..., :, None] * PEER_N_KEYS + i2[..., None, :]).reshape(T, PEER_HEADS, PEER_TOPK * PEER_TOPK)
    best, pos = lax.top_k(cand, PEER_TOPK)
    eidx = jnp.take_along_axis(cidx, pos, axis=-1).reshape(T, PEER_HEADS * PEER_TOPK)
    gate = jax.nn.softmax(best, axis=-1).reshape(T, PEER_HEADS * PEER_TOPK)
    NB = T // PEER_TOKEN_BLOCK

    def expert_block(args):
        xb, ib, gb = args
        u = w_down[ib]
        a = jnp.einsum('tkd,td->tk', u, xb).astype(jnp.float32)
        a = jax.nn.gelu(a, approximate=False) * gb
        vsel = w_up[ib]
        return jnp.einsum('tk,tkd->td', a.astype(vsel.dtype), vsel)

    out = lax.map(expert_block, (xt.reshape(NB, PEER_TOKEN_BLOCK, D),
                                 eidx.reshape(NB, PEER_TOKEN_BLOCK, -1),
                                 gate.reshape(NB, PEER_TOKEN_BLOCK, -1)))
    return out.reshape(B, S, D).astype(h.dtype)

def setup_inputs(seed: int = 0) -> dict:
    key = jax.random.key(seed)
    ks = jax.random.split(key, 24)
    D = D_MODEL
    H, E = MLSTM_HEADS, MLSTM_HEAD_DIM
    nrm = jax.random.normal
    std = D ** -0.5
    x = nrm(ks[0], (BATCH, SEQ, D), jnp.float32)
    w_qk = nrm(ks[1], (DEPTH, D, 2 * ATTN_WIDTH)) * std
    w_va = nrm(ks[2], (DEPTH, D, ATTN_WIDTH)) * std * DEEPNORM_BETA
    w_xm = nrm(ks[3], (DEPTH, D, MLSTM_WIDTH)) * std
    w_vm = nrm(ks[4], (DEPTH, D, MLSTM_WIDTH)) * std * DEEPNORM_BETA
    w_om = nrm(ks[5], (DEPTH, D, MLSTM_WIDTH)) * std
    w_gt = nrm(ks[6], (DEPTH, D, 2 * H)) * std * 0.1
    w_in = jnp.concatenate([w_qk, w_va, w_xm, w_vm, w_om, w_gt], axis=-1)
    conv_w = nrm(ks[7], (DEPTH, MLSTM_CONV, MLSTM_WIDTH)) * (MLSTM_CONV ** -0.5)
    conv_b = nrm(ks[8], (DEPTH, MLSTM_WIDTH)) * 0.02
    w_mq = nrm(ks[9], (DEPTH, H, E, E)) * (E ** -0.5)
    w_mk = nrm(ks[10], (DEPTH, H, E, E)) * (E ** -0.5)
    b_igate = nrm(ks[11], (DEPTH, H)) * 0.1
    b_fgate = jnp.linspace(3.0, 6.0, H)[None, :] + nrm(ks[12], (DEPTH, H)) * 0.1
    mh_norm_g = 1.0 + 0.02 * nrm(ks[13], (DEPTH, MLSTM_WIDTH))
    w_out = nrm(ks[14], (DEPTH, MIX_WIDTH, D)) * (MIX_WIDTH ** -0.5) * DEEPNORM_BETA
    ln1_g = 1.0 + 0.02 * nrm(ks[15], (DEPTH, D))
    ln1_b = 0.02 * nrm(ks[16], (DEPTH, D))
    peer_w_query = nrm(ks[17], (DEPTH, D, PEER_HEADS * PEER_KEY_DIM)) * std
    peer_sub_keys = nrm(ks[18], (DEPTH, PEER_HEADS, 2, PEER_N_KEYS, PEER_KEY_DIM // 2)) * ((PEER_KEY_DIM // 2) ** -0.5)
    peer_w_down = nrm(ks[19], (DEPTH, PEER_N_EXPERTS, D)) * std
    peer_w_up = nrm(ks[20], (DEPTH, PEER_N_EXPERTS, D)) * DEEPNORM_BETA
    ln2_g = 1.0 + 0.02 * nrm(ks[21], (DEPTH, D))
    ln2_b = 0.02 * nrm(ks[22], (DEPTH, D))
    return {"x": x, "w_in": w_in, "conv_w": conv_w, "conv_b": conv_b, "w_mq": w_mq, "w_mk": w_mk,
            "b_igate": b_igate, "b_fgate": b_fgate, "mh_norm_g": mh_norm_g, "w_out": w_out,
            "ln1_g": ln1_g, "ln1_b": ln1_b, "peer_w_query": peer_w_query, "peer_sub_keys": peer_sub_keys,
            "peer_w_down": peer_w_down, "peer_w_up": peer_w_up, "ln2_g": ln2_g, "ln2_b": ln2_b}

def reference(x, w_in, conv_w, conv_b, w_mq, w_mk, b_igate, b_fgate, mh_norm_g, w_out, ln1_g, ln1_b,
              peer_w_query, peer_sub_keys, peer_w_down, peer_w_up, ln2_g, ln2_b):
    h = x
    for l in range(DEPTH):
        mix = _token_mixing(h, w_in[l], conv_w[l], conv_b[l], w_mq[l], w_mk[l], b_igate[l], b_fgate[l],
                            mh_norm_g[l], w_out[l])
        h = _layer_norm(DEEPNORM_ALPHA * h + mix, ln1_g[l], ln1_b[l])
        ffn = _peer(h, peer_w_query[l], peer_sub_keys[l], peer_w_down[l], peer_w_up[l])
        h = _layer_norm(DEEPNORM_ALPHA * h + ffn, ln2_g[l], ln2_b[l])
    return h


_drawn_inputs = setup_inputs


def setup_inputs(seed=0):
    import zlib

    import numpy as np

    out = dict(_drawn_inputs(seed))
    spreads = {}
    factors = {'conv_b': 2.816, 'b_igate': 8.0, 'mh_norm_g': 3.479, 'ln2_g': 2.739, 'ln2_b': 2.828}
    for name, (base, spread) in spreads.items():
        noise = np.random.default_rng([zlib.crc32(name.encode()), seed]).standard_normal(out[name].shape)
        drawn = base * np.exp(spread * noise) if base else spread * noise
        out[name] = jnp.asarray(drawn.astype(out[name].dtype))
    for name, factor in factors.items():
        out[name] = (out[name] * factor).astype(out[name].dtype)
    return out
```

```python
from contextlib import ExitStack

import concourse.bass as bass
from concourse import mybir

F32 = mybir.dt.float32
U32 = mybir.dt.uint32
ALU = mybir.AluOpType
ACT = mybir.ActivationFunctionType
X = mybir.AxisListType.X

P = 128
S = 512
D = 1024
NB = S // P
KD = D // P
W = 512
AH, AE = 8, 64
MH, ME = 4, 128
TAPS = 4
PH, NK, TOPK = 8, 128, 16
ALPHA = 2.0 ** 0.25
EPS = 1e-5
NEG = -1e30
LOWEST = -3e38
RING = 8

GATES = 0
XM, VM, QA, KA = 1, 5, 9, 13
MQ, MK, KM = 17, 21, 25
VA, OM = 29, 33
PROJ_ITEMS = 37
PS0, PS_PER = NB, 1 + AH + 2
PT_PER = 1 + AH + 4
PV_PER = 1 + AH


def build(nc, xT, x, w_in, w_gate, conv, gate_bias, w_mq, w_mk, mh_g, w_out, ln1, w_query, sub_keys,
          w_down, w_up, ln2, consts, out):
    with ExitStack() as ctx:
        def sem(name):
            return ctx.enter_context(nc.semaphore(name))

        def sb(stack, name, shape, dt=F32):
            return stack.enter_context(nc.sbuf_tensor(name, shape, dt))

        pj = [ctx.enter_context(nc.psum_tensor(f"proj{i}", [P, 512], F32)) for i in range(2)]
        ps = [ctx.enter_context(nc.psum_tensor(f"score{i}", [P, 512], F32)) for i in range(2)]
        pt = [ctx.enter_context(nc.psum_tensor(f"turn{i}", [P, 512], F32)) for i in range(2)]
        py = ctx.enter_context(nc.psum_tensor("py", [P, 2, 512], F32))
        po, pi = py[:, 0, :], py[:, 1, :]

        cst = sb(ctx, "cst", [P, 4 * P + 2 * S + 32])
        ident, triu, ones = cst[:, 0:P], cst[:, P:2 * P], cst[:, 2 * P:3 * P]
        tril_bias = cst[:, 3 * P:4 * P]
        attn_bias = cst[:, 4 * P:4 * P + S]
        attn_count = cst[:, 4 * P + S:4 * P + 2 * S]
        iota16 = cst[:, 4 * P + 2 * S:4 * P + 2 * S + 16]
        eps = cst[:, 4 * P + 2 * S + 16:4 * P + 2 * S + 17]
        h1 = sb(ctx, "h1", [P, NB, D])
        stats = sb(ctx, "stats", [P, 4, 6])
        mv = sb(ctx, "mv", [P, 4, 2])
        sd = sb(ctx, "sd", [P, 4])
        rstd = sb(ctx, "rstd", [P, 4])

        early = ExitStack()
        h1T = sb(early, "h1T", [P, KD, S])
        mixing = ExitStack()
        ln1_sb = sb(mixing, "ln1_sb", [P, 2, D])
        mhg = sb(mixing, "mhg", [P, W])
        xT_sb = sb(mixing, "xT_sb", [P, KD, S])
        wp = [sb(mixing, f"wpiece{i}", [P, KD, W]) for i in range(2)]
        wg_sb = sb(mixing, "wg_sb", [P, KD, 2 * MH])
        conv_sb = sb(mixing, "conv_sb", [P, MH, TAPS + 1])
        gbias = sb(mixing, "gbias", [P, 2 * MH])
        xm = sb(mixing, "xm", [P, MH, S + TAPS])
        vm = sb(mixing, "vm", [P, NB, W])
        om = sb(mixing, "om", [P, NB, W])
        qa = sb(mixing, "qa", [P, 4, S])
        ka = sb(mixing, "ka", [P, 4, S])
        va = sb(mixing, "va", [P, NB, W])
        xc = sb(mixing, "xc", [P, MH, S])
        qm = sb(mixing, "qm", [P, MH, S])
        kmT = sb(mixing, "kmT", [P, MH, S])
        km = sb(mixing, "km", [P, NB, MH, ME])
        rm = sb(mixing, "rm", [P, NB, MH, P])
        wmq, wmk = rm[:, 0], rm[:, 1]
        diag_r = xm[:, :, 0:S].rearrange("p c (h s) -> p c h s", h=MH)
        cat = sb(mixing, "cat", [P, D])
        catT = sb(mixing, "catT", [P, KD, P])
        ct = sb(mixing, "ct", [P, MH, ME])
        nst = sb(mixing, "nst", [P, MH])
        sw = [sb(mixing, f"sw{i}", [P, S]) for i in range(2)]
        pT = [sb(mixing, f"pT{i}", [P, S]) for i in range(2)]
        gt = sb(mixing, "gt", [P, NB, 2 * MH])
        sv = sb(mixing, "sv", [P, 20, 16])
        ew = sb(mixing, "ew", [P, 4, 16])
        hv = sb(mixing, "hv", [P, 8, AH])
        ip, ff, nf, lg, logf, bc, bl, rr, rmax, mmax, mxl, mx, nmx, lexp, mn = (
            sv[:, i, :] for i in range(15))
        mprev = sv[:, 15:17, :].rearrange("p a b -> p (a b)")
        w_inter, e_mt, a_dec, w_k = (ew[:, i, :] for i in range(4))
        kw = xc
        mixing.close()

        query = ExitStack()
        scores = sb(query, "scores", [P, NB * PH + 1, 2 * NK])
        wq = [sb(query, f"wq{i}", [P, KD, 2 * NK]) for i in range(2)]
        sk = [sb(query, f"sk{i}", [P, 2, NK]) for i in range(2)]
        qry = [sb(query, f"qry{i}", [P, 2, S]) for i in range(2)]
        query.close()
        early.close()

        peer = ExitStack()
        skip = sb(peer, "skip", [P, KD, S])
        scores_again = sb(peer, "scores_again", [P, NB * PH + 1, 2 * NK])
        gd = [sb(peer, f"down_rows{i}", [P, D]) for i in range(RING)]
        gu = [sb(peer, f"up_rows{i}", [P, D]) for i in range(RING)]
        junk = sb(peer, "junk", [P, D])
        hblk = sb(peer, "hblk", [P, D])
        ln2_sb = sb(peer, "ln2_sb", [P, 2, D])
        dg = skip[:].rearrange("p a b -> p (a b)")[:, 0:2 * TOPK * P].rearrange(
            "p (q k m) -> p q k m", q=2, k=TOPK)
        zeros = sb(peer, "zeros", [P, P])
        sc = sb(peer, "sc", [P, 2, NK])
        sc2 = sb(peer, "sc2", [P, 2, NK])
        top = sb(peer, "top", [P, 2, TOPK])
        topi = sb(peer, "topi", [P, 2, TOPK], U32)
        cand = sb(peer, "cand", [P, TOPK * TOPK])
        cand2 = sb(peer, "cand2", [P, TOPK * TOPK])
        best = sb(peer, "best", [P, TOPK])
        pos = sb(peer, "pos", [P, TOPK], U32)
        hl = sb(peer, "hl", [P, 2, TOPK], U32)
        eq = sb(peer, "eq", [P, 2, TOPK, TOPK])
        e12 = sb(peer, "e12", [P, 2, TOPK])
        idx = [sb(peer, f"idx{i}", [P, TOPK], U32) for i in range(2)]
        shifted = [sb(peer, f"shifted{i}", [P, TOPK]) for i in range(2)]
        ge = [sb(peer, f"gate_exp{i}", [P, TOPK]) for i in range(2)]
        gs = [sb(peer, f"gate_sum{i}", [P, 1]) for i in range(2)]
        grs = sb(peer, "gate_rs", [P, 1])
        u = [sb(peer, f"u{i}", [P, TOPK]) for i in range(2)]
        gl = [sb(peer, f"gelu{i}", [P, TOPK]) for i in range(2)]
        a = [sb(peer, f"a{i}", [P, TOPK]) for i in range(2)]
        ctx.callback(peer.close)

        const_in, x_in, xT_in, small_in, ln2_in = (sem(n) for n in (
            "const_in", "x_in", "xT_in", "small_in", "ln2_in"))
        wp_in = [sem(f"wp_in{i}") for i in range(2)]
        wq_in = [sem(f"wq_in{i}") for i in range(2)]
        proj_done, proj_copied = sem("proj_done"), sem("proj_copied")
        pads_zero = sem("pads_zero")
        conv_done, conv_exp, xc_ready = sem("conv_done"), sem("conv_exp"), sem("xc_ready")
        gate_pre, gate_ln, logf_ready, gate_sums = (sem(n) for n in (
            "gate_pre", "gate_ln", "logf_ready", "gate_sums"))
        r_ready, diag_ready, args_ready, weights_ready = (sem(n) for n in (
            "r_ready", "diag_ready", "args_ready", "weights_ready"))
        ps_done, ps_read = sem("ps_done"), sem("ps_read")
        pt_done, pt_copied = sem("pt_done"), sem("pt_copied")
        mexp_done, mp_ready, kw_ready = sem("mexp_done"), sem("mp_ready"), sem("kw_ready")
        ml_done, inter_scaled, num_done = sem("ml_done"), sem("inter_scaled"), sem("num_done")
        upd_done, state_ready = sem("upd_done"), sem("state_ready")
        var_ready, sd_ready, ogate_exp = sem("var_ready"), sem("sd_ready"), sem("ogate_exp")
        masked, aexp_done, ap_ready, pv_done = (sem(n) for n in ("masked", "aexp_done", "ap_ready", "pv_done"))
        cat_ready, h1_ready = sem("cat_ready"), sem("h1_ready")
        dve_step, act_step = sem("dve_step"), sem("act_step")
        qry_done, qry_copied, sc_done, sc_copied = (sem(n) for n in (
            "qry_done", "qry_copied", "sc_done", "sc_copied"))
        down_in = [sem(f"down_in{i}") for i in range(RING)]
        up_in = [sem(f"up_in{i}") for i in range(RING)]
        down_free, up_free = sem("down_free"), sem("up_free")
        idx_ready, shifted_ready, gates_ready = sem("idx_ready"), sem("shifted_ready"), sem("gates_ready")
        u_ready, gelu_ready, a_ready, dg_ready = (sem(n) for n in ("u_ready", "gelu_ready", "a_ready", "dg_ready"))
        y_done, y_read, peer_step, block_step = (sem(n) for n in ("y_done", "y_read", "peer_step", "block_step"))
        var2_ready, sd2_ready, out_ready, out_sent = (sem(n) for n in (
            "var2_ready", "sd2_ready", "out_ready", "out_sent"))
        zeros_ready = sem("zeros_ready")
        dve_alone, pool_alone = sem("dve_alone"), sem("pool_alone")

        block = ctx.enter_context(nc.Block())

        piece_used = [VM, QA, KA, MQ, OM, PROJ_ITEMS]

        @block.sync
        def _(sp):
            sp.dma_start(xT_sb[:], xT.rearrange("(k p) t -> p k t", p=P)).then_inc(xT_in, 16)
            sp.dma_start(wg_sb[:], w_gate.rearrange("(k p) n -> p k n", p=P)).then_inc(small_in, 16)
            w_order = [3, 4, 0, 1, 2, 5]
            for n in range(8):
                if n >= 2:
                    sp.wait_ge(proj_done, piece_used[n - 2])
                src = (w_in[:, w_order[n] * W:(w_order[n] + 1) * W] if n < 6
                       else w_out[:, (n - 6) * W:(n - 5) * W])
                sp.dma_start(wp[n % 2][:], src.rearrange("(k p) n -> p k n", p=P)).then_inc(wp_in[n % 2], 16)
                if n == 0:
                    sp.dma_start(cst[:], consts).then_inc(const_in, 16)
                    sp.dma_start(conv_sb[:], conv).then_inc(small_in, 16)
                    sp.dma_start(gbias[:], gate_bias.to_broadcast([P, 2 * MH])).then_inc(small_in, 16)
                    sp.dma_start(wmq, w_mq.rearrange("h e f -> e h f")).then_inc(small_in, 16)
                    sp.dma_start(wmk, w_mk.rearrange("h e f -> e h f")).then_inc(small_in, 16)
                    sp.dma_start(mhg[:], mh_g.to_broadcast([P, W])).then_inc(small_in, 16)
                    for i in range(2):
                        sp.dma_start(ln1_sb[:, i, :], ln1[i:i + 1, :].to_broadcast([P, D])).then_inc(small_in, 16)
                    for c in range(NB):
                        sp.dma_start(h1[:, c, :], x[c * P:(c + 1) * P, :]).then_inc(x_in, 16)
            for h in range(PH):
                if h < 2:
                    sp.wait_ge(h1_ready, NB)
                    sp.wait_ge(pt_copied, PT_PER * NB)
                else:
                    sp.wait_ge(sc_done, 2 * (h - 1))
                sp.dma_start(wq[h % 2][:], w_query[:, h * 2 * NK:(h + 1) * 2 * NK].rearrange(
                    "(k p) n -> p k n", p=P)).then_inc(wq_in[h % 2], 16)
                sp.dma_start(sk[h % 2][:], sub_keys[:, h]).then_inc(wq_in[h % 2], 16)
            sp.wait_ge(sc_copied, 2 + 2 * PH)
            for i in range(2):
                sp.dma_start(ln2_sb[:, i, :], ln2[i:i + 1, :].to_broadcast([P, D])).then_inc(ln2_in, 16)
            with sp.Fori(0, NB, 1) as b:
                sp.wait_ge(out_ready, b + 1)
                sp.dma_start(out[bass.ds(b * P, P), :], h1[:, bass.ds(b, 1), :].rearrange("p a d -> p (a d)")).then_inc(out_sent, 16)
            sp.wait_ge(out_sent, 16 * NB)

        @block.tensor
        def _(pe):
            mm = nc.tensor.matmul

            def open_proj(n):
                if n >= 2:
                    pe.wait_ge(proj_copied, n - 1)
                return pj[n % 2]

            def wide(n0, piece):
                pe.wait_ge(wp_in[piece % 2], 16 * (piece // 2 + 1))
                for i in range(4):
                    o = open_proj(n0 + i)
                    for k in range(KD):
                        last = mm(o[:], wp[piece % 2][:, k, i * P:(i + 1) * P], xT_sb[:, k, :],
                                  start=k == 0, stop=k == KD - 1)
                    last.then_inc(proj_done, 1)

            def tall(n0, piece):
                pe.wait_ge(wp_in[piece % 2], 16 * (piece // 2 + 1))
                for c in range(NB):
                    o = open_proj(n0 + c)
                    for k in range(KD):
                        last = mm(o[:], xT_sb[:, k, c * P:(c + 1) * P], wp[piece % 2][:, k, :],
                                  start=k == 0, stop=k == KD - 1)
                    last.then_inc(proj_done, 1)

            pe.wait_ge(xT_in, 16)
            pe.wait_ge(small_in, 16 * 8)
            for c in range(NB):
                for k in range(KD):
                    last = mm(pj[0][:, c * 8:c * 8 + 8], xT_sb[:, k, c * P:(c + 1) * P], wg_sb[:, k, :],
                              start=k == 0, stop=k == KD - 1)
            last.then_inc(proj_done, 1)
            wide(XM, 0)
            tall(VM, 1)
            wide(QA, 2)
            wide(KA, 3)
            for n0, w in ((MQ, wmq), (MK, wmk)):
                for h in range(MH):
                    o = open_proj(n0 + h)
                    pe.wait_ge(xc_ready, h + 1)
                    mm(o[:], w[:, h, :], xc[:, h, :], start=True, stop=True).then_inc(proj_done, 1)
            for h in range(MH):
                o = open_proj(KM + h)
                for c in range(NB):
                    last = mm(o[:, c * P:(c + 1) * P], xc[:, h, c * P:(c + 1) * P], wmk[:, h, :],
                              start=True, stop=True)
                last.then_inc(proj_done, 1)
            pe.wait_ge(const_in, 16)
            pe.wait_ge(logf_ready, 1)
            mm(pi[:, 0:16], triu, logf, start=True, stop=True)
            mm(pi[:, 16:32], ones, logf, start=True, stop=True).then_inc(gate_sums, 1)
            tall(VA, 4)
            tall(OM, 5)
            pe.wait_ge(diag_ready, NB * MH)
            for c in range(NB):
                if c >= 2:
                    pe.wait_ge(ps_read, c - 1)
                mm(ps[c % 2][:], ones, xm[:, c, 0:S], start=True, stop=True).then_inc(ps_done, 1)

            def open_score(n):
                pe.wait_ge(ps_read, n - 1)
                return ps[n % 2]

            def open_turn(n):
                if n >= 2:
                    pe.wait_ge(pt_copied, n - 1)
                return pt[n % 2]

            for c in range(NB):
                t = slice(c * P, (c + 1) * P)
                n_ps, n_pt = PS0 + PS_PER * c, PT_PER * c
                if c == 0:
                    pe.wait_ge(proj_copied, PROJ_ITEMS)
                o = open_score(n_ps)
                for h in range(MH):
                    last = mm(o[:, h * P:(h + 1) * P], qm[:, h, t], kmT[:, h, t], start=True, stop=True)
                last.then_inc(ps_done, 1)
                pe.wait_ge(state_ready, c + 1)
                if c >= 1:
                    pe.wait_ge(inter_scaled, c)
                for h in range(MH):
                    mm(pi[:, h * P:(h + 1) * P], qm[:, h, t], ct[:, h, :], start=True, stop=True)
                for h in range(MH):
                    last = mm(pj[1][:, h:h + 1], qm[:, h, t], nst[:, h:h + 1], start=True, stop=True)
                if c < NB - 1:
                    pe.wait_ge(kw_ready, c + 1)
                    for h in range(MH):
                        mm(pj[0][:, h * P:(h + 1) * P], kw[:, h, 0:ME], vm[:, c, h * ME:(h + 1) * ME],
                           start=True, stop=True)
                    for h in range(MH):
                        last = mm(pj[1][:, 4 + h:5 + h], kw[:, h, 0:ME], ones[:, 0:1], start=True, stop=True)
                last.then_inc(upd_done, 1)
                pe.wait_ge(mp_ready, c + 1)
                o = open_turn(n_pt)
                for h in range(MH):
                    last = nc.tensor.transpose(o[:, h * P:(h + 1) * P], sw[0][:, h * P:(h + 1) * P], ident)
                last.then_inc(pt_done, 1)
                pe.wait_ge(pt_copied, n_pt + 1)
                if c >= 1:
                    pe.wait_ge(cat_ready, c)
                for h in range(MH):
                    last = mm(po[:, h * P:(h + 1) * P], pT[(PV_PER * c) % 2][:, h * P:(h + 1) * P],
                              vm[:, c, h * ME:(h + 1) * ME], start=True, stop=True)
                last.then_inc(pv_done, 1)
                for i in range(AH + 2):
                    if i < AH:
                        o = open_score(n_ps + 1 + i)
                        r = slice((i % 2) * AE, (i % 2 + 1) * AE)
                        mm(o[:, 0:(c + 1) * P], qa[r, i // 2, t], ka[r, i // 2, 0:(c + 1) * P],
                           start=True, stop=True).then_inc(ps_done, 1)
                    if 1 <= i <= AH:
                        h = i - 1
                        pe.wait_ge(ap_ready, AH * c + h + 1)
                        o = open_turn(n_pt + 1 + h)
                        for j in range(c + 1):
                            last = nc.tensor.transpose(o[:, j * P:(j + 1) * P],
                                                       sw[(h + 1) % 2][:, j * P:(j + 1) * P], ident)
                        last.then_inc(pt_done, 1)
                    if i >= 2:
                        h = i - 2
                        pe.wait_ge(pt_copied, n_pt + 2 + h)
                        if h == 0:
                            pe.wait_ge(num_done, c + 1)
                        for j in range(c + 1):
                            last = mm(po[:, h * AE:(h + 1) * AE],
                                      pT[(PV_PER * c + 1 + h) % 2][:, j * P:(j + 1) * P],
                                      va[:, j, h * AE:(h + 1) * AE], start=j == 0, stop=j == c)
                        last.then_inc(pv_done, 1)
                pe.wait_ge(cat_ready, c + 1)
                for i in range(2):
                    o = open_turn(n_pt + 1 + AH + i)
                    for j in range(4):
                        k = 4 * i + j
                        last = nc.tensor.transpose(o[:, j * P:(j + 1) * P], cat[:, k * P:(k + 1) * P], ident)
                    last.then_inc(pt_done, 1)
                pe.wait_ge(pt_copied, n_pt + 3 + AH)
                for i in range(2):
                    if c == 0:
                        pe.wait_ge(wp_in[i], 16 * 4)
                    o = open_score(n_ps + 1 + AH + i)
                    for k in range(KD):
                        last = mm(o[:], catT[:, k, :], wp[i][:, k, :], start=k == 0, stop=k == KD - 1)
                    last.then_inc(ps_done, 1)
                pe.wait_ge(h1_ready, c + 1)
                for i in range(2):
                    o = open_turn(n_pt + 3 + AH + i)
                    for j in range(4):
                        k = 4 * i + j
                        last = nc.tensor.transpose(o[:, j * P:(j + 1) * P], h1[:, c, k * P:(k + 1) * P], ident)
                    last.then_inc(pt_done, 1)

            pe.wait_ge(pt_copied, PT_PER * NB)
            pe.wait_ge(ps_read, PS0 + PS_PER * NB)
            with pe.Fori(0, PH // 2, 1) as pair:
                h0 = pair * 2
                for q in range(2):
                    pe.wait_ge(wq_in[q], h0 * 16 + 32)
                    for side in range(2):
                        pe.wait_ge(qry_copied, h0 * 2 + (2 * q + side + 1))
                        for k in range(KD):
                            last = mm(pj[side][:], wq[q][:, k, side * P:(side + 1) * P], h1T[:, k, :],
                                      start=k == 0, stop=k == KD - 1)
                        last.then_inc(qry_done, 1)
                    pe.wait_ge(qry_copied, h0 * 2 + (2 * q + 2 + 2))
                    for half in range(2):
                        pe.wait_ge(sc_copied, h0 * 2 + (2 * q + half + 1))
                        for b in range(2):
                            for side in range(2):
                                blk = 2 * half + b
                                last = mm(ps[half][:, (2 * b + side) * P:(2 * b + side + 1) * P],
                                          qry[q][:, side, blk * P:(blk + 1) * P], sk[q][:, side, :],
                                          start=True, stop=True)
                        last.then_inc(sc_done, 1)

            pe.wait_ge(zeros_ready, 1)
            with pe.Fori(0, NB, 1) as b:
                pe.wait_ge(y_read, b + 1)
                for half in range(2):
                    mm(py[:, half, :], zeros[:], attn_count, start=True, stop=False, skip_group_check=True)
                with pe.Fori(0, PH // 2, 1) as pair:
                    h0 = pair * 2
                    for q in range(2):
                        for k in range(TOPK):
                            pe.wait_ge(dg_ready, (b * PH + h0) * TOPK + (q * TOPK + k + 1))
                            pe.wait_ge(up_in[k % RING], (b * PH + h0) * 32 + (32 * q + 16 * (k // RING + 1)))
                            for half in range(2):
                                last = mm(py[:, half, :], dg[:, q, k, :], gu[k % RING][:, half * 512:(half + 1) * 512],
                                          start=False, stop=False, skip_group_check=True)
                            last.then_inc(up_free, 1)

        @block.scalar
        def _(act):
            run = nc.scalar.activation
            steps = [0]

            def dep(ins):
                steps[0] += 1
                ins.then_inc(act_step, 1)
                act.wait_ge(act_step, steps[0])

            def take(n, dst, scale=1.0):
                act.wait_ge(proj_done, n + 1)
                src = pj[n % 2][:, 0:dst.free_size()] if n == GATES else pj[n % 2][:]
                if len(dst.shape) == 3:
                    src = src.rearrange("p (a b) -> p a b", a=dst.shape[1])
                run(dst, src, ACT.Copy, scale=scale).then_inc(proj_copied, 1)

            take(GATES, gt[:])

            def silu_exp(h):
                act.wait_ge(conv_done, h + 1)
                run(xc[:, h, :], kmT[:, h, :], ACT.Exp, scale=-1.0).then_inc(conv_exp, 1)

            for h in range(MH):
                act.wait_ge(pads_zero, 1)
                take(XM + h, xm[:, h, TAPS - 1:TAPS - 1 + S])
                if h >= 1:
                    silu_exp(h - 1)
            take(VM, vm[:, 0, :])
            silu_exp(MH - 1)
            for c in range(1, NB):
                take(VM + c, vm[:, c, :])
            act.wait_ge(gate_pre, 1)
            dep(run(lexp, mn, ACT.Exp))
            act.wait_ge(const_in, 16)
            run(lg, lexp, ACT.Ln, bias=ones[:, 0:1]).then_inc(gate_ln, 1)
            for i in range(4):
                take(QA + i, qa[:, i, :])
            for i in range(4):
                take(KA + i, ka[:, i, :])
            act.wait_ge(xc_ready, MH)
            for h in range(MH):
                take(MQ + h, qm[:, h, :], scale=float(ME) ** -0.5)
            for h in range(MH):
                take(MK + h, kmT[:, h, :])
            for h in range(MH):
                take(KM + h, km[:, :, h, :])
            act.wait_ge(r_ready, 1)
            for k in range(NB * MH):
                run(diag_r[:, k // MH, k % MH, :], ident, ACT.Copy, scale=rr[:, k:k + 1]).then_inc(diag_ready, 1)
            for c in range(NB):
                take(VA + c, va[:, c, :])
            for c in range(NB):
                take(OM + c, om[:, c, :])
            act.wait_ge(args_ready, 1)
            run(ew[:].rearrange("p a b -> p (a b)"), ew[:].rearrange("p a b -> p (a b)"), ACT.Exp).then_inc(weights_ready, 1)
            act.wait_ge(weights_ready, 1)

            def turned(n, dst):
                act.wait_ge(pt_done, n + 1)
                src = pt[n % 2][:, 0:dst.free_size()]
                if len(dst.shape) == 3:
                    src = src.rearrange("p (a b) -> p a b", a=dst.shape[1])
                run(dst, src, ACT.Copy).then_inc(pt_copied, 1)

            for c in range(NB):
                n_pt, n_pv = PT_PER * c, PV_PER * c
                if c >= 1:
                    act.wait_ge(pt_done, n_pt - 4)
                for h in range(MH):
                    k = 4 * c + h
                    last = run(sw[0][:, h * P:(h + 1) * P], rm[:, c, h, :], ACT.Exp, bias=nmx[:, k:k + 1])
                last.then_inc(mexp_done, 1)
                if c < NB - 1:
                    if c == 0:
                        act.wait_ge(proj_done, PROJ_ITEMS)
                    else:
                        act.wait_ge(upd_done, c)
                    for h in range(MH):
                        last = run(kw[:, h, 0:ME], km[:, c, h, :], ACT.Copy, scale=w_k[:, 4 * c + h:4 * c + h + 1])
                    last.then_inc(kw_ready, 1)
                run(om[:, c, :], om[:, c, :], ACT.Exp, scale=-1.0).then_inc(ogate_exp, 1)
                act.wait_ge(upd_done, c + 1)
                for h in range(MH):
                    last = run(catT[:, 4 + h, :], pi[:, h * P:(h + 1) * P], ACT.Copy,
                               scale=w_inter[:, 4 * c + h:4 * c + h + 1])
                last.then_inc(inter_scaled, 1)
                if c >= 1:
                    act.wait_ge(pv_done, n_pv - 1)
                turned(n_pt, pT[n_pv % 2][:])
                act.wait_ge(var_ready, 2 * c + 1)
                run(sd[:], mv[:, :, 1], ACT.Sqrt, bias=eps).then_inc(sd_ready, 1)
                for i in range(AH + 1):
                    if i < AH:
                        act.wait_ge(masked, AH * c + i + 1)
                        v = sw[(i + 1) % 2][:, 0:(c + 1) * P]
                        run(v, v, ACT.Exp, scale=float(AE) ** -0.5,
                            bias=hv[:, 0, i:i + 1]).then_inc(aexp_done, 1)
                    if i >= 1:
                        if n_pv + i >= 2:
                            act.wait_ge(pv_done, n_pv + i - 1)
                        turned(n_pt + i, pT[(n_pv + i) % 2][:, 0:(c + 1) * P])
                for i in range(2):
                    turned(n_pt + 1 + AH + i, catT[:, 4 * i:4 * i + 4, :])
                act.wait_ge(var_ready, 2 * c + 2)
                run(sd[:, 0:1], mv[:, 0, 1:2], ACT.Sqrt, bias=eps).then_inc(sd_ready, 1)
                for i in range(2):
                    turned(n_pt + 3 + AH + i, h1T[:, 4 * i:4 * i + 4, c * P:(c + 1) * P])

            act.sem_inc(qry_copied, 2)
            with act.Fori(0, PH // 2, 1) as pair:
                h0 = pair * 2
                for q in range(2):
                    for side in range(2):
                        act.wait_ge(qry_done, h0 * 2 + (2 * q + side + 1))
                        run(qry[q][:, side, :], pj[side][:], ACT.Copy).then_inc(qry_copied, 1)

            act.wait_ge(shifted_ready, 1)
            run(ge[0][:], shifted[0][:], ACT.Exp, accum_out=gs[0][:]).then_inc(gates_ready, 1)
            with act.Fori(0, NB, 1) as b:
                with act.Fori(0, PH // 2, 1) as pair:
                    h0 = pair * 2
                    for q in range(2):
                        step = b * PH + h0 + q
                        act.wait_ge(u_ready, step + 1)
                        run(gl[q][:], u[q][:], ACT.Gelu).then_inc(gelu_ready, 1)
                        act.wait_ge(a_ready, step + 1)
                        act.wait_ge(up_free, (b * PH + h0) * TOPK + (q * TOPK + 1))
                        for k in range(TOPK):
                            run(dg[:, q, k, :], ident, ACT.Copy, scale=a[q][:, k:k + 1]).then_inc(dg_ready, 1)
                        act.wait_ge(shifted_ready, step + 2)
                        run(ge[1 - q][:], shifted[1 - q][:], ACT.Exp,
                            accum_out=gs[1 - q][:]).then_inc(gates_ready, 1)
                act.wait_ge(var2_ready, b + 1)
                run(sd[:, 0:1], mv[:, 0, 1:2], ACT.Sqrt, bias=eps).then_inc(sd2_ready, 1)

        @block.vector
        def _(dve):
            v = nc.vector
            steps = [0]

            def dep(ins):
                steps[0] += 1
                ins.then_inc(dve_step, 1)
                dve.wait_ge(dve_step, steps[0])

            def spread(col, n):
                return col.unsqueeze(2).to_broadcast([P, col.shape[1], n])

            def blocks(ap, n=MH):
                return ap.rearrange("p (a b) -> p a b", a=n)

            dve.wait_ge(small_in, 16 * 8)
            dve.wait_ge(proj_copied, 1)
            g3 = gt[:]
            v.tensor_tensor(ip.rearrange("p (c h) -> p c h", c=NB), g3[:, :, 0:MH],
                            gbias[:, 0:MH].unsqueeze(1).to_broadcast([P, NB, MH]), ALU.add)
            dep(v.tensor_tensor(ff.rearrange("p (c h) -> p c h", c=NB), g3[:, :, MH:2 * MH],
                                gbias[:, MH:2 * MH].unsqueeze(1).to_broadcast([P, NB, MH]), ALU.add))
            dep(v.tensor_scalar(nf, ff, -1.0, None, ALU.mult))
            v.tensor_tensor(mn, nf, ff, ALU.min).then_inc(gate_pre, 1)

            def conv_head(h):
                dve.wait_ge(proj_copied, XM + h + 1)
                y = kmT[:, h, :]
                dep(v.tensor_scalar(y, xm[:, h, 0:S], conv_sb[:, h, 0:1], conv_sb[:, h, TAPS:TAPS + 1],
                                    ALU.mult, ALU.add))
                for j in range(1, TAPS):
                    ins = v.scalar_tensor_tensor(y, xm[:, h, j:j + S], conv_sb[:, h, j:j + 1], y,
                                                 ALU.mult, ALU.add)
                    if j < TAPS - 1:
                        dep(ins)
                ins.then_inc(conv_done, 1)

            def silu(h):
                dve.wait_ge(conv_exp, h + 1)
                dve.wait_ge(conv_done, h + 1)
                dep(v.tensor_scalar(xc[:, h, :], xc[:, h, :], 1.0, None, ALU.add))
                dep(v.reciprocal(xc[:, h, :], xc[:, h, :]))
                v.tensor_tensor(xc[:, h, :], xc[:, h, :], kmT[:, h, :], ALU.mult).then_inc(xc_ready, 1)

            for h in range(MH):
                conv_head(h)
                if h:
                    silu(h - 1)
            silu(MH - 1)
            dve.wait_ge(gate_ln, 1)
            dep(v.tensor_scalar(ff, ff, 0.0, None, ALU.min))
            v.tensor_tensor(logf, ff, lg, ALU.subtract).then_inc(logf_ready, 1)
            dve.wait_ge(gate_sums, 1)
            v.tensor_copy(bl, pi[:, 16:32])
            dep(v.tensor_copy(bc, pi[:, 0:16]))
            v.tensor_tensor(rr, ip, bc, ALU.subtract).then_inc(r_ready, 1)
            for c in range(NB):
                dve.wait_ge(ps_done, c + 1)
                if c == 0:
                    dve.wait_ge(proj_done, VA)
                    dve.wait_ge(const_in, 16)
                v.tensor_reduce(rmax[:, 4 * c:4 * c + 4], blocks(ps[c % 2][:]), X, ALU.max)
                dep(v.tensor_tensor(rm[:, c], blocks(ps[c % 2][:]),
                                    tril_bias.unsqueeze(1).to_broadcast([P, MH, P]), ALU.add))
                v.tensor_reduce(mmax[:, 4 * c:4 * c + 4], rm[:, c], X, ALU.max).then_inc(ps_read, 1)
            dep(v.memset(mprev[:, 0:4], 0.0))
            for c in range(NB):
                g = slice(4 * c, 4 * c + 4)
                dep(v.tensor_tensor(mxl[:, g], mprev[:, g], rmax[:, g], ALU.max))
                dep(v.tensor_tensor(mprev[:, 4 * c + 4:4 * c + 8], mxl[:, g], bl[:, g], ALU.add))
            dve.wait_ge(ps_read, NB)
            dep(v.tensor_tensor(mx, mprev[:, 0:16], mmax, ALU.max))
            v.tensor_scalar(nmx, mx, -1.0, None, ALU.mult)
            v.tensor_tensor(w_inter, mprev[:, 0:16], mx, ALU.subtract)
            v.tensor_tensor(a_dec, mprev[:, 0:16], mxl, ALU.subtract)
            v.tensor_tensor(w_k, rr, mxl, ALU.subtract)
            dep(v.tensor_tensor(e_mt, bc, mx, ALU.add))
            v.tensor_scalar(e_mt, e_mt, -1.0, None, ALU.mult).then_inc(args_ready, 1)
            v.memset(ct[:], 0.0)
            v.memset(nst[:], 0.0).then_inc(state_ready, 1)
            dve.wait_ge(weights_ready, 1)

            for c in range(NB):
                n_ps, k0 = PS0 + PS_PER * c, 4 * c
                g = slice(k0, k0 + 4)
                rs_sum, den, nden = hv[:, 1, 0:4], hv[:, 2, 0:4], hv[:, 3, 0:4]
                dve.wait_ge(mexp_done, c + 1)
                dve.wait_ge(ps_done, n_ps + 1)
                v.tensor_tensor(sw[0][:], sw[0][:], ps[n_ps % 2][:], ALU.mult).then_inc(ps_read, 1)
                dve.wait_ge(ps_read, n_ps + 1)
                dep(v.tensor_reduce(rs_sum, blocks(sw[0][:]), X, ALU.add))
                dve.sem_inc(mp_ready, 1)
                dve.wait_ge(upd_done, c + 1)
                dep(v.tensor_tensor(den, w_inter[:, g], pj[1][:, 0:4], ALU.mult))
                dep(v.tensor_tensor(den, den, rs_sum, ALU.add))
                dep(v.tensor_scalar(nden, den, -1.0, None, ALU.mult))
                dep(v.tensor_tensor(den, den, nden, ALU.max))
                dep(v.tensor_tensor(den, den, e_mt[:, g], ALU.max))
                dep(v.reciprocal(den, den))
                if c < NB - 1:
                    for h in range(MH):
                        dep(v.scalar_tensor_tensor(ct[:, h, :], ct[:, h, :], a_dec[:, k0 + h:k0 + h + 1],
                                                   pj[0][:, h * P:(h + 1) * P], ALU.mult, ALU.add))
                    dep(v.tensor_tensor(nst[:], nst[:], a_dec[:, g], ALU.mult))
                    v.tensor_tensor(nst[:], nst[:], pj[1][:, 4:8], ALU.add).then_inc(state_ready, 1)
                hm = cat[:, W:2 * W]
                dve.wait_ge(inter_scaled, c + 1)
                dve.wait_ge(pv_done, PV_PER * c + 1)
                v.tensor_tensor(blocks(hm), catT[:, 4:8, :], blocks(po), ALU.add).then_inc(num_done, 1)
                dve.wait_ge(num_done, c + 1)
                dep(v.tensor_tensor(blocks(hm), blocks(hm), spread(den, ME), ALU.mult))
                for h in range(MH):
                    dep(v.bn_stats(stats[:, h, :], hm[:, h * ME:(h + 1) * ME]))
                for h in range(MH):
                    ins = v.bn_aggr(mv[:, h, :], stats[:, h, :])
                ins.then_inc(var_ready, 1)
                dve.wait_ge(ogate_exp, c + 1)
                dep(v.tensor_scalar(om[:, c, :], om[:, c, :], 1.0, None, ALU.add))
                dep(v.reciprocal(om[:, c, :], om[:, c, :]))
                dep(v.tensor_tensor(om[:, c, :], om[:, c, :], mhg[:], ALU.mult))
                dve.wait_ge(sd_ready, 2 * c + 1)
                dep(v.reciprocal(rstd[:], sd[:]))
                for h in range(MH):
                    ins = v.tensor_scalar(hm[:, h * ME:(h + 1) * ME], hm[:, h * ME:(h + 1) * ME],
                                          mv[:, h, 0:1], rstd[:, h:h + 1], ALU.subtract, ALU.mult)
                dep(ins)
                dep(v.tensor_tensor(hm, hm, om[:, c, :], ALU.mult))
                for i in range(AH + 1):
                    if i < AH:
                        wide = slice(0, (c + 1) * P)
                        off = slice((NB - 1 - c) * P, S)
                        dve.wait_ge(ps_done, n_ps + 2 + i)
                        if i >= 2:
                            dve.wait_ge(pt_done, PT_PER * c + i)
                        elif i == 1:
                            dve.wait_ge(pt_done, PT_PER * c + 1)
                        s = sw[(i + 1) % 2][:, wide]
                        v.tensor_tensor(s, ps[(n_ps + 1 + i) % 2][:, wide], attn_bias[:, off],
                                        ALU.add).then_inc(ps_read, 1)
                        dve.wait_ge(ps_read, n_ps + 2 + i)
                        dep(v.tensor_reduce(hv[:, 4, i:i + 1], s, X, ALU.max))
                        v.tensor_scalar(hv[:, 0, i:i + 1], hv[:, 4, i:i + 1], -float(AE) ** -0.5, None,
                                        ALU.mult).then_inc(masked, 1)
                    if i >= 1:
                        dve.wait_ge(aexp_done, AH * c + i)
                        s = sw[i % 2][:, wide]
                        v.tensor_tensor_reduce(out=s, in0=s, in1=attn_count[:, off], scale=1.0, scalar=0.0,
                                               op0=ALU.mult, op1=ALU.add,
                                               accum_out=hv[:, 5, i - 1:i]).then_inc(ap_ready, 1)
                dve.wait_ge(ap_ready, AH * (c + 1))
                dep(v.reciprocal(hv[:, 6, :], hv[:, 5, :]))
                dve.wait_ge(pv_done, PV_PER * (c + 1))
                v.tensor_tensor(blocks(cat[:, 0:W], AH), blocks(po, AH), spread(hv[:, 6, :], AE),
                                ALU.mult).then_inc(cat_ready, 1)
                dve.wait_ge(x_in, 16 * NB)
                hb = h1[:, c, :]
                for i in range(2):
                    n = n_ps + 1 + AH + i
                    dve.wait_ge(ps_done, n + 1)
                    hh = hb[:, i * 512:(i + 1) * 512]
                    v.scalar_tensor_tensor(hh, hh, ALPHA, ps[n % 2][:], ALU.mult, ALU.add).then_inc(ps_read, 1)
                    dve.wait_ge(ps_read, n + 1)
                    dep(v.bn_stats(stats[:, i, :], hh))
                v.bn_aggr(mv[:, 0, :], stats[:, 0:2, :]).then_inc(var_ready, 1)
                dve.wait_ge(sd_ready, 2 * c + 2)
                dep(v.reciprocal(rstd[:, 0:1], sd[:, 0:1]))
                dep(v.tensor_scalar(hb, hb, mv[:, 0, 0:1], rstd[:, 0:1], ALU.subtract, ALU.mult))
                dep(v.tensor_tensor(hb, hb, ln1_sb[:, 0, :], ALU.mult))
                v.tensor_tensor(hb, hb, ln1_sb[:, 1, :], ALU.add).then_inc(h1_ready, 1)
                dve.wait_ge(h1_ready, c + 1)

            dve.wait_ge(pt_copied, PT_PER * NB)
            dep(v.memset(scores[:, NB * PH, :], 0.0))
            dve.sem_inc(sc_copied, 2)
            s4 = scores[:, 0:NB * PH, :].rearrange("p (b h) n -> p b (h n)", b=NB)
            with dve.Fori(0, PH // 2, 1) as pair:
                h0 = pair * 2
                for q in range(2):
                    for half in range(2):
                        dve.wait_ge(sc_done, h0 * 2 + (2 * q + half + 1))
                        v.tensor_copy(s4[:, 2 * half:2 * half + 2, bass.ds((h0 + q) * (2 * NK), 2 * NK)],
                                      ps[half][:].rearrange("p (b n) -> p b n", b=2)).then_inc(sc_copied, 1)

            dve.wait_ge(sc_copied, 2 + 2 * PH)
            v.memset(zeros[:], 0.0).then_inc(zeros_ready, 1)
            dve.sem_inc(y_read, 1)

            def stand_alone():
                dve.sem_inc(dve_alone, 1)

            def top16(src, src2, vals, inds, dep):
                dep(v.max(vals[:, 0:8], src))
                dep(v.max_index(inds[:, 0:8], vals[:, 0:8], src))
                dep(v.match_replace(src2, vals[:, 0:8], src, LOWEST))
                dep(v.max(vals[:, 8:16], src2))
                dep(v.max_index(inds[:, 8:16], vals[:, 8:16], src2))

            def pick(step, q, dep):
                dep(v.tensor_copy(sc[:], scores[:, bass.ds(step, 1), :].rearrange("p a (s n) -> p (a s) n", s=2)
                                  if not isinstance(step, int) else
                                  scores[:, step, :].rearrange("p (s n) -> p s n", s=2)))
                for side in range(2):
                    top16(sc[:, side, :], sc2[:, side, :], top[:, side, :], topi[:, side, :], dep)
                dep(v.tensor_tensor(cand[:].rearrange("p (i j) -> p i j", i=TOPK),
                                    top[:, 0, :].unsqueeze(2).to_broadcast([P, TOPK, TOPK]),
                                    top[:, 1, :].unsqueeze(1).to_broadcast([P, TOPK, TOPK]), ALU.add))
                top16(cand[:], cand2[:], best[:], pos[:], dep)
                v.tensor_scalar(shifted[q][:], best[:], best[:, 0:1], None, ALU.subtract).then_inc(shifted_ready, 1)
                dep(v.tensor_scalar(hl[:, 0, :], pos[:], 4, None, ALU.logical_shift_right))
                dep(v.tensor_scalar(hl[:, 1, :], pos[:], 15, None, ALU.bitwise_and))
                ranks = iota16.unsqueeze(1).to_broadcast([P, TOPK, TOPK])
                for side in range(2):
                    dep(v.tensor_tensor(eq[:, side], ranks, hl[:, side, :].unsqueeze(2).to_broadcast([P, TOPK, TOPK]),
                                        ALU.is_equal))
                for side in range(2):
                    dep(v.tensor_tensor(eq[:, side], eq[:, side],
                                        topi[:, side, :].unsqueeze(1).to_broadcast([P, TOPK, TOPK]), ALU.mult))
                dep(v.tensor_reduce(e12[:], eq[:], X, ALU.add))
                v.scalar_tensor_tensor(idx[q][:], e12[:, 0, :], float(NK), e12[:, 1, :],
                                       ALU.mult, ALU.add).then_inc(idx_ready, 1)

            pick(0, 0, dep)
            dve.wait_ge(ln2_in, 32)
            with dve.Fori(0, NB, 1) as b:
                bcount = [0]

                def bdep(ins):
                    bcount[0] += 1
                    ins.then_inc(block_step, 1)
                    dve.wait_ge(block_step, bcount[0])

                hb = h1[:, bass.ds(b, 1), :].rearrange("p a d -> p (a d)")
                bdep(v.tensor_copy(hblk[:], hb))
                with dve.Fori(0, PH // 2, 1) as pair:
                    h0 = pair * 2
                    count = [0]

                    def ldep(ins):
                        count[0] += 1
                        ins.then_inc(peer_step, 1)
                        dve.wait_ge(peer_step, count[0])

                    for q in range(2):
                        for k in range(TOPK):
                            dve.wait_ge(down_in[k % RING], (b * PH + h0) * 32 + (32 * q + 16 * (k // RING + 1)))
                            v.tensor_tensor_reduce(
                                out=gd[k % RING][:], in0=gd[k % RING][:], in1=hblk[:], scale=1.0, scalar=0.0,
                                op0=ALU.mult, op1=ALU.add, accum_out=u[q][:, k:k + 1]).then_inc(down_free, 1)
                        dve.wait_ge(down_free, (b * PH + h0) * TOPK + (RING + TOPK * (q + 1)))
                        dve.sem_inc(u_ready, 1)
                        dve.wait_ge(gates_ready, b * PH + h0 + (q + 1))
                        ldep(v.reciprocal(grs[:], gs[q][:]))
                        ldep(v.tensor_scalar(ge[q][:], ge[q][:], grs[:], None, ALU.mult))
                        dve.wait_ge(gelu_ready, b * PH + h0 + (q + 1))
                        v.tensor_tensor(a[q][:], gl[q][:], ge[q][:], ALU.mult).then_inc(a_ready, 1)
                        pick(b * PH + h0 + (q + 1), 1 - q, ldep)
                    dve.sem_clear(peer_step)
                dve.wait_ge(up_free, b * (PH * TOPK) + (RING + PH * TOPK))
                bdep(v.tensor_scalar(junk[:], hblk[:], ALPHA, None, ALU.mult))
                bdep(v.tensor_tensor(junk[:], junk[:], py[:].rearrange("p a b -> p (a b)"), ALU.add))
                dve.sem_inc(y_read, 1)
                bdep(v.bn_stats(stats[:, 0, :], junk[:, 0:512]))
                bdep(v.bn_stats(stats[:, 1, :], junk[:, 512:1024]))
                v.bn_aggr(mv[:, 0, :], stats[:, 0:2, :]).then_inc(var2_ready, 1)
                dve.wait_ge(sd2_ready, b + 1)
                bdep(v.reciprocal(rstd[:, 0:1], sd[:, 0:1]))
                bdep(v.tensor_scalar(junk[:], junk[:], mv[:, 0, 0:1], rstd[:, 0:1], ALU.subtract, ALU.mult))
                bdep(v.tensor_tensor(junk[:], junk[:], ln2_sb[:, 0, :], ALU.mult))
                bdep(v.tensor_tensor(hb, junk[:], ln2_sb[:, 1, :], ALU.add))
                dve.sem_clear(block_step)
                dve.sem_inc(out_ready, 1)

        @block.gpsimd
        def _(pool):
            nc.gpsimd.memset(xm[:, :, 0:TAPS - 1], 0.0).then_inc(pads_zero, 1)
            pool.sem_inc(down_free, RING)
            pool.sem_inc(up_free, RING)

            def gather(dst, table, col, landed):
                nc.gpsimd.indirect_dma_start(
                    out=dst, out_offset=None, in_=table,
                    in_offset=bass.IndirectOffsetOnAxis(ap=col, axis=0)).then_inc(landed, 16)

            with pool.Fori(0, NB, 1) as b:
                with pool.Fori(0, PH // 2, 1) as pair:
                    h0 = pair * 2
                    for q in range(2):
                        pool.wait_ge(idx_ready, b * PH + h0 + (q + 1))
                        for k in range(TOPK):
                            pool.wait_ge(down_free, (b * PH + h0) * TOPK + (q * TOPK + k + 1))
                            pool.sem_inc(pool_alone, 1)
                            gather(gd[k % RING][:], w_down, idx[q][:, k:k + 1], down_in[k % RING])
                        for k in range(TOPK):
                            pool.wait_ge(up_free, (b * PH + h0) * TOPK + (q * TOPK + k + 1))
                            pool.sem_inc(pool_alone, 1)
                            gather(gu[k % RING][:], w_up, idx[q][:, k:k + 1], up_in[k % RING])


def shape_constants():
    import numpy as np
    t, s = np.arange(P)[:, None], np.arange(P)[None, :]
    dist = t - (np.arange(S)[None, :] - (S - P))
    count = (((dist >= 0) & (dist <= 128)).astype(np.float32)
             + ((dist >= 0) & (dist % 4 == 0) & (dist <= 512)) + ((dist >= 0) & (dist % 16 == 0)))
    tail = np.zeros((P, 32), np.float32)
    tail[:, 0:16] = np.arange(16)
    tail[:, 16] = EPS
    return np.concatenate([np.eye(P), (t <= s), np.ones((P, P)), np.where(s <= t, 0.0, NEG),
                           np.where(count > 0, 0.0, NEG), count, tail], axis=1).astype(np.float32)


def kernel(**inputs):
    import numpy as _np
    import concourse.bacc as _bacc
    from concourse import mybir as _mybir
    from concourse.bass_utils import run_bass_kernel_spmd as _run

    a = {k: _np.asarray(v) for k, v in inputs.items()}
    x = a["x"][0]
    w_in = a["w_in"][0]
    conv = _np.concatenate([a["conv_w"][0], a["conv_b"]], axis=0)
    laid = {
        "xT": x.T,
        "x": x,
        "w_in": w_in[:, :6 * W],
        "w_gate": w_in[:, 6 * W:],
        "conv": conv.reshape(TAPS + 1, MH, ME).transpose(2, 1, 0),
        "gate_bias": _np.concatenate([a["b_igate"], a["b_fgate"]], axis=1),
        "w_mq": a["w_mq"][0],
        "w_mk": a["w_mk"][0],
        "mh_g": a["mh_norm_g"],
        "w_out": a["w_out"][0],
        "ln1": _np.concatenate([a["ln1_g"], a["ln1_b"]], axis=0),
        "w_query": a["peer_w_query"][0],
        "sub_keys": a["peer_sub_keys"][0].transpose(3, 0, 1, 2),
        "w_down": a["peer_w_down"][0],
        "w_up": a["peer_w_up"][0],
        "ln2": _np.concatenate([a["ln2_g"], a["ln2_b"]], axis=0),
        "consts": shape_constants(),
    }
    nc = _bacc.Bacc("TRN2", target_bir_lowering=False, num_devices=1)
    arrays, args = {}, []
    for name, v in laid.items():
        arrays[f"in_{name}"] = _np.ascontiguousarray(v)
        args.append(nc.dram_tensor(f"in_{name}", v.shape, _mybir.dt.from_np(v.dtype), kind="ExternalInput").ap())
    args.append(nc.dram_tensor("out_0", (S, D), F32, kind="ExternalOutput").ap())
    build(nc, *args)
    r = _run(nc, [arrays], core_ids=[0])
    return _np.asarray(r.results[0]["out_0"]).reshape(1, S, D)
```

```python
from contextlib import ExitStack

import concourse.bass as bass
from concourse import mybir

F32 = mybir.dt.float32
F32R = mybir.dt.float32r
U32 = mybir.dt.uint32
ALU = mybir.AluOpType
ACT = mybir.ActivationFunctionType
X = mybir.AxisListType.X

P = 128
S = 512
D = 1024
NB = S // P
KD = D // P
W = 512
AH, AE = 8, 64
MH, ME = 4, 128
TAPS = 4
PH, NK, TOPK = 8, 128, 16
ALPHA = 2.0 ** 0.25
EPS = 1e-5
NEG = -1e30
LOWEST = -3e38
STEPS = NB * PH
TILES = NK
TPS = 3
GATE_STEPS = STEPS + PH
LONE_STEPS = TILES // TPS - GATE_STEPS
REST = TILES % TPS
PIECE = NK // 4
TOK = 4
GPS = 4
GROUPS = STEPS * GPS
UTS = 4
HALF = P // 2

GATES = 0
XM, OM, VM, QA = 1, 5, 9, 13
MQ, MK, KM = 17, 21, 25
KA, VA = 29, 33
PROJ_ITEMS = 37


def mixing_order():
    order = []
    for c in range(NB):
        if c == 0:
            between = [[], [("ml", 0, 0)], [], [("ml", 0, 1)], [("ml", 0, 2)], [("ml", 0, 3), ("ml", 1, 0)],
                       [("ml", 0, 4)], [("ml", 1, 1)], [("ml", 1, 2)], [("ml", 1, 3)], [("ml", 1, 4)]]
        else:
            p, n = c - 1, c + 1
            between = [[("cat", p, 0)], [("cat", p, 1)], [("out", p, 0)], [("ml", n, 0)], [("out", p, 1)],
                       [("ml", n, 1), ("ln", p, 0)], [("ml", n, 2)], [("ln", p, 1), ("ml", n, 3)],
                       [("h1T", p, 0)], [("ml", n, 4), ("h1T", p, 1)], []]
        for i in range(AH + 3):
            order.append(("head", c, i))
            order += [stage for stage in between[i] if stage[:2] != ("ml", NB)]
    order += [(kind, NB - 1, i) for kind in ("cat", "out", "ln", "h1T") for i in range(2)]
    return order


def bank_items(order):
    score, turn = {}, {}
    for kind, c, i in order:
        if (kind, i) == ("ml", 0) or kind == "out" or (kind == "head" and i < AH):
            score[kind, c, i] = NB + len(score)
        if (kind, i) == ("ml", 1) or kind in ("cat", "h1T"):
            turn[kind, c, i] = len(turn)
        if kind == "head" and 2 <= i <= AH + 1:
            turn[kind, c, i - 2] = len(turn)
    return score, turn


def build(nc, xT, x, w_in, w_gate, conv, gate_bias, w_mq, w_mk, mh_g, w_out, ln1, w_query, sub_keys,
          w_downT, w_up, ln2, consts, gates_dram, act_dram, out):
    order = mixing_order()
    score_item, turn_item = bank_items(order)
    h1T_items = {turn_item["h1T", c, i]: 2 * c + i for c in range(NB) for i in range(2)}
    score_items, turn_items = NB + len(score_item), len(turn_item)

    with ExitStack() as ctx:
        def sem(name):
            return ctx.enter_context(nc.semaphore(name))

        def sb(stack, name, shape, dt=F32):
            return stack.enter_context(nc.sbuf_tensor(name, shape, dt))

        pj = [ctx.enter_context(nc.psum_tensor(f"proj{i}", [P, 512], F32)) for i in range(2)]
        ps = [ctx.enter_context(nc.psum_tensor(f"score{i}", [P, 512], F32)) for i in range(2)]
        pt = [ctx.enter_context(nc.psum_tensor(f"turn{i}", [P, 512], F32)) for i in range(2)]
        py = ctx.enter_context(nc.psum_tensor("py", [P, 2, 512], F32))
        po, pi = py[:, 0, :], py[:, 1, :]

        cst = sb(ctx, "cst", [P, 5 * P + 2 * S + 32])
        ident, triu, ones = cst[:, 0:P], cst[:, P:2 * P], cst[:, 2 * P:3 * P]
        tril_bias = cst[:, 3 * P:4 * P]
        attn_bias = cst[:, 4 * P:4 * P + S]
        attn_count = cst[:, 4 * P + S:4 * P + 2 * S]
        iota16 = cst[:, 4 * P + 2 * S:4 * P + 2 * S + 16]
        eps = cst[:, 4 * P + 2 * S + 16:4 * P + 2 * S + 17]
        iota128 = cst[:, 4 * P + 2 * S + 32:5 * P + 2 * S + 32]
        h1 = sb(ctx, "h1", [P, NB, D])
        stats = sb(ctx, "stats", [P, 4, 6])
        mv = sb(ctx, "mv", [P, 4, 2])
        sd = sb(ctx, "sd", [P, 4])
        rstd = sb(ctx, "rstd", [P, 4])
        ln_stats = sb(ctx, "ln_stats", [P, 2, 6])
        ln_mv = sb(ctx, "ln_mv", [P, 2])
        ln_sd = sb(ctx, "ln_sd", [P, 2])
        shift = sb(ctx, "shift", [P, 4])

        h1T_hi = sb(ctx, "h1T_hi", [P, KD, S], F32R)

        xT_scope = ExitStack()
        xT_sb = sb(xT_scope, "xT_sb", [P, KD, S])
        xT_scope.close()
        h1T_lo = sb(ctx, "h1T_lo", [P, KD, S], F32R)
        mixing = ExitStack()
        ln1_sb = sb(mixing, "ln1_sb", [P, 2, D])
        mhg = sb(mixing, "mhg", [P, W])
        wp = [sb(mixing, f"wpiece{i}", [P, KD, W]) for i in range(2)]
        wg_sb = sb(mixing, "wg_sb", [P, KD, 2 * MH])
        conv_sb = sb(mixing, "conv_sb", [P, MH, TAPS + 1])
        gbias = sb(mixing, "gbias", [P, 2 * MH])
        xm = sb(mixing, "xm", [P, MH, S + TAPS])
        vm = sb(mixing, "vm", [P, NB, W])
        om = sb(mixing, "om", [P, NB, W])
        qa = sb(mixing, "qa", [P, 4, S])
        ka = sb(mixing, "ka", [P, 4, S])
        va = sb(mixing, "va", [P, NB, W])
        xc = sb(mixing, "xc", [P, MH, S])
        qm = sb(mixing, "qm", [P, MH, S])
        kmT = sb(mixing, "kmT", [P, MH, S])
        km = sb(mixing, "km", [P, NB, MH, ME])
        rm = sb(mixing, "rm", [P, NB, MH, P])
        wmq, wmk = rm[:, 0], rm[:, 1]
        diag_r = xm[:, :, 0:S].rearrange("p c (h s) -> p c h s", h=MH)
        cat = sb(mixing, "cat", [P, W])
        catT = sb(mixing, "catT", [P, KD, P])
        ct = sb(mixing, "ct", [P, MH, ME])
        nst = sb(mixing, "nst", [P, MH])
        sw = [sb(mixing, f"sw{i}", [P, S]) for i in range(2)] + [xm[:, 0, 0:S]]
        pT = [sb(mixing, f"pT{i}", [P, S]) for i in range(2)]
        gt = sb(mixing, "gt", [P, NB, 2 * MH])
        sv = sb(mixing, "sv", [P, 20, 16])
        ew = sb(mixing, "ew", [P, 4, 16])
        hv = sb(mixing, "hv", [P, 8, AH])
        ip, ff, nf, lg, logf, bc, bl, rr, rmax, mmax, mxl, mx, nmx, lexp, mn = (
            sv[:, i, :] for i in range(15))
        mprev = sv[:, 15:17, :].rearrange("p a b -> p (a b)")
        w_inter, e_mt, a_dec, w_k = (ew[:, i, :] for i in range(4))
        kw, inter, swm, pTm = (xc[:, :, i * P:(i + 1) * P] for i in range(4))
        mixing.close()

        scores_scope = ExitStack()
        scores = sb(scores_scope, "scores", [P, STEPS, 2 * NK])
        query = ExitStack()
        wq = [sb(query, f"wq{i}", [P, KD, 2 * NK]) for i in range(2)]
        wq_hi = [sb(query, f"wq_hi{i}", [P, KD, 2 * NK], F32R) for i in range(2)]
        wq_lo = [sb(query, f"wq_lo{i}", [P, KD, 2 * NK], F32R) for i in range(2)]
        sk = [sb(query, f"sk{i}", [P, 2, NK]) for i in range(2)]
        qry = [sb(query, f"qry{i}", [P, 2, S]) for i in range(2)]
        query.close()

        down = ExitStack()
        stage = [sb(down, f"stage{i}", [P, NK, HALF]) for i in range(2)]
        raw = ExitStack()
        wd = [sb(raw, f"wd{i}", [P, KD, P]) for i in range(TPS)]
        raw.close()
        wd_lo = [sb(down, f"wd_lo{i}", [P, KD, P], F32R) for i in range(TPS)]
        wd_hi = [sb(down, f"wd_hi{i}", [P, KD, P], F32R) for i in range(TPS)]
        gel = [sb(down, f"gel{i}", [P, S]) for i in range(TPS)]
        hot2 = sb(down, "hot2", [P, 2, TOK, P])
        hot1 = sb(down, "hot1", [P, 2, TOK, P])
        picks = sb(down, "picks", [P, 3, PH * TOPK])
        picksT = sb(down, "picksT", [P, 3, P])
        cols = sb(down, "cols", [P, 3, 4 * TOK])
        sc = sb(down, "sc", [P, 2, NK])
        sc2 = sb(down, "sc2", [P, 2, NK])
        top = sb(down, "top", [P, 2, TOPK])
        topi = sb(down, "topi", [P, 2, TOPK], U32)
        cand = sb(down, "cand", [P, TOPK * TOPK])
        cand2 = sb(down, "cand2", [P, TOPK * TOPK])
        best = sb(down, "best", [P, TOPK])
        pos = sb(down, "pos", [P, TOPK], U32)
        hl = sb(down, "hl", [P, 2, TOPK], U32)
        eq = sb(down, "eq", [P, 2, TOPK, TOPK])
        e12g = sb(down, "e12g", [P, 3, TOPK])
        shifted = sb(down, "shifted", [P, TOPK])
        gate_exp = sb(down, "gate_exp", [P, TOPK])
        gate_sum = sb(down, "gate_sum", [P, 1])
        gate_rs = sb(down, "gate_rs", [P, 1])
        down.close()
        scores_scope.close()

        wu = [sb(ctx, f"wu{i}", [P, D]) for i in range(2)]
        wu_hi = [sb(ctx, f"wu_hi{i}", [P, D], F32R) for i in range(2)]
        wu_lo = [sb(ctx, f"wu_lo{i}", [P, D], F32R) for i in range(2)]
        gts = [sb(ctx, f"gates{i}", [P, 2 * NB, UTS, HALF]) for i in range(2)]
        acts = [sb(ctx, f"acts{i}", [P, UTS, S]) for i in range(2)]
        ga = [sb(ctx, f"ga{i}", [P, S]) for i in range(2)]
        ga_hi = [sb(ctx, f"ga_hi{i}", [P, S], F32R) for i in range(2)]
        ga_lo = [sb(ctx, f"ga_lo{i}", [P, S], F32R) for i in range(2)]
        ln2_sb = sb(ctx, "ln2_sb", [P, 2, D])

        const_in, x_in, xT_in, small_in, ln2_in = (sem(n) for n in (
            "const_in", "x_in", "xT_in", "small_in", "ln2_in"))
        wp_in = [sem(f"wp_in{i}") for i in range(2)]
        wq_in = [sem(f"wq_in{i}") for i in range(2)]
        proj_done, proj_copied = sem("proj_done"), sem("proj_copied")
        pads_zero = sem("pads_zero")
        conv_done, conv_exp, xc_ready = sem("conv_done"), sem("conv_exp"), sem("xc_ready")
        gate_pre, gate_ln, logf_ready, gate_sums = (sem(n) for n in (
            "gate_pre", "gate_ln", "logf_ready", "gate_sums"))
        r_ready, diag_ready, args_ready, weights_ready = (sem(n) for n in (
            "r_ready", "diag_ready", "args_ready", "weights_ready"))
        ps_done, ps_read = sem("ps_done"), sem("ps_read")
        pt_done, pt_copied = sem("pt_done"), sem("pt_copied")
        mexp_done, mp_ready, kw_ready = sem("mexp_done"), sem("mp_ready"), sem("kw_ready")
        inter_scaled, num_done, mpv_done = sem("inter_scaled"), sem("num_done"), sem("mpv_done")
        ml_ready, ln_var_ready, ln_sd_ready, wg_in = (sem(n) for n in (
            "ml_ready", "ln_var_ready", "ln_sd_ready", "wg_in"))
        upd_done, state_ready = sem("upd_done"), sem("state_ready")
        var_ready, sd_ready, ogate_exp = sem("var_ready"), sem("sd_ready"), sem("ogate_exp")
        masked, aexp_done, ap_ready, pv_done = (sem(n) for n in ("masked", "aexp_done", "ap_ready", "pv_done"))
        cat_ready, h1_ready = sem("cat_ready"), sem("h1_ready")
        dve_step, act_step = sem("dve_step"), sem("act_step")
        qry_done, qry_copied, sc_done, sc_copied = (sem(n) for n in (
            "qry_done", "qry_copied", "sc_done", "sc_copied"))
        h1T_split, wq_hi_ready, wq_lo_ready = sem("h1T_split"), sem("wq_hi_ready"), sem("wq_lo_ready")
        wd_in = [sem(f"wd_in{i}") for i in range(TPS)]
        wd_hi_ready, wd_lo_ready, down_done, gelu_done = (sem(n) for n in (
            "wd_hi_ready", "wd_lo_ready", "down_done", "gelu_done"))
        act_out = [sem(f"act_out{i}") for i in range(TPS)]
        stage_out = [sem(f"stage_out{i}") for i in range(2)]
        shifted_ready, gates_ready, picks_ready, turned_ready, picksT_ready = (sem(n) for n in (
            "shifted_ready", "gates_ready", "picks_ready", "turned_ready", "picksT_ready"))
        hot_ready, gmat_done, gmat_staged = sem("hot_ready"), sem("gmat_done"), sem("gmat_staged")
        loop_step, dve_alone = sem("loop_step"), sem("dve_alone")
        wu_in = [sem(f"wu_in{i}") for i in range(2)]
        ga_in = [sem(f"ga_in{i}") for i in range(2)]
        wu_hi_ready, wu_lo_ready, ga_ready, ga_hi_ready, ga_lo_ready, up_done = (sem(n) for n in (
            "wu_hi_ready", "wu_lo_ready", "ga_ready", "ga_hi_ready", "ga_lo_ready", "up_done"))
        rstd2_ready, norm_ready, scaled_ready, out_ready, out_sent = (sem(n) for n in (
            "rstd2_ready", "norm_ready", "scaled_ready", "out_ready", "out_sent"))
        var2_ready, sd2_ready = sem("var2_ready"), sem("sd2_ready")

        block = ctx.enter_context(nc.Block())
        down_banks = [pj[0][:], pj[1][:], po]

        piece_used = [OM, VM, QA, MQ, VA, PROJ_ITEMS]

        @block.sync
        def _(sp):
            sp.dma_start(xT_sb[:], xT.rearrange("(k p) t -> p k t", p=P)).then_inc(xT_in, 16)
            sp.dma_start(wg_sb[:], w_gate).then_inc(wg_in, 16)
            w_order = [3, 5, 4, 0, 1, 2]
            for n in range(8):
                if n >= 2:
                    sp.wait_ge(proj_done, piece_used[n - 2])
                src = (w_in[:, w_order[n] * W:(w_order[n] + 1) * W] if n < 6
                       else w_out[:, (n - 6) * W:(n - 5) * W])
                sp.dma_start(wp[n % 2][:], src.rearrange("(k p) n -> p k n", p=P)).then_inc(wp_in[n % 2], 16)
                if n == 0:
                    sp.dma_start(cst[:], consts).then_inc(const_in, 16)
                    sp.dma_start(conv_sb[:], conv).then_inc(small_in, 16)
                    sp.dma_start(gbias[:], gate_bias.to_broadcast([P, 2 * MH])).then_inc(small_in, 16)
                    sp.dma_start(wmq, w_mq.rearrange("h e f -> e h f")).then_inc(small_in, 16)
                    sp.dma_start(wmk, w_mk.rearrange("h e f -> e h f")).then_inc(small_in, 16)
                    sp.dma_start(mhg[:], mh_g.to_broadcast([P, W])).then_inc(small_in, 16)
                    for i in range(2):
                        sp.dma_start(ln1_sb[:, i, :], ln1[i:i + 1, :].to_broadcast([P, D])).then_inc(small_in, 16)
                    for c in range(NB):
                        sp.dma_start(h1[:, c, :], x[c * P:(c + 1) * P, :]).then_inc(x_in, 16)
            for h in range(PH):
                if h < 2:
                    sp.wait_ge(h1_ready, NB)
                    sp.wait_ge(pt_copied, turn_items)
                else:
                    sp.wait_ge(wq_lo_ready, h - 1)
                    sp.wait_ge(sc_done, 2 * (h - 1))
                sp.dma_start(wq[h % 2][:], w_query[:, h * 2 * NK:(h + 1) * 2 * NK].rearrange(
                    "(k p) n -> p k n", p=P)).then_inc(wq_in[h % 2], 16)
                sp.dma_start(sk[h % 2][:], sub_keys[:, h]).then_inc(wq_in[h % 2], 16)
            sp.wait_ge(sc_copied, 2 + 2 * PH)
            def load_down(n, j):
                sp.wait_ge(down_done, n + 1)
                sp.dma_start(wd[j][:].rearrange("p k e -> p (k e)"),
                             w_downT[bass.ds(n * P, P), :]).then_inc(wd_in[j], 16)

            with sp.Fori(0, TILES // TPS, 1) as s:
                for j in range(TPS):
                    load_down(s * TPS + j, j)
            for j in range(REST):
                load_down(TILES - REST + j, j)
            sp.wait_ge(picks_ready, STEPS)
            for q in range(2):
                sp.wait_ge(stage_out[q], 16 * (4 * NB + 1))
            for i in range(2):
                sp.dma_start(ln2_sb[:, i, :], ln2[i:i + 1, :].to_broadcast([P, D])).then_inc(ln2_in, 16)
            for part in range(2):
                for j in range(TPS):
                    tiles = (part + 1) * TILES // 2
                    sp.wait_ge(act_out[j], 16 * ((tiles - j + TPS - 1) // TPS + 1))
                with sp.Fori(part * (TILES // UTS // 4), (part + 1) * (TILES // UTS // 4), 1) as pair:
                    for q in range(2):
                        for j in range(UTS):
                            n = pair * (2 * UTS) + (q * UTS + j)
                            if j == 0:
                                sp.wait_ge(ga_ready, n + UTS)
                                sp.dma_start(gts[q][:].rearrange("p n i t -> p n (i t)"),
                                             gates_dram[:, :, bass.ds(n * HALF, UTS * HALF)]).then_inc(ga_in[q], 16)
                                sp.dma_start(acts[q][:], act_dram[:, bass.ds(n, UTS), :]).then_inc(ga_in[q], 16)
                            sp.wait_ge(wu_lo_ready, n + 1)
                            sp.dma_start(wu[j % 2][:], w_up[bass.ds(n * P, P), :]).then_inc(wu_in[j % 2], 16)
            for b in range(NB):
                sp.wait_ge(out_ready, b + 1)
                sp.dma_start(out[b * P:(b + 1) * P, :], h1[:, b, :]).then_inc(out_sent, 16)
            sp.wait_ge(out_sent, 16 * NB)

        def down_steps(eng, body, after_group=None):
            body(0, first=True, gates=False)
            with eng.Fori(1, PH, 1) as h:
                body(h, gates=False)
            if after_group:
                after_group(0)

            def half_block(block, half, select=True, store=True):
                with eng.Fori(0, PH // 2, 1) as quarter:
                    body(quarter + (block * PH + half * (PH // 2)), select=select, store=store,
                         half=half, quarter=quarter, block=block)

            half_block(1, 0, store=False)
            with eng.Fori(1, NB - 1, 1) as g:
                half_block(g, 1)
                if after_group:
                    after_group(g)
                half_block(g + 1, 0)
            half_block(NB - 1, 1)
            if after_group:
                after_group(NB - 1)
            half_block(NB, 0, select=False)
            half_block(NB, 1, select=False)
            with eng.Fori(0, LONE_STEPS, 1) as lone:
                body(lone + GATE_STEPS, select=False, gates=False, lone=lone)
            body(GATE_STEPS + LONE_STEPS, select=False, gates=False, tiles=REST)

        @block.tensor
        def _(pe):
            mm = nc.tensor.matmul

            def open_proj(n):
                if n >= 2:
                    pe.wait_ge(proj_copied, n - 1)
                return pj[n % 2]

            def wide(n0, piece):
                pe.wait_ge(wp_in[piece % 2], 16 * (piece // 2 + 1))
                for i in range(4):
                    o = open_proj(n0 + i)
                    for k in range(KD):
                        last = mm(o[:], wp[piece % 2][:, k, i * P:(i + 1) * P], xT_sb[:, k, :],
                                  start=k == 0, stop=k == KD - 1)
                    last.then_inc(proj_done, 1)

            def tall(n0, piece):
                pe.wait_ge(wp_in[piece % 2], 16 * (piece // 2 + 1))
                for c in range(NB):
                    o = open_proj(n0 + c)
                    for k in range(KD):
                        last = mm(o[:], xT_sb[:, k, c * P:(c + 1) * P], wp[piece % 2][:, k, :],
                                  start=k == 0, stop=k == KD - 1)
                    last.then_inc(proj_done, 1)

            pe.wait_ge(xT_in, 16)
            pe.wait_ge(wg_in, 16)
            for c in range(NB):
                for k in range(KD):
                    last = mm(pj[0][:, c * 8:c * 8 + 8], xT_sb[:, k, c * P:(c + 1) * P], wg_sb[:, k, :],
                              start=k == 0, stop=k == KD - 1)
            last.then_inc(proj_done, 1)
            wide(XM, 0)
            tall(OM, 1)
            tall(VM, 2)
            wide(QA, 3)
            for n0, w in ((MQ, wmq), (MK, wmk)):
                for h in range(MH):
                    o = open_proj(n0 + h)
                    pe.wait_ge(xc_ready, h + 1)
                    mm(o[:], w[:, h, :], xc[:, h, :], start=True, stop=True).then_inc(proj_done, 1)
            for h in range(MH):
                o = open_proj(KM + h)
                for c in range(NB):
                    last = mm(o[:, c * P:(c + 1) * P], xc[:, h, c * P:(c + 1) * P], wmk[:, h, :],
                              start=True, stop=True)
                last.then_inc(proj_done, 1)
            pe.wait_ge(const_in, 16)
            pe.wait_ge(logf_ready, 1)
            mm(pi[:, 0:16], triu, logf, start=True, stop=True)
            mm(pi[:, 16:32], ones, logf, start=True, stop=True).then_inc(gate_sums, 1)
            wide(KA, 4)
            tall(VA, 5)
            pe.wait_ge(diag_ready, NB * MH)
            for c in range(NB):
                if c >= 2:
                    pe.wait_ge(ps_read, c - 1)
                mm(ps[c % 2][:], ones, xm[:, c, 0:S], start=True, stop=True).then_inc(ps_done, 1)

            def open_score(n):
                pe.wait_ge(ps_read, n - 1)
                return ps[n % 2]

            def open_turn(n):
                if n - 2 in h1T_items:
                    pe.wait_ge(h1T_split, h1T_items[n - 2] + 1)
                if n >= 2:
                    pe.wait_ge(pt_copied, n - 1)
                return pt[n % 2]

            def mlstm(c, part):
                t = slice(c * P, (c + 1) * P)
                if part == 0:
                    if c == 0:
                        pe.wait_ge(proj_copied, PROJ_ITEMS)
                    o = open_score(score_item["ml", c, 0])
                    for h in range(MH):
                        last = mm(o[:, h * P:(h + 1) * P], qm[:, h, t], kmT[:, h, t], start=True, stop=True)
                    last.then_inc(ps_done, 1)
                    pe.wait_ge(state_ready, c + 1)
                    if c >= 1:
                        pe.wait_ge(num_done, c)
                    for h in range(MH):
                        mm(pi[:, h * P:(h + 1) * P], qm[:, h, t], ct[:, h, :], start=True, stop=True)
                    for h in range(MH):
                        last = mm(pj[1][:, h:h + 1], qm[:, h, t], nst[:, h:h + 1], start=True, stop=True)
                    if c < NB - 1:
                        pe.wait_ge(kw_ready, c + 1)
                        for h in range(MH):
                            mm(pj[0][:, h * P:(h + 1) * P], kw[:, h, :], vm[:, c, h * ME:(h + 1) * ME],
                               start=True, stop=True)
                        for h in range(MH):
                            last = mm(pj[1][:, 4 + h:5 + h], kw[:, h, :], ones[:, 0:1], start=True, stop=True)
                    last.then_inc(upd_done, 1)
                elif part == 1:
                    pe.wait_ge(mp_ready, c + 1)
                    o = open_turn(turn_item["ml", c, 1])
                    for h in range(MH):
                        last = nc.tensor.transpose(o[:, h * P:(h + 1) * P], swm[:, h, :], ident)
                    last.then_inc(pt_done, 1)
                elif part == 2:
                    pe.wait_ge(pt_copied, turn_item["ml", c, 1] + 1)
                    pe.wait_ge(inter_scaled, c + 1)
                    for h in range(MH):
                        last = mm(pi[:, h * P:(h + 1) * P], pTm[:, h, :], vm[:, c, h * ME:(h + 1) * ME],
                                  start=True, stop=True)
                    last.then_inc(mpv_done, 1)

            def head(c, i):
                if i < AH:
                    o = open_score(score_item["head", c, i])
                    r = slice((i % 2) * AE, (i % 2 + 1) * AE)
                    mm(o[:, 0:(c + 1) * P], qa[r, i // 2, c * P:(c + 1) * P], ka[r, i // 2, 0:(c + 1) * P],
                       start=True, stop=True).then_inc(ps_done, 1)
                if 2 <= i <= AH + 1:
                    g = AH * c + i - 2
                    pe.wait_ge(ap_ready, g + 1)
                    o = open_turn(turn_item["head", c, i - 2])
                    for j in range(c + 1):
                        last = nc.tensor.transpose(o[:, j * P:(j + 1) * P], sw[g % 3][:, j * P:(j + 1) * P], ident)
                    last.then_inc(pt_done, 1)
                if i >= 3:
                    h, g = i - 3, AH * c + i - 3
                    pe.wait_ge(pt_copied, turn_item["head", c, h] + 1)
                    if h == 0 and c >= 1:
                        pe.wait_ge(cat_ready, c)
                    for j in range(c + 1):
                        last = mm(po[:, h * AE:(h + 1) * AE], pT[g % 2][:, j * P:(j + 1) * P],
                                  va[:, j, h * AE:(h + 1) * AE], start=j == 0, stop=j == c)
                    last.then_inc(pv_done, 1)

            def turn_cat(c, i):
                pe.wait_ge(ml_ready if i else cat_ready, c + 1)
                o = open_turn(turn_item["cat", c, i])
                for j in range(4):
                    src = om[:, c, :] if i else cat[:]
                    last = nc.tensor.transpose(o[:, j * P:(j + 1) * P], src[:, j * P:(j + 1) * P], ident)
                last.then_inc(pt_done, 1)

            def project_out(c, i):
                pe.wait_ge(pt_copied, turn_item["cat", c, 1] + 1)
                if c == 0:
                    pe.wait_ge(wp_in[i], 16 * 4)
                o = open_score(score_item["out", c, i])
                for k in range(KD):
                    last = mm(o[:], catT[:, k, :], wp[i][:, k, :], start=k == 0, stop=k == KD - 1)
                last.then_inc(ps_done, 1)

            def turn_h1(c, i):
                pe.wait_ge(h1_ready, c + 1)
                o = open_turn(turn_item["h1T", c, i])
                for j in range(4):
                    k = 4 * i + j
                    last = nc.tensor.transpose(o[:, j * P:(j + 1) * P], h1[:, c, k * P:(k + 1) * P], ident)
                last.then_inc(pt_done, 1)

            for kind, c, i in order:
                if kind == "ml":
                    mlstm(c, i)
                elif kind == "head":
                    head(c, i)
                elif kind == "cat":
                    turn_cat(c, i)
                elif kind == "out":
                    project_out(c, i)
                elif kind == "h1T":
                    turn_h1(c, i)

            pe.wait_ge(pt_copied, turn_items)
            pe.wait_ge(h1T_split, 2 * NB)
            pe.wait_ge(ps_read, score_items)
            with pe.Fori(0, PH // 2, 1) as pair:
                h0 = pair * 2
                for q in range(2):
                    pe.wait_ge(wq_lo_ready, h0 + (q + 1))
                    pe.wait_ge(wq_in[q], h0 * 16 + 32)
                    for side in range(2):
                        pe.wait_ge(qry_copied, h0 * 2 + (2 * q + side + 1))
                        for k in range(KD):
                            cs = slice(side * P, (side + 1) * P)
                            mm(pj[side][:], wq_hi[q][:, k, cs], h1T_hi[:, k, :], start=k == 0, stop=False)
                            mm(pj[side][:], wq_hi[q][:, k, cs], h1T_lo[:, k, :], start=False, stop=False)
                            last = mm(pj[side][:], wq_lo[q][:, k, cs], h1T_hi[:, k, :],
                                      start=False, stop=k == KD - 1)
                        last.then_inc(qry_done, 1)
                    pe.wait_ge(qry_copied, h0 * 2 + (2 * q + 2 + 2))
                    for half in range(2):
                        pe.wait_ge(sc_copied, h0 * 2 + (2 * q + half + 1))
                        for b in range(2):
                            for side in range(2):
                                blk = 2 * half + b
                                last = mm(ps[half][:, (2 * b + side) * P:(2 * b + side + 1) * P],
                                          qry[q][:, side, blk * P:(blk + 1) * P], sk[q][:, side, :],
                                          start=True, stop=True)
                        last.then_inc(sc_done, 1)

            pe.wait_ge(sc_copied, 2 + 2 * PH)

            def step(s, first=False, gates=True, select=True, tiles=TPS, half=0, quarter=0, block=0,
                     store=True, lone=None):
                for j in range(TPS):
                    for group in ((0,), (1,), (2, 3))[j] if gates else ():
                        m = (s - PH) * GPS + group
                        pe.wait_ge(hot_ready, m + 1)
                        pe.wait_ge(gmat_staged, m + 1)
                        for r in range(TOK):
                            last = mm(ps[group % 2][:, r * P:(r + 1) * P], hot2[:, group % 2, r, :],
                                      hot1[:, group % 2, r, :], start=True, stop=True)
                        last.then_inc(gmat_done, 1)
                    if j < tiles:
                        pe.wait_ge(wd_lo_ready, s * TPS + (j + 1))
                        pe.wait_ge(gelu_done, s * TPS + (j + 1))
                        o = down_banks[j]
                        for k in range(KD):
                            mm(o, wd_hi[j][:, k, :], h1T_hi[:, k, :], start=k == 0, stop=False)
                            mm(o, wd_hi[j][:, k, :], h1T_lo[:, k, :], start=False, stop=False)
                            last = mm(o, wd_lo[j][:, k, :], h1T_hi[:, k, :], start=False, stop=k == KD - 1)
                        last.then_inc(down_done, 1)

            def turn_picks(g):
                pe.wait_ge(picks_ready, (g + 1) * PH)
                for i in range(3):
                    last = nc.tensor.transpose(pt[0][:, i * P:(i + 1) * P], picks[:, i, :], ident)
                last.then_inc(turned_ready, 1)

            down_steps(pe, step, after_group=turn_picks)

            banks = [[pj[0], pj[1]], [ps[0], ps[1]], [pt[0], pt[1]], [py[:, 0, :], py[:, 1, :]]]
            pe.wait_ge(gmat_staged, 2 + GROUPS)
            pe.wait_ge(gelu_done, TPS + TILES)
            pe.wait_ge(picksT_ready, NB)

            def up(n, q, first=False):
                pe.wait_ge(wu_lo_ready, n + 3)
                pe.wait_ge(ga_lo_ready, n + 1)
                for b in range(NB):
                    t = slice(b * P, (b + 1) * P)
                    for ga_part, wu_part in ((ga_hi, wu_hi), (ga_hi, wu_lo), (ga_lo, wu_hi)):
                        for i in range(2):
                            last = mm(banks[b][i][:, 0:512], ga_part[q][:, t],
                                      wu_part[q][:, i * 512:(i + 1) * 512],
                                      start=first and (ga_part, wu_part) == (ga_hi, wu_hi), stop=False,
                                      skip_group_check=True)
                last.then_inc(up_done, 1)

            for q in range(2):
                up(q, q, first=q == 0)
            with pe.Fori(1, TILES // 2, 1) as pair:
                for q in range(2):
                    up(pair * 2 + q, q)

        @block.scalar
        def _(act):
            run = nc.scalar.activation
            steps = [0]

            def dep(ins):
                steps[0] += 1
                ins.then_inc(act_step, 1)
                act.wait_ge(act_step, steps[0])

            def take(n, dst, scale=1.0):
                act.wait_ge(proj_done, n + 1)
                src = pj[n % 2][:, 0:dst.free_size()] if n == GATES else pj[n % 2][:]
                if len(dst.shape) == 3:
                    src = src.rearrange("p (a b) -> p a b", a=dst.shape[1])
                run(dst, src, ACT.Copy, scale=scale).then_inc(proj_copied, 1)

            take(GATES, gt[:])

            def silu_exp(h):
                act.wait_ge(conv_done, h + 1)
                run(xc[:, h, :], kmT[:, h, :], ACT.Exp, scale=-1.0).then_inc(conv_exp, 1)

            for h in range(MH):
                act.wait_ge(pads_zero, 1)
                take(XM + h, xm[:, h, TAPS - 1:TAPS - 1 + S])
                if h >= 1:
                    silu_exp(h - 1)
            for c in range(NB):
                act.wait_ge(proj_done, OM + c + 1)
                run(om[:, c, :], pj[(OM + c) % 2][:], ACT.Exp, scale=-1.0).then_inc(proj_copied, 1)
                if c == 0:
                    silu_exp(MH - 1)
            act.wait_ge(gate_pre, 1)
            dep(run(lexp, mn, ACT.Exp))
            act.wait_ge(const_in, 16)
            run(lg, lexp, ACT.Ln, bias=ones[:, 0:1]).then_inc(gate_ln, 1)
            for c in range(NB):
                take(VM + c, vm[:, c, :])
            for i in range(4):
                take(QA + i, qa[:, i, :])
            act.wait_ge(xc_ready, MH)
            for h in range(MH):
                take(MQ + h, qm[:, h, :], scale=float(ME) ** -0.5)
            for h in range(MH):
                take(MK + h, kmT[:, h, :])
            for h in range(MH):
                take(KM + h, km[:, :, h, :])
            act.wait_ge(r_ready, 1)
            for i in range(4):
                for k in range(i * MH, (i + 1) * MH):
                    run(diag_r[:, i, k % MH, :], ident, ACT.Copy, scale=rr[:, k:k + 1]).then_inc(diag_ready, 1)
                take(KA + i, ka[:, i, :])
            for c in range(NB):
                take(VA + c, va[:, c, :])
            act.wait_ge(args_ready, 1)
            run(ew[:].rearrange("p a b -> p (a b)"), ew[:].rearrange("p a b -> p (a b)"), ACT.Exp).then_inc(weights_ready, 1)
            act.wait_ge(weights_ready, 1)

            def turned(n, dst):
                act.wait_ge(pt_done, n + 1)
                src = pt[n % 2][:, 0:dst.free_size()]
                if len(dst.shape) == 3:
                    src = src.rearrange("p (a b) -> p a b", a=dst.shape[1])
                run(dst, src, ACT.Copy).then_inc(pt_copied, 1)

            def mlstm(c, part):
                if part == 0:
                    if c == 0:
                        act.wait_ge(proj_done, KA)
                    else:
                        act.wait_ge(pt_done, turn_item["ml", c - 1, 1] + 1)
                    for h in range(MH):
                        k = 4 * c + h
                        last = run(swm[:, h, :], rm[:, c, h, :], ACT.Exp, bias=nmx[:, k:k + 1])
                    last.then_inc(mexp_done, 1)
                    if c < NB - 1:
                        if c >= 1:
                            act.wait_ge(upd_done, c)
                        for h in range(MH):
                            last = run(kw[:, h, :], km[:, c, h, :], ACT.Copy, scale=w_k[:, 4 * c + h:4 * c + h + 1])
                        last.then_inc(kw_ready, 1)
                elif part == 1:
                    act.wait_ge(upd_done, c + 1)
                    if c >= 1:
                        act.wait_ge(ml_ready, c)
                    for h in range(MH):
                        last = run(inter[:, h, :], pi[:, h * P:(h + 1) * P], ACT.Copy,
                                   scale=w_inter[:, 4 * c + h:4 * c + h + 1])
                    last.then_inc(inter_scaled, 1)
                    if c >= 1:
                        act.wait_ge(mpv_done, c)
                    turned(turn_item["ml", c, 1], pTm)
                elif part == 3:
                    act.wait_ge(var_ready, c + 1)
                    run(sd[:], mv[:, :, 1], ACT.Sqrt, bias=eps).then_inc(sd_ready, 1)

            def head(c, i):
                if i < AH:
                    g = AH * c + i
                    act.wait_ge(masked, g + 1)
                    v = sw[g % 3][:, 0:(c + 1) * P]
                    run(v, v, ACT.Exp, scale=float(AE) ** -0.5, bias=hv[:, 0, i:i + 1]).then_inc(aexp_done, 1)
                if 2 <= i <= AH + 1:
                    g = AH * c + i - 2
                    if g >= 2:
                        act.wait_ge(pv_done, g - 1)
                    turned(turn_item["head", c, i - 2], pT[g % 2][:, 0:(c + 1) * P])

            for kind, c, i in order:
                if kind == "ml":
                    mlstm(c, i)
                elif kind == "head":
                    head(c, i)
                elif kind == "cat":
                    if c >= 1:
                        act.wait_ge(ps_done, score_item["out", c - 1, 1] + 1)
                    turned(turn_item["cat", c, i], catT[:, 4 * i:4 * i + 4, :])
                elif kind == "ln" and i == 0:
                    act.wait_ge(ln_var_ready, c + 1)
                    run(ln_sd[:, 0:1], ln_mv[:, 1:2], ACT.Sqrt, bias=eps).then_inc(ln_sd_ready, 1)
                elif kind == "h1T":
                    turned(turn_item["h1T", c, i], h1T_hi[:, 4 * i:4 * i + 4, c * P:(c + 1) * P])

            act.sem_inc(qry_copied, 2)

            def split_query(q, n):
                act.wait_ge(wq_in[q], n)
                run(wq_hi[q][:], wq[q][:], ACT.Copy).then_inc(wq_hi_ready, 1)

            with act.Fori(0, PH // 2, 1) as pair:
                h0 = pair * 2
                for q in range(2):
                    split_query(q, h0 * 16 + 32)
                for q in range(2):
                    for side in range(2):
                        act.wait_ge(qry_done, h0 * 2 + (2 * q + side + 1))
                        run(qry[q][:, side, :], pj[side][:], ACT.Copy).then_inc(qry_copied, 1)

            act.sem_inc(gelu_done, TPS)
            act.sem_inc(gmat_staged, 2)
            act.sem_inc(up_done, 2)
            for q in range(TPS):
                act.sem_inc(act_out[q], 16)
            for q in range(2):
                act.sem_inc(stage_out[q], 16)

            def gelu(s, j):
                n = s * TPS + j
                act.wait_ge(down_done, n + (TPS + 1))
                act.wait_ge(act_out[j], (s + 1) * 16)
                run(gel[j][:], down_banks[j], ACT.Gelu).then_inc(gelu_done, 1)
                act.wait_ge(gelu_done, n + (TPS + 1))
                act.dma_start(act_dram[:, n, :] if isinstance(n, int) else
                              act_dram[:, bass.ds(n, 1), :].rearrange("p a t -> p (a t)"),
                              gel[j][:]).then_inc(act_out[j], 16)

            def high_part(j, s):
                act.wait_ge(wd_in[j], s * 16 + 16)
                run(wd_hi[j][:], wd[j][:], ACT.Copy).then_inc(wd_hi_ready, 1)

            def step(s, first=False, gates=True, select=True, tiles=TPS, half=0, quarter=0, block=0,
                     store=True, lone=None):
                for j in range(GPS):
                    if j < tiles:
                        if tiles == TPS or j + 1 < tiles:
                            high_part((j + 1) % TPS, s + (j + 1) // TPS)
                        if select and j == 1:
                            act.wait_ge(shifted_ready, s + 1)
                            run(gate_exp[:], shifted[:], ACT.Exp, accum_out=gate_sum[:]).then_inc(gates_ready, 1)
                        if j:
                            gelu(s, j - 1)
                        elif not first:
                            gelu(s - 1, TPS - 1)
                        if j == 1 and gates and store:
                            store_gates(1 - half, (block - 1) * 2 + (half - 1), quarter,
                                        (block - 1) * (PH * GPS) + (half * (PH // 2 * GPS) + 2))
                        if j < 2 and lone is not None:
                            store_gates(1, 2 * NB - 1, lone * 2 + j, GROUPS + 2)
                    if gates:
                        m = (s - PH) * GPS + j
                        act.wait_ge(gmat_done, m + 3)
                        if j == 0:
                            act.wait_ge(stage_out[half], block * 64 - 48)
                        run(stage[half][:, :, bass.ds(quarter * 16 + TOK * j, TOK)],
                            ps[j % 2][:].rearrange("p (t i) -> p i t", t=TOK), ACT.Copy).then_inc(gmat_staged, 1)

            def store_gates(buffer, n, piece, staged):
                act.wait_ge(gmat_staged, staged)
                half_block = (gates_dram[:, n, :] if isinstance(n, int) else
                              gates_dram[:, bass.ds(n, 1), :].rearrange("p a t -> p (a t)"))
                act.dma_start(half_block[:, bass.ds(piece * (PIECE * HALF), PIECE * HALF)],
                              stage[buffer][:].rearrange("p i t -> p (i t)")[
                                  :, bass.ds(piece * (PIECE * HALF), PIECE * HALF)]).then_inc(stage_out[buffer], 16)

            act.wait_ge(sc_copied, 2 + 2 * PH)
            high_part(0, 0)
            down_steps(act, step)
            gelu(TILES // TPS, REST - 1)

            with act.Fori(0, TILES // 2, 1) as pair:
                for q in range(2):
                    n = pair * 2 + q
                    act.wait_ge(wu_in[q], pair * 16 + 16)
                    act.wait_ge(up_done, n + 1)
                    run(wu_hi[q][:], wu[q][:], ACT.Copy).then_inc(wu_hi_ready, 1)
                    act.wait_ge(ga_ready, n + 9)
                    run(ga_hi[q][:], ga[q][:], ACT.Copy).then_inc(ga_hi_ready, 1)
            for b in range(NB):
                act.wait_ge(var2_ready, b + 1)
                run(sd[:, b:b + 1], mv[:, b, 1:2], ACT.Sqrt, bias=eps).then_inc(sd2_ready, 1)
                act.wait_ge(rstd2_ready, b + 1)
                run(h1[:, b, :], h1[:, b, :], ACT.Identity, scale=rstd[:, b:b + 1],
                    bias=shift[:, b:b + 1]).then_inc(norm_ready, 1)

        @block.vector
        def _(dve):
            v = nc.vector
            steps = [0]

            def dep(ins):
                steps[0] += 1
                ins.then_inc(dve_step, 1)
                dve.wait_ge(dve_step, steps[0])

            def spread(col, n):
                return col.unsqueeze(2).to_broadcast([P, col.shape[1], n])

            def blocks(ap, n=MH):
                return ap.rearrange("p (a b) -> p a b", a=n)

            dve.wait_ge(small_in, 16 * 7)
            dve.wait_ge(proj_copied, 1)
            g3 = gt[:]
            v.tensor_tensor(ip.rearrange("p (c h) -> p c h", c=NB), g3[:, :, 0:MH],
                            gbias[:, 0:MH].unsqueeze(1).to_broadcast([P, NB, MH]), ALU.add)
            dep(v.tensor_tensor(ff.rearrange("p (c h) -> p c h", c=NB), g3[:, :, MH:2 * MH],
                                gbias[:, MH:2 * MH].unsqueeze(1).to_broadcast([P, NB, MH]), ALU.add))
            dep(v.tensor_scalar(nf, ff, -1.0, None, ALU.mult))
            v.tensor_tensor(mn, nf, ff, ALU.min).then_inc(gate_pre, 1)

            def conv_head(h):
                dve.wait_ge(proj_copied, XM + h + 1)
                y = kmT[:, h, :]
                dep(v.tensor_scalar(y, xm[:, h, 0:S], conv_sb[:, h, 0:1], conv_sb[:, h, TAPS:TAPS + 1],
                                    ALU.mult, ALU.add))
                for j in range(1, TAPS):
                    ins = v.scalar_tensor_tensor(y, xm[:, h, j:j + S], conv_sb[:, h, j:j + 1], y,
                                                 ALU.mult, ALU.add)
                    if j < TAPS - 1:
                        dep(ins)
                ins.then_inc(conv_done, 1)

            def silu(h):
                dve.wait_ge(conv_exp, h + 1)
                dve.wait_ge(conv_done, h + 1)
                dep(v.tensor_scalar(xc[:, h, :], xc[:, h, :], 1.0, None, ALU.add))
                dep(v.reciprocal(xc[:, h, :], xc[:, h, :]))
                v.tensor_tensor(xc[:, h, :], xc[:, h, :], kmT[:, h, :], ALU.mult).then_inc(xc_ready, 1)

            for h in range(MH):
                conv_head(h)
                if h:
                    silu(h - 1)
            silu(MH - 1)
            for c in range(NB):
                dve.wait_ge(proj_copied, OM + c + 1)
                dep(v.tensor_scalar(om[:, c, :], om[:, c, :], 1.0, None, ALU.add))
                dep(v.reciprocal(om[:, c, :], om[:, c, :]))
                dep(v.tensor_tensor(om[:, c, :], om[:, c, :], mhg[:], ALU.mult))
            dve.wait_ge(gate_ln, 1)
            dep(v.tensor_scalar(ff, ff, 0.0, None, ALU.min))
            v.tensor_tensor(logf, ff, lg, ALU.subtract).then_inc(logf_ready, 1)
            dve.wait_ge(gate_sums, 1)
            v.tensor_copy(bl, pi[:, 16:32])
            dep(v.tensor_copy(bc, pi[:, 0:16]))
            v.tensor_tensor(rr, ip, bc, ALU.subtract).then_inc(r_ready, 1)
            for c in range(NB):
                dve.wait_ge(ps_done, c + 1)
                if c == 0:
                    dve.wait_ge(proj_done, KA)
                    dve.wait_ge(const_in, 16)
                v.tensor_reduce(rmax[:, 4 * c:4 * c + 4], blocks(ps[c % 2][:]), X, ALU.max)
                dep(v.tensor_tensor(rm[:, c], blocks(ps[c % 2][:]),
                                    tril_bias.unsqueeze(1).to_broadcast([P, MH, P]), ALU.add))
                v.tensor_reduce(mmax[:, 4 * c:4 * c + 4], rm[:, c], X, ALU.max).then_inc(ps_read, 1)
            dep(v.memset(mprev[:, 0:4], 0.0))
            for c in range(NB):
                g = slice(4 * c, 4 * c + 4)
                dep(v.tensor_tensor(mxl[:, g], mprev[:, g], rmax[:, g], ALU.max))
                dep(v.tensor_tensor(mprev[:, 4 * c + 4:4 * c + 8], mxl[:, g], bl[:, g], ALU.add))
            dve.wait_ge(ps_read, NB)
            dep(v.tensor_tensor(mx, mprev[:, 0:16], mmax, ALU.max))
            v.tensor_scalar(nmx, mx, -1.0, None, ALU.mult)
            v.tensor_tensor(w_inter, mprev[:, 0:16], mx, ALU.subtract)
            v.tensor_tensor(a_dec, mprev[:, 0:16], mxl, ALU.subtract)
            v.tensor_tensor(w_k, rr, mxl, ALU.subtract)
            dep(v.tensor_tensor(e_mt, bc, mx, ALU.add))
            v.tensor_scalar(e_mt, e_mt, -1.0, None, ALU.mult).then_inc(args_ready, 1)
            v.memset(ct[:], 0.0)
            v.memset(nst[:], 0.0).then_inc(state_ready, 1)
            dve.wait_ge(weights_ready, 1)

            rs_sum, den, nden = hv[:, 1, 0:4], hv[:, 2, 0:4], hv[:, 3, 0:4]

            def mlstm(c, part):
                k0, g = 4 * c, slice(4 * c, 4 * c + 4)
                if part == 0:
                    n = score_item["ml", c, 0]
                    dve.wait_ge(mexp_done, c + 1)
                    dve.wait_ge(ps_done, n + 1)
                    v.tensor_tensor(swm, swm, blocks(ps[n % 2][:]), ALU.mult).then_inc(ps_read, 1)
                    dve.wait_ge(ps_read, n + 1)
                    dep(v.tensor_reduce(rs_sum, swm, X, ALU.add))
                    dve.sem_inc(mp_ready, 1)
                elif part == 1:
                    dve.wait_ge(upd_done, c + 1)
                    dep(v.tensor_tensor(den, w_inter[:, g], pj[1][:, 0:4], ALU.mult))
                    dep(v.tensor_tensor(den, den, rs_sum, ALU.add))
                    dep(v.tensor_scalar(nden, den, -1.0, None, ALU.mult))
                    dep(v.tensor_tensor(den, den, nden, ALU.max))
                    dep(v.tensor_tensor(den, den, e_mt[:, g], ALU.max))
                    dep(v.reciprocal(den, den))
                    if c < NB - 1:
                        for h in range(MH):
                            dep(v.scalar_tensor_tensor(ct[:, h, :], ct[:, h, :], a_dec[:, k0 + h:k0 + h + 1],
                                                       pj[0][:, h * P:(h + 1) * P], ALU.mult, ALU.add))
                        dep(v.tensor_tensor(nst[:], nst[:], a_dec[:, g], ALU.mult))
                        v.tensor_tensor(nst[:], nst[:], pj[1][:, 4:8], ALU.add).then_inc(state_ready, 1)
                elif part == 3:
                    dve.wait_ge(inter_scaled, c + 1)
                    dve.wait_ge(mpv_done, c + 1)
                    v.tensor_tensor(inter, inter, blocks(pi), ALU.add).then_inc(num_done, 1)
                    dve.wait_ge(num_done, c + 1)
                    dep(v.tensor_tensor(inter, inter, spread(den, ME), ALU.mult))
                    for h in range(MH):
                        dep(v.bn_stats(stats[:, h, :], inter[:, h, :]))
                    for h in range(MH):
                        ins = v.bn_aggr(mv[:, h, :], stats[:, h, :])
                    ins.then_inc(var_ready, 1)
                elif part == 4:
                    dve.wait_ge(sd_ready, c + 1)
                    dep(v.reciprocal(rstd[:], sd[:]))
                    for h in range(MH):
                        ins = v.tensor_scalar(inter[:, h, :], inter[:, h, :],
                                              mv[:, h, 0:1], rstd[:, h:h + 1], ALU.subtract, ALU.mult)
                    dep(ins)
                    v.tensor_tensor(blocks(om[:, c, :]), inter, blocks(om[:, c, :]), ALU.mult).then_inc(ml_ready, 1)

            def head(c, i):
                wide = slice(0, (c + 1) * P)
                off = slice((NB - 1 - c) * P, S)
                if i < AH:
                    n, g = score_item["head", c, i], AH * c + i
                    dve.wait_ge(ps_done, n + 1)
                    if g >= 3:
                        before = turn_item["head", (g - 3) // AH, (g - 3) % AH]
                        dve.wait_ge(pt_done, before + 1)
                    s = sw[g % 3][:, wide]
                    v.tensor_tensor(s, ps[n % 2][:, wide], attn_bias[:, off], ALU.add).then_inc(ps_read, 1)
                    dve.wait_ge(ps_read, n + 1)
                    dep(v.tensor_reduce(hv[:, 4, i:i + 1], s, X, ALU.max))
                    v.tensor_scalar(hv[:, 0, i:i + 1], hv[:, 4, i:i + 1], -float(AE) ** -0.5, None,
                                    ALU.mult).then_inc(masked, 1)
                if 1 <= i <= AH:
                    g = AH * c + i - 1
                    dve.wait_ge(aexp_done, g + 1)
                    s = sw[g % 3][:, wide]
                    v.tensor_tensor_reduce(out=s, in0=s, in1=attn_count[:, off], scale=1.0, scalar=0.0,
                                           op0=ALU.mult, op1=ALU.add,
                                           accum_out=hv[:, 5, i - 1:i]).then_inc(ap_ready, 1)
                if i == AH + 2:
                    dve.wait_ge(ap_ready, AH * (c + 1))
                    dep(v.reciprocal(hv[:, 6, :], hv[:, 5, :]))
                    dve.wait_ge(pv_done, AH * (c + 1))
                    if c >= 1:
                        dve.wait_ge(pt_done, turn_item["cat", c - 1, 0] + 1)
                    v.tensor_tensor(blocks(cat[:], AH), blocks(po, AH), spread(hv[:, 6, :], AE),
                                    ALU.mult).then_inc(cat_ready, 1)

            def layer_norm(c, part):
                hb = h1[:, c, :]
                if part == 0:
                    v.bn_aggr(ln_mv[:], ln_stats[:]).then_inc(ln_var_ready, 1)
                else:
                    dve.wait_ge(ln_sd_ready, c + 1)
                    dep(v.reciprocal(ln_sd[:, 1:2], ln_sd[:, 0:1]))
                    dep(v.tensor_scalar(hb, hb, ln_mv[:, 0:1], ln_sd[:, 1:2], ALU.subtract, ALU.mult))
                    dep(v.tensor_tensor(hb, hb, ln1_sb[:, 0, :], ALU.mult))
                    v.tensor_tensor(hb, hb, ln1_sb[:, 1, :], ALU.add).then_inc(h1_ready, 1)
                    dve.wait_ge(h1_ready, c + 1)

            for kind, c, i in order:
                if kind == "ml":
                    mlstm(c, i)
                elif kind == "head":
                    head(c, i)
                elif kind == "out":
                    n = score_item["out", c, i]
                    dve.wait_ge(x_in, 16 * NB)
                    dve.wait_ge(ps_done, n + 1)
                    hh = h1[:, c, i * 512:(i + 1) * 512]
                    v.scalar_tensor_tensor(hh, hh, ALPHA, ps[n % 2][:], ALU.mult, ALU.add).then_inc(ps_read, 1)
                    dve.wait_ge(ps_read, n + 1)
                    dep(v.bn_stats(ln_stats[:, i, :], hh))
                elif kind == "ln":
                    layer_norm(c, i)
                elif kind == "h1T":
                    n = turn_item["h1T", c, i]
                    dve.wait_ge(pt_copied, n + 1)
                    part = (slice(None), slice(4 * i, 4 * i + 4), slice(c * P, (c + 1) * P))
                    v.tensor_tensor(h1T_lo[part], blocks(pt[n % 2][:]), h1T_hi[part].bitcast(F32),
                                    ALU.subtract).then_inc(h1T_split, 1)

            dve.wait_ge(pt_copied, turn_items)
            dve.sem_inc(sc_copied, 2)
            s4 = scores[:].rearrange("p (b h) n -> p b (h n)", b=NB)

            def split_query(q, n):
                dve.wait_ge(wq_hi_ready, n)
                v.tensor_tensor(wq_lo[q][:], wq[q][:], wq_hi[q][:].bitcast(F32),
                                ALU.subtract).then_inc(wq_lo_ready, 1)

            with dve.Fori(0, PH // 2, 1) as pair:
                h0 = pair * 2
                for q in range(2):
                    split_query(q, h0 + (q + 1))
                for q in range(2):
                    for half in range(2):
                        dve.wait_ge(sc_done, h0 * 2 + (2 * q + half + 1))
                        v.tensor_copy(s4[:, 2 * half:2 * half + 2, bass.ds((h0 + q) * (2 * NK), 2 * NK)],
                                      ps[half][:].rearrange("p (b n) -> p b n", b=2)).then_inc(sc_copied, 1)
            dve.wait_ge(sc_copied, 2 + 2 * PH)

            def top16(src, src2, vals, inds, dep):
                dep(v.max(vals[:, 0:8], src))
                dep(v.max_index(inds[:, 0:8], vals[:, 0:8], src))
                dep(v.match_replace(src2, vals[:, 0:8], src, LOWEST))
                dep(v.max(vals[:, 8:16], src2))
                dep(v.max_index(inds[:, 8:16], vals[:, 8:16], src2))

            def stand_alone():
                dve.sem_inc(dve_alone, 1)

            dve.sem_inc(down_done, TPS)
            dve.sem_inc(gmat_done, 2)

            ranks = iota16.unsqueeze(1).to_broadcast([P, TOPK, TOPK])

            def step(s, first=False, gates=True, select=True, tiles=TPS, half=0, quarter=0, block=0,
                     store=True, lone=None):
                count = [0]

                def dep(ins):
                    count[0] += 1
                    ins.then_inc(loop_step, 1)
                    dve.wait_ge(loop_step, count[0])

                def select_part(part):
                    if part == 0:
                        dep(v.tensor_copy(sc[:], (scores[:, s, :] if isinstance(s, int) else
                                                  scores[:, bass.ds(s, 1), :].rearrange("p a n -> p (a n)"))
                                          .rearrange("p (s n) -> p s n", s=2)))
                    if part < 2:
                        top16(sc[:, part, :], sc2[:, part, :], top[:, part, :], topi[:, part, :], dep)
                    elif part == 2:
                        dep(v.tensor_tensor(cand[:].rearrange("p (i j) -> p i j", i=TOPK),
                                            top[:, 0, :].unsqueeze(2).to_broadcast([P, TOPK, TOPK]),
                                            top[:, 1, :].unsqueeze(1).to_broadcast([P, TOPK, TOPK]), ALU.add))
                        top16(cand[:], cand2[:], best[:], pos[:], dep)
                        v.tensor_scalar(shifted[:], best[:], best[:, 0:1], None, ALU.subtract).then_inc(shifted_ready, 1)
                    else:
                        v.tensor_scalar(hl[:, 0, :], pos[:], 4, None, ALU.logical_shift_right)
                        dep(v.tensor_scalar(hl[:, 1, :], pos[:], 15, None, ALU.bitwise_and))
                        for side in range(2):
                            ins = v.tensor_tensor(eq[:, side], ranks,
                                                  hl[:, side, :].unsqueeze(2).to_broadcast([P, TOPK, TOPK]),
                                                  ALU.is_equal)
                        dep(ins)
                        for side in range(2):
                            ins = v.tensor_tensor(eq[:, side], eq[:, side],
                                                  topi[:, side, :].unsqueeze(1).to_broadcast([P, TOPK, TOPK]),
                                                  ALU.mult)
                        dep(ins)
                        dep(v.tensor_reduce(e12g[:, 0:2, :], eq[:], X, ALU.add))
                        dve.wait_ge(gates_ready, s + 1)
                        dep(v.reciprocal(gate_rs[:], gate_sum[:]))
                        dep(v.tensor_scalar(e12g[:, 2, :], gate_exp[:], gate_rs[:], None, ALU.mult))
                        head = s if isinstance(s, int) else (s if not gates else quarter + half * (PH // 2))
                        v.tensor_copy(picks[:, :, bass.ds(head * TOPK, TOPK)], e12g[:]).then_inc(picks_ready, 1)

                if gates:
                    dep(v.tensor_copy(cols[:], picksT[:, :, bass.ds(quarter * 16 + half * HALF, 16)]))
                for j in range(TPS):
                    for group in ((0,), (1,), (2, 3))[j] if gates else ():
                        m = (s - PH) * GPS + group
                        dve.wait_ge(gmat_done, m + 1)
                        v.tensor_tensor(hot2[:, group % 2], iota128.unsqueeze(1).to_broadcast([P, TOK, P]),
                                        cols[:, 1, group * TOK:(group + 1) * TOK].unsqueeze(2)
                                        .to_broadcast([P, TOK, P]), ALU.is_equal)
                        for r in range(TOK):
                            t = TOK * group + r
                            last = v.tensor_scalar(hot1[:, group % 2, r, :], iota128, cols[:, 0, t:t + 1],
                                                   cols[:, 2, t:t + 1], ALU.is_equal, ALU.mult)
                        last.then_inc(hot_ready, 1)
                    for part in ((0, 1), (2,), (3,))[j] if select else ():
                        select_part(part)
                if select:
                    dve.wait_ge(picks_ready, s + 1)
                if gates:
                    dve.wait_ge(hot_ready, (s - PH) * GPS + GPS)
                stand_alone()
                dve.sem_clear(loop_step)

            def keep_turned(g):
                dve.wait_ge(turned_ready, g + 1)
                v.tensor_copy(picksT[:], pt[0][:, 0:3 * P].rearrange("p (a b) -> p a b", a=3)).then_inc(picksT_ready, 1)
                dve.wait_ge(picksT_ready, g + 1)
                stand_alone()

            down_steps(dve, step, after_group=keep_turned)

            dve.wait_ge(gmat_done, 2 + GROUPS)
            dve.sem_inc(wu_lo_ready, 2)
            dve.sem_inc(ga_ready, 2 * UTS)
            with dve.Fori(0, TILES // UTS // 2, 1) as pair:
                for q in range(2):
                    for j in range(UTS):
                        n = pair * (2 * UTS) + (q * UTS + j)
                        if j == 0:
                            dve.wait_ge(ga_in[q], pair * 32 + 32)
                        v.tensor_tensor(ga[j % 2][:].rearrange("p (n t) -> p n t", t=HALF),
                                        acts[q][:, j, :].rearrange("p (n t) -> p n t", t=HALF),
                                        gts[q][:, :, j, :], ALU.mult).then_inc(ga_ready, 1)
                        dve.wait_ge(wu_hi_ready, n + 1)
                        v.tensor_tensor(wu_lo[j % 2][:], wu[j % 2][:], wu_hi[j % 2][:].bitcast(F32),
                                        ALU.subtract).then_inc(wu_lo_ready, 1)
                        dve.wait_ge(ga_hi_ready, n + 1)
                        v.tensor_tensor(ga_lo[j % 2][:], ga[j % 2][:], ga_hi[j % 2][:].bitcast(F32),
                                        ALU.subtract).then_inc(ga_lo_ready, 1)

            banks = [[pj[0], pj[1]], [ps[0], ps[1]], [pt[0], pt[1]], [py[:, 0, :], py[:, 1, :]]]
            dve.wait_ge(up_done, 2 + TILES)
            dve.wait_ge(ln2_in, 32)
            def residual(b):
                for i in range(2):
                    hh = h1[:, b, i * 512:(i + 1) * 512]
                    dep(v.scalar_tensor_tensor(hh, hh, ALPHA, banks[b][i][:, 0:512], ALU.mult, ALU.add))
                    dep(v.bn_stats(stats[:, 2 * (b % 2) + i, :], hh))
                v.bn_aggr(mv[:, b, :], stats[:, 2 * (b % 2):2 * (b % 2) + 2, :]).then_inc(var2_ready, 1)

            residual(0)
            for b in range(NB):
                dve.wait_ge(sd2_ready, b + 1)
                dep(v.reciprocal(rstd[:, b:b + 1], sd[:, b:b + 1]))
                v.tensor_scalar(shift[:, b:b + 1], mv[:, b, 0:1], rstd[:, b:b + 1], -1.0,
                                ALU.mult, ALU.mult).then_inc(rstd2_ready, 1)
                if b + 1 < NB:
                    residual(b + 1)
                dve.wait_ge(norm_ready, b + 1)
                v.tensor_tensor(h1[:, b, :], h1[:, b, :], ln2_sb[:, 0, :], ALU.mult).then_inc(scaled_ready, 1)

        @block.gpsimd
        def _(pool):
            nc.gpsimd.memset(xm[:, :, 0:TAPS - 1], 0.0).then_inc(pads_zero, 1)

            def low_part(n, j):
                pool.wait_ge(wd_hi_ready, n + 1)
                nc.gpsimd.tensor_tensor(wd_lo[j][:], wd[j][:], wd_hi[j][:].bitcast(F32),
                                        ALU.subtract).then_inc(wd_lo_ready, 1)

            with pool.Fori(0, TILES // TPS, 1) as s:
                for j in range(TPS):
                    low_part(s * TPS + j, j)
            for j in range(REST):
                low_part(TILES - REST + j, j)
            for b in range(NB):
                pool.wait_ge(scaled_ready, b + 1)
                nc.gpsimd.tensor_tensor(h1[:, b, :], h1[:, b, :], ln2_sb[:, 1, :], ALU.add).then_inc(out_ready, 1)


def shape_constants():
    import numpy as np
    t, s = np.arange(P)[:, None], np.arange(P)[None, :]
    dist = t - (np.arange(S)[None, :] - (S - P))
    count = (((dist >= 0) & (dist <= 128)).astype(np.float32)
             + ((dist >= 0) & (dist % 4 == 0) & (dist <= 512)) + ((dist >= 0) & (dist % 16 == 0)))
    tail = np.zeros((P, 32), np.float32)
    tail[:, 0:16] = np.arange(16)
    tail[:, 16] = EPS
    return np.concatenate([np.eye(P), (t <= s), np.ones((P, P)), np.where(s <= t, 0.0, NEG),
                           np.where(count > 0, 0.0, NEG), count, tail,
                           np.broadcast_to(np.arange(P), (P, P))], axis=1).astype(np.float32)


def kernel(**inputs):
    import numpy as _np
    import concourse.bacc as _bacc
    from concourse import mybir as _mybir
    from concourse.bass_utils import run_bass_kernel_spmd as _run

    a = {k: _np.asarray(v) for k, v in inputs.items()}
    x = a["x"][0]
    w_in = a["w_in"][0]
    conv = _np.concatenate([a["conv_w"][0], a["conv_b"]], axis=0)
    laid = {
        "xT": x.T,
        "x": x,
        "w_in": w_in[:, :6 * W],
        "w_gate": w_in[:, 6 * W:].reshape(KD, P, 2 * MH).transpose(1, 0, 2),
        "conv": conv.reshape(TAPS + 1, MH, ME).transpose(2, 1, 0),
        "gate_bias": _np.concatenate([a["b_igate"], a["b_fgate"]], axis=1),
        "w_mq": a["w_mq"][0],
        "w_mk": a["w_mk"][0],
        "mh_g": a["mh_norm_g"],
        "w_out": a["w_out"][0],
        "ln1": _np.concatenate([a["ln1_g"], a["ln1_b"]], axis=0),
        "w_query": a["peer_w_query"][0],
        "sub_keys": a["peer_sub_keys"][0].transpose(3, 0, 1, 2),
        "w_downT": a["peer_w_down"][0].reshape(NK, NK, KD, P).transpose(0, 3, 2, 1).reshape(NK * P, KD * NK),
        "w_up": a["peer_w_up"][0],
        "ln2": _np.concatenate([a["ln2_g"], a["ln2_b"]], axis=0),
        "consts": shape_constants(),
    }
    nc = _bacc.Bacc("TRN2", target_bir_lowering=False, num_devices=1)
    arrays, args = {}, []
    for name, v in laid.items():
        arrays[f"in_{name}"] = _np.ascontiguousarray(v)
        args.append(nc.dram_tensor(f"in_{name}", v.shape, _mybir.dt.from_np(v.dtype), kind="ExternalInput").ap())
    args.append(nc.dram_tensor("gates_dram", (P, 2 * NB, NK * HALF), F32).ap())
    args.append(nc.dram_tensor("act_dram", (P, TILES, S), F32).ap())
    args.append(nc.dram_tensor("out_0", (S, D), F32, kind="ExternalOutput").ap())
    build(nc, *args)
    r = _run(nc, [arrays], core_ids=[0])
    return _np.asarray(r.results[0]["out_0"]).reshape(1, S, D)
```

```python
from contextlib import ExitStack

import concourse.bass as bass
from concourse import mybir

F32 = mybir.dt.float32
F32R = mybir.dt.float32r
U32 = mybir.dt.uint32
ALU = mybir.AluOpType
ACT = mybir.ActivationFunctionType
X = mybir.AxisListType.X

P = 128
S = 512
D = 1024
NB = S // P
KD = D // P
W = 512
HW = 256
PIECES = 12
AH, AE = 8, 64
MH, ME = 4, 128
TAPS = 4
PH, NK, TOPK = 8, 128, 16
ALPHA = 2.0 ** 0.25
EPS = 1e-5
NEG = -1e30
LOWEST = -3e38
STEPS = NB * PH
TILES = NK
TPS = 3
GATE_STEPS = STEPS + PH
LONE_STEPS = TILES // TPS - GATE_STEPS
REST = TILES % TPS
PIECE = NK // 4
TOK = 4
GPS = 4
GROUPS = STEPS * GPS
UTS = 4
HALF = P // 2

XM, GATES, VM, GATES_TURNED, QA = 0, 4, 5, 13, 14
MQ, MK, KM = 18, 22, 26
KA, VA = 30, 34
PROJ_ITEMS = 42


def mixing_order():
    order = [("ml", 0, 0)]
    for c in range(NB):
        if c == 0:
            between = [[], [("om", 0, 0)], [("ml", 0, 1)], [("om", 1, 0), ("om", 0, 1), ("ml", 0, 2)], [("om", 0, 2)],
                       [("om", 2, 0), ("om", 0, 3), ("ml", 0, 3)], [("om", 0, 4), ("ml", 1, 0)],
                       [("ml", 0, 4), ("om", 3, 0), ("om", 1, 1)], [("ml", 1, 1), ("om", 1, 2)],
                       [("ml", 1, 2), ("om", 1, 3)], [("om", 1, 4), ("ml", 1, 3)]]
        else:
            p, n = c - 1, c + 1
            between = [[("cat", p, 0)], [("cat", p, 1)], [("out", p, 0)], [("ml", n, 0)], [("out", p, 1)],
                       [("ml", n, 1)], [("ml", n, 2)], [("ml", n, 3), ("ln", p, 0)], [("ln", p, 1), ("ml", n, 4)],
                       [("ln", p, 2)], [("h1T", p, 0), ("h1T", p, 1)]]
            if c == 1:
                between[0].append(("ml", 1, 4))
            if n < NB:
                for i in range(4):
                    between[i].append(("om", n, i + 1))
        for i in range(AH + 3):
            order.append(("head", c, i))
            order += [stage for stage in between[i] if stage[:2] != ("ml", NB)]
    last = NB - 1
    order += [("cat", last, 0), ("cat", last, 1), ("wq", last, 0), ("out", last, 0), ("wq", last, 1),
              ("out", last, 1), ("ln", last, 0), ("ln", last, 1), ("ln", last, 2), ("h1T", last, 0), ("h1T", last, 1)]
    return order


def bank_items(order):
    score, turn = {}, {}
    for kind, c, i in order:
        if (kind, i) in (("ml", 0), ("om", 0)) or kind == "out" or (kind == "head" and i < AH):
            score[kind, c, i] = NB + len(score)
        if (kind, i) == ("ml", 1) or kind in ("cat", "h1T"):
            turn[kind, c, i] = len(turn)
        if kind == "head" and 2 <= i <= AH + 1:
            turn[kind, c, i - 2] = len(turn)
    return score, turn


def build(nc, xT, x, w_in, w_gate, conv, gate_bias, w_mq, w_mk, mh_g, w_out, ln1, w_query, sub_keys,
          w_downT, w_up, ln2, consts, gates_dram, act_dram, out):
    order = mixing_order()
    score_item, turn_item = bank_items(order)
    h1T_items = {turn_item["h1T", c, i]: 2 * c + i for c in range(NB) for i in range(2)}
    score_items, turn_items = NB + len(score_item), len(turn_item)

    with ExitStack() as ctx:
        def sem(name):
            return ctx.enter_context(nc.semaphore(name))

        def sb(stack, name, shape, dt=F32):
            return stack.enter_context(nc.sbuf_tensor(name, shape, dt))

        pj = [ctx.enter_context(nc.psum_tensor(f"proj{i}", [P, 512], F32)) for i in range(2)]
        ps = [ctx.enter_context(nc.psum_tensor(f"score{i}", [P, 512], F32)) for i in range(2)]
        pt = [ctx.enter_context(nc.psum_tensor(f"turn{i}", [P, 512], F32)) for i in range(2)]
        py = ctx.enter_context(nc.psum_tensor("py", [P, 2, 512], F32))
        po, pi = py[:, 0, :], py[:, 1, :]

        cst = sb(ctx, "cst", [P, 5 * P + 2 * S + 32])
        ident, triu, ones = cst[:, 0:P], cst[:, P:2 * P], cst[:, 2 * P:3 * P]
        tril_bias = cst[:, 3 * P:4 * P]
        attn_bias = cst[:, 4 * P:4 * P + S]
        attn_count = cst[:, 4 * P + S:4 * P + 2 * S]
        iota16 = cst[:, 4 * P + 2 * S:4 * P + 2 * S + 16]
        eps = cst[:, 4 * P + 2 * S + 16:4 * P + 2 * S + 17]
        iota128 = cst[:, 4 * P + 2 * S + 32:5 * P + 2 * S + 32]
        before_x = ExitStack()
        wp_hi = [sb(before_x, f"wp_hi{i}", [P, KD, HW], F32R) for i in range(2)]
        before_x.close()
        h1 = sb(ctx, "h1", [P, NB, D])
        stats = sb(ctx, "stats", [P, 4, 6])
        mv = sb(ctx, "mv", [P, 4, 2])
        sd = sb(ctx, "sd", [P, 4])
        rstd = sb(ctx, "rstd", [P, 4])
        ln_stats = sb(ctx, "ln_stats", [P, 2, 6])
        ln_mv = sb(ctx, "ln_mv", [P, 2])
        ln_sd = sb(ctx, "ln_sd", [P, 3])
        shift = sb(ctx, "shift", [P, 4])

        h1T_hi = sb(ctx, "h1T_hi", [P, KD, S], F32R)

        xT_scope = ExitStack()
        xT_sb = sb(xT_scope, "xT_sb", [P, KD, S])
        xT_scope.close()
        h1T_lo = sb(ctx, "h1T_lo", [P, KD, S], F32R)
        x_hi, x_lo = h1T_hi, h1T_lo
        mixing = ExitStack()
        pieces = ExitStack()
        wp = [sb(pieces, f"wpiece{i}", [P, KD, HW]) for i in range(4)]
        pieces.close()
        low = ExitStack()
        wp_lo = [sb(low, f"wpiece_lo{i}", [P, KD, HW], F32R) for i in range(4)]
        low.close()
        wo = [sb(mixing, f"w_out{i}", [P, KD, W]) for i in range(2)]
        rm = sb(mixing, "rm", [P, NB, MH, P])
        km = sb(mixing, "km", [P, NB, MH, ME])
        qm = sb(mixing, "qm", [P, MH, S])
        kmT = sb(mixing, "kmT", [P, MH, S])
        vm = sb(mixing, "vm", [P, NB, W])
        qa = sb(mixing, "qa", [P, 4, S])
        ka = sb(mixing, "ka", [P, 4, S])
        va = sb(mixing, "va", [P, NB, W])
        ln1_sb = sb(mixing, "ln1_sb", [P, 2, D])
        mhg = sb(mixing, "mhg", [P, W])
        wg_sb = sb(mixing, "wg_sb", [P, KD, 2 * MH])
        wg_hi = sb(mixing, "wg_hi", [P, KD, 2 * MH], F32R)
        wg_lo = sb(mixing, "wg_lo", [P, KD, 2 * MH], F32R)
        conv_sb = sb(mixing, "conv_sb", [P, MH, TAPS + 1])
        gbias = sb(mixing, "gbias", [P, 2 * MH])
        xm = sb(mixing, "xm", [P, MH, S + TAPS])
        om = sb(mixing, "om", [P, NB, W])
        xc = sb(mixing, "xc", [P, MH, S])
        wmq, wmk = rm[:, 0], rm[:, 1]
        diag_r = xm[:, :, 0:S].rearrange("p c (h s) -> p c h s", h=MH)
        cat = sb(mixing, "cat", [P, W])
        gT = cat
        catT = sb(mixing, "catT", [P, KD, P])
        ct = sb(mixing, "ct", [P, MH, ME])
        nst = sb(mixing, "nst", [P, MH])
        sw = [sb(mixing, f"sw{i}", [P, S]) for i in range(2)] + [xm[:, 0, 0:S]]
        pT = [sb(mixing, f"pT{i}", [P, S]) for i in range(2)]
        gt = sb(mixing, "gt", [P, NB, 2 * MH])
        sv = sb(mixing, "sv", [P, 20, 16])
        ew = sb(mixing, "ew", [P, 4, 16])
        hv = sb(mixing, "hv", [P, 8, AH])
        ip, ff, nf, lg, logf, bc, bl, rr, rmax, mmax, mxl, mx, nmx, lexp, mn = (
            sv[:, i, :] for i in range(15))
        mprev = sv[:, 15:17, :].rearrange("p a b -> p (a b)")
        w_inter, e_mt, a_dec, w_k = (ew[:, i, :] for i in range(4))
        kw, inter, swm, pTm = (xc[:, :, i * P:(i + 1) * P] for i in range(4))
        mixing.close()

        scores_scope = ExitStack()
        scores = sb(scores_scope, "scores", [P, STEPS, 2 * NK])
        query = ExitStack()
        wq = [sb(query, f"wq{i}", [P, KD, 2 * NK]) for i in range(2)]
        wq_hi = [sb(query, f"wq_hi{i}", [P, KD, 2 * NK], F32R) for i in range(2)]
        wq_lo = [sb(query, f"wq_lo{i}", [P, KD, 2 * NK], F32R) for i in range(2)]
        sk = sb(query, "sk", [P, PH * 2, NK])
        qry = [sb(query, f"qry{i}", [P, 2, S]) for i in range(2)]
        query.close()

        down = ExitStack()
        stage = [sb(down, f"stage{i}", [P, NK, HALF]) for i in range(2)]
        raw = ExitStack()
        wd = [sb(raw, f"wd{i}", [P, KD, P]) for i in range(TPS)]
        raw.close()
        wd_lo = [sb(down, f"wd_lo{i}", [P, KD, P], F32R) for i in range(TPS)]
        wd_hi = [sb(down, f"wd_hi{i}", [P, KD, P], F32R) for i in range(TPS)]
        gel = [sb(down, f"gel{i}", [P, S]) for i in range(TPS)]
        hot2 = sb(down, "hot2", [P, 2, TOK, P])
        hot1 = sb(down, "hot1", [P, 2, TOK, P])
        picks = sb(down, "picks", [P, 3, PH * TOPK])
        picksT = sb(down, "picksT", [P, 3, P])
        cols = sb(down, "cols", [P, 3, 4 * TOK])
        sc = sb(down, "sc", [P, 2, NK])
        sc2 = sb(down, "sc2", [P, 2, NK])
        top = sb(down, "top", [P, 2, TOPK])
        topi = sb(down, "topi", [P, 2, TOPK], U32)
        cand = sb(down, "cand", [P, TOPK * TOPK])
        cand2 = sb(down, "cand2", [P, TOPK * TOPK])
        best = sb(down, "best", [P, TOPK])
        pos = sb(down, "pos", [P, TOPK], U32)
        hl = sb(down, "hl", [P, 2, TOPK], U32)
        eq = sb(down, "eq", [P, 2, TOPK, TOPK])
        e12g = sb(down, "e12g", [P, 3, TOPK])
        shifted = sb(down, "shifted", [P, TOPK])
        gate_exp = sb(down, "gate_exp", [P, TOPK])
        gate_sum = sb(down, "gate_sum", [P, 1])
        gate_rs = sb(down, "gate_rs", [P, 1])
        down.close()
        scores_scope.close()

        wu = [sb(ctx, f"wu{i}", [P, D]) for i in range(2)]
        wu_hi = [sb(ctx, f"wu_hi{i}", [P, D], F32R) for i in range(2)]
        wu_lo = [sb(ctx, f"wu_lo{i}", [P, D], F32R) for i in range(2)]
        gts = [sb(ctx, f"gates{i}", [P, 2 * NB, UTS, HALF]) for i in range(2)]
        acts = [sb(ctx, f"acts{i}", [P, UTS, S]) for i in range(2)]
        ga = [sb(ctx, f"ga{i}", [P, S]) for i in range(2)]
        ga_hi = [sb(ctx, f"ga_hi{i}", [P, S], F32R) for i in range(2)]
        ga_lo = [sb(ctx, f"ga_lo{i}", [P, S], F32R) for i in range(2)]
        ln2_sb = sb(ctx, "ln2_sb", [P, 2, D])

        const_in, x_in, small_in, ln2_in = (sem(n) for n in ("const_in", "x_in", "small_in", "ln2_in"))
        xT_in = [sem(f"xT_in{i}") for i in range(4)]
        x_hi_ready, x_lo_ready, wp_hi_ready, wp_lo_ready, wg_split = (sem(n) for n in (
            "x_hi_ready", "x_lo_ready", "wp_hi_ready", "wp_lo_ready", "wg_split"))
        wg_hi_ready = sem("wg_hi_ready")
        first_in, first_hi_ready, first_lo_ready = (sem(n) for n in ("first_in", "first_hi_ready", "first_lo_ready"))
        wo_in = [sem(f"wo_in{i}") for i in range(2)]
        wp_in = [sem(f"wp_in{i}") for i in range(4)]
        wq_in = [sem(f"wq_in{i}") for i in range(2)]
        proj_done, proj_copied = sem("proj_done"), sem("proj_copied")
        pads_zero = sem("pads_zero")
        conv_done, conv_exp, xc_ready = sem("conv_done"), sem("conv_exp"), sem("xc_ready")
        gate_pre, gate_ln, logf_ready, gate_sums = (sem(n) for n in (
            "gate_pre", "gate_ln", "logf_ready", "gate_sums"))
        r_ready, diag_ready, args_ready, weights_ready = (sem(n) for n in (
            "r_ready", "diag_ready", "args_ready", "weights_ready"))
        ps_done, ps_read = sem("ps_done"), sem("ps_read")
        pt_done, pt_copied = sem("pt_done"), sem("pt_copied")
        mexp_done, mp_ready, kw_ready = sem("mexp_done"), sem("mp_ready"), sem("kw_ready")
        inter_scaled, num_done, mpv_done = sem("inter_scaled"), sem("num_done"), sem("mpv_done")
        ogate_ready, sigmoid_ready = sem("ogate_ready"), sem("sigmoid_ready")
        ln_rstd_ready, ln_norm_ready, ln_scaled = (sem(n) for n in (
            "ln_rstd_ready", "ln_norm_ready", "ln_scaled"))
        ml_ready, ln_var_ready, ln_sd_ready, wg_in = (sem(n) for n in (
            "ml_ready", "ln_var_ready", "ln_sd_ready", "wg_in"))
        upd_done, state_ready = sem("upd_done"), sem("state_ready")
        var_ready, sd_ready, ogate_exp = sem("var_ready"), sem("sd_ready"), sem("ogate_exp")
        aexp_done, ap_ready, pv_done = (sem(n) for n in ("aexp_done", "ap_ready", "pv_done"))
        cat_ready, h1_ready = sem("cat_ready"), sem("h1_ready")
        dve_step, act_step = sem("dve_step"), sem("act_step")
        sk_in = sem("sk_in")
        qry_done, qry_copied, sc_done, sc_copied = (sem(n) for n in (
            "qry_done", "qry_copied", "sc_done", "sc_copied"))
        h1T_split, wq_hi_ready, wq_lo_ready = sem("h1T_split"), sem("wq_hi_ready"), sem("wq_lo_ready")
        wd_in = [sem(f"wd_in{i}") for i in range(TPS)]
        wd_hi_ready, wd_lo_ready, down_done, gelu_done = (sem(n) for n in (
            "wd_hi_ready", "wd_lo_ready", "down_done", "gelu_done"))
        act_out = [sem(f"act_out{i}") for i in range(TPS)]
        stage_out = [sem(f"stage_out{i}") for i in range(2)]
        shifted_ready, gates_ready, picks_ready, turned_ready, picksT_ready = (sem(n) for n in (
            "shifted_ready", "gates_ready", "picks_ready", "turned_ready", "picksT_ready"))
        hot_ready, gmat_done, gmat_staged = sem("hot_ready"), sem("gmat_done"), sem("gmat_staged")
        loop_step, dve_alone = sem("loop_step"), sem("dve_alone")
        wu_in = [sem(f"wu_in{i}") for i in range(2)]
        ga_in = [sem(f"ga_in{i}") for i in range(2)]
        wu_hi_ready, wu_lo_ready, ga_ready, ga_hi_ready, ga_lo_ready, up_done = (sem(n) for n in (
            "wu_hi_ready", "wu_lo_ready", "ga_ready", "ga_hi_ready", "ga_lo_ready", "up_done"))
        rstd2_ready, norm_ready, scaled_ready, out_ready, out_sent = (sem(n) for n in (
            "rstd2_ready", "norm_ready", "scaled_ready", "out_ready", "out_sent"))
        block_done = sem("block_done")
        var2_ready, sd2_ready = sem("var2_ready"), sem("sd2_ready")

        block = ctx.enter_context(nc.Block())
        down_banks = [pj[0][:], pj[1][:], po]

        piece_used = [XM + 2, GATES, VM + 4, GATES_TURNED, QA + 2, MQ, KA + 2, VA, VA + 4, PROJ_ITEMS]

        @block.sync
        def _(sp):
            def load_piece(n):
                col = (3, 4, 0, 1, 2, 5)[n // 2] * W + n % 2 * HW
                sp.dma_start(wp[n % 4][:], w_in[:, col:col + HW].rearrange("(k p) n -> p k n", p=P)).then_inc(
                    wp_in[n % 4], 16)

            def load_first(i):
                sp.dma_start(wp[0][:, :, i * P:(i + 1) * P], w_in[:, 3 * W + i * P:3 * W + (i + 1) * P].rearrange(
                    "(k p) n -> p k n", p=P)).then_inc(wp_in[0] if i else first_in, 16)

            for i in range(4):
                sp.dma_start(xT_sb[:, 2 * i:2 * i + 2, :],
                             xT[2 * i * P:(2 * i + 2) * P, :].rearrange("(k p) t -> p k t", p=P)).then_inc(xT_in[i], 16)
                if i == 0:
                    load_first(0)
            load_first(1)
            load_piece(1)
            sp.dma_start(wg_sb[:], w_gate).then_inc(wg_in, 16)
            sp.dma_start(conv_sb[:], conv).then_inc(small_in, 16)
            sp.dma_start(gbias[:], gate_bias.to_broadcast([P, 2 * MH])).then_inc(small_in, 16)
            load_piece(2)
            load_piece(3)
            sp.dma_start(cst[:], consts).then_inc(const_in, 16)
            sp.dma_start(wmq, w_mq.rearrange("h e f -> e h f")).then_inc(small_in, 16)
            sp.dma_start(wmk, w_mk.rearrange("h e f -> e h f")).then_inc(small_in, 16)
            sp.dma_start(mhg[:], mh_g.to_broadcast([P, W])).then_inc(small_in, 16)
            for i in range(2):
                sp.dma_start(ln1_sb[:, i, :], ln1[i:i + 1, :].to_broadcast([P, D])).then_inc(small_in, 16)
            for n in range(4, PIECES):
                sp.wait_ge(proj_done, piece_used[n - 4])
                load_piece(n)
            for i in range(2):
                if i == 0:
                    sp.wait_ge(proj_done, PROJ_ITEMS)
                else:
                    sp.wait_ge(ps_done, score_item["om", NB - 1, 0] + 1)
                sp.dma_start(wo[i][:], w_out[:, i * W:(i + 1) * W].rearrange("(k p) n -> p k n", p=P)).then_inc(
                    wo_in[i], 16)
            for c in range(NB):
                sp.dma_start(h1[:, c, :], x[c * P:(c + 1) * P, :]).then_inc(x_in, 16)
            sp.wait_ge(mexp_done, NB)
            for h in range(PH):
                if h >= 2:
                    sp.wait_ge(wq_lo_ready, h - 1)
                sp.dma_start(wq[h % 2][:], w_query[:, h * 2 * NK:(h + 1) * 2 * NK].rearrange(
                    "(k p) n -> p k n", p=P)).then_inc(wq_in[h % 2], 16)
                if h == 1:
                    sp.wait_ge(ps_done, score_item["head", NB - 1, AH - 1] + 1)
                    sp.dma_start(sk[:], sub_keys).then_inc(sk_in, 16)
            def load_down(n, j):
                sp.wait_ge(down_done, n + 1)
                sp.dma_start(wd[j][:].rearrange("p k e -> p (k e)"),
                             w_downT[bass.ds(n * P, P), :]).then_inc(wd_in[j], 16)

            with sp.Fori(0, TILES // TPS, 1) as s:
                for j in range(TPS):
                    load_down(s * TPS + j, j)
            for j in range(REST):
                load_down(TILES - REST + j, j)
            sp.wait_ge(picks_ready, STEPS)
            for q in range(2):
                sp.wait_ge(stage_out[q], 16 * (4 * NB + 1))
            for part in range(2):
                for j in range(TPS):
                    tiles = (part + 1) * TILES // 2
                    sp.wait_ge(act_out[j], 16 * ((tiles - j + TPS - 1) // TPS + 1))
                with sp.Fori(part * (TILES // UTS // 4), (part + 1) * (TILES // UTS // 4), 1) as pair:
                    for q in range(2):
                        for j in range(UTS):
                            n = pair * (2 * UTS) + (q * UTS + j)
                            if j == 0:
                                sp.wait_ge(ga_ready, n + UTS)
                                sp.dma_start(gts[q][:].rearrange("p n i t -> p n (i t)"),
                                             gates_dram[:, :, bass.ds(n * HALF, UTS * HALF)]).then_inc(ga_in[q], 16)
                                sp.dma_start(acts[q][:], act_dram[:, bass.ds(n, UTS), :]).then_inc(ga_in[q], 16)
                            sp.wait_ge(wu_lo_ready, n + 1)
                            sp.dma_start(wu[j % 2][:], w_up[bass.ds(n * P, P), :]).then_inc(wu_in[j % 2], 16)
                if part == 0:
                    for i in range(2):
                        sp.dma_start(ln2_sb[:, i, :], ln2[i:i + 1, :].to_broadcast([P, D])).then_inc(ln2_in, 16)
            for n in range(2 * NB):
                sp.wait_ge(out_ready, n + 1)
                cs = slice(n % 2 * 512, (n % 2 + 1) * 512)
                sp.dma_start(out[n // 2 * P:(n // 2 + 1) * P, cs], h1[:, n // 2, cs]).then_inc(out_sent, 16)
            sp.wait_ge(out_sent, 32 * NB)

        def down_steps(eng, body, after_group=None):
            body(0, first=True, gates=False)
            with eng.Fori(1, PH, 1) as h:
                body(h, gates=False)
            if after_group:
                after_group(0)

            def half_block(block, half, select=True, store=True):
                with eng.Fori(0, PH // 2, 1) as quarter:
                    body(quarter + (block * PH + half * (PH // 2)), select=select, store=store,
                         half=half, quarter=quarter, block=block)

            half_block(1, 0, store=False)
            with eng.Fori(1, NB - 1, 1) as g:
                half_block(g, 1)
                if after_group:
                    after_group(g)
                half_block(g + 1, 0)
            half_block(NB - 1, 1)
            if after_group:
                after_group(NB - 1)
            half_block(NB, 0, select=False)
            half_block(NB, 1, select=False)
            with eng.Fori(0, LONE_STEPS, 1) as lone:
                body(lone + GATE_STEPS, select=False, gates=False, lone=lone)
            body(GATE_STEPS + LONE_STEPS, select=False, gates=False, tiles=REST)

        @block.tensor
        def _(pe):
            mm = nc.tensor.matmul

            def open_proj(n):
                if n >= 2:
                    pe.wait_ge(proj_copied, n - 1)
                return pj[n % 2]

            def three(o, w_parts, x_parts, turned, k, last_k=KD - 1):
                for wi, xi in ((0, 0), (0, 1), (1, 0)):
                    w, x_part = w_parts[wi], x_parts[xi]
                    ins = mm(o, *((x_part, w) if turned else (w, x_part)), start=k == 0 and wi == xi,
                             stop=k == last_k and wi == 1)
                return ins

            def wide(n0, piece):
                for i in range(2):
                    if n0 + i == XM:
                        pe.wait_ge(first_lo_ready, 1)
                    else:
                        pe.wait_ge(wp_lo_ready, piece + 1)
                    o = open_proj(n0 + i)
                    for k in range(KD):
                        cs = slice(i * P, (i + 1) * P)
                        if n0 + i == XM:
                            pe.wait_ge(x_lo_ready, k // 2 + 1)
                        last = three(o[:], (wp_hi[piece % 2][:, k, cs], wp_lo[piece % 4][:, k, cs]),
                                     (x_hi[:, k, :], x_lo[:, k, :]), False, k)
                    last.then_inc(proj_done, 1)

            def tall_item(o, c, piece):
                for k in range(KD):
                    t = slice(c * P, (c + 1) * P)
                    last = three(o, (wp_hi[piece % 2][:, k, :], wp_lo[piece % 4][:, k, :]),
                                 (x_hi[:, k, t], x_lo[:, k, t]), True, k)
                return last

            def tall(n0, piece):
                pe.wait_ge(wp_lo_ready, piece + 1)
                for c in range(NB):
                    tall_item(open_proj(n0 + c)[:, 0:HW], c, piece).then_inc(proj_done, 1)

            wide(XM, 0)
            wide(XM + 2, 1)
            o = open_proj(GATES)
            pe.wait_ge(wg_split, 1)
            for k in range(KD):
                last = three(o[0:2 * MH, :], (wg_hi[:, k, :], wg_lo[:, k, :]), (x_hi[:, k, :], x_lo[:, k, :]), False, k)
            last.then_inc(proj_done, 1)
            tall(VM, 2)
            tall(VM + 4, 3)
            o = open_proj(GATES_TURNED)
            pe.wait_ge(const_in, 16)
            pe.wait_ge(proj_copied, GATES + 1)
            for c in range(NB):
                last = nc.tensor.transpose(o[:, c * 8:c * 8 + 8], gT[0:2 * MH, c * P:(c + 1) * P],
                                           ident[0:2 * MH, 0:2 * MH])
            last.then_inc(proj_done, 1)
            wide(QA, 4)
            wide(QA + 2, 5)
            for n0, w in ((MQ, wmq), (MK, wmk)):
                for h in range(MH):
                    o = open_proj(n0 + h)
                    pe.wait_ge(xc_ready, h + 1)
                    mm(o[:], w[:, h, :], xc[:, h, :], start=True, stop=True).then_inc(proj_done, 1)
            for h in range(MH):
                o = open_proj(KM + h)
                for c in range(NB):
                    last = mm(o[:, c * P:(c + 1) * P], xc[:, h, c * P:(c + 1) * P], wmk[:, h, :],
                              start=True, stop=True)
                last.then_inc(proj_done, 1)
            pe.wait_ge(const_in, 16)
            pe.wait_ge(logf_ready, 1)
            mm(pi[:, 0:16], triu, logf, start=True, stop=True)
            mm(pi[:, 16:32], ones, logf, start=True, stop=True).then_inc(gate_sums, 1)
            wide(KA, 6)
            wide(KA + 2, 7)
            for c in range(NB):
                pe.wait_ge(diag_ready, (c + 1) * MH)
                if c >= 2:
                    pe.wait_ge(ps_read, c - 1)
                mm(ps[c % 2][:], ones, xm[:, c, 0:S], start=True, stop=True).then_inc(ps_done, 1)
                if c == 1:
                    tall(VA, 8)
            tall(VA + 4, 9)

            def open_score(n):
                pe.wait_ge(ps_read, n - 1)
                return ps[n % 2]

            def open_turn(n):
                if n - 2 in h1T_items:
                    pe.wait_ge(h1T_split, h1T_items[n - 2] + 1)
                if n >= 2:
                    pe.wait_ge(pt_copied, n - 1)
                return pt[n % 2]

            def project_gate(c):
                o = open_score(score_item["om", c, 0])
                for half in range(2):
                    pe.wait_ge(wp_lo_ready, PIECES - 1 + half)
                    last = tall_item(o[:, half * HW:(half + 1) * HW], c, PIECES - 2 + half)
                last.then_inc(ps_done, 1)

            def mlstm(c, part):
                t = slice(c * P, (c + 1) * P)
                if part == 0:
                    if c == 0:
                        pe.wait_ge(proj_copied, PROJ_ITEMS)
                    o = open_score(score_item["ml", c, 0])
                    for h in range(MH):
                        last = mm(o[:, h * P:(h + 1) * P], qm[:, h, t], kmT[:, h, t], start=True, stop=True)
                    last.then_inc(ps_done, 1)
                    pe.wait_ge(state_ready, c + 1)
                    if c >= 1:
                        pe.wait_ge(num_done, c)
                    for h in range(MH):
                        mm(pi[:, h * P:(h + 1) * P], qm[:, h, t], ct[:, h, :], start=True, stop=True)
                    for h in range(MH):
                        last = mm(pj[1][:, h:h + 1], qm[:, h, t], nst[:, h:h + 1], start=True, stop=True)
                    if c < NB - 1:
                        pe.wait_ge(kw_ready, c + 1)
                        for h in range(MH):
                            mm(pj[0][:, h * P:(h + 1) * P], kw[:, h, :], vm[:, c, h * ME:(h + 1) * ME],
                               start=True, stop=True)
                        for h in range(MH):
                            last = mm(pj[1][:, 4 + h:5 + h], kw[:, h, :], ones[:, 0:1], start=True, stop=True)
                    last.then_inc(upd_done, 1)
                elif part == 1:
                    pe.wait_ge(mp_ready, c + 1)
                    o = open_turn(turn_item["ml", c, 1])
                    for h in range(MH):
                        last = nc.tensor.transpose(o[:, h * P:(h + 1) * P], swm[:, h, :], ident)
                    last.then_inc(pt_done, 1)
                elif part == 2:
                    pe.wait_ge(pt_copied, turn_item["ml", c, 1] + 1)
                    pe.wait_ge(inter_scaled, c + 1)
                    for h in range(MH):
                        last = mm(pi[:, h * P:(h + 1) * P], pTm[:, h, :], vm[:, c, h * ME:(h + 1) * ME],
                                  start=True, stop=True)
                    last.then_inc(mpv_done, 1)

            def head(c, i):
                if i < AH:
                    o = open_score(score_item["head", c, i])
                    r = slice((i % 2) * AE, (i % 2 + 1) * AE)
                    mm(o[:, 0:(c + 1) * P], qa[r, i // 2, c * P:(c + 1) * P], ka[r, i // 2, 0:(c + 1) * P],
                       start=True, stop=True).then_inc(ps_done, 1)
                if 2 <= i <= AH + 1:
                    g = AH * c + i - 2
                    pe.wait_ge(ap_ready, g + 1)
                    o = open_turn(turn_item["head", c, i - 2])
                    for j in range(c + 1):
                        last = nc.tensor.transpose(o[:, j * P:(j + 1) * P], sw[g % 3][:, j * P:(j + 1) * P], ident)
                    last.then_inc(pt_done, 1)
                if i >= 3:
                    h, g = i - 3, AH * c + i - 3
                    pe.wait_ge(pt_copied, turn_item["head", c, h] + 1)
                    if h == 0 and c >= 1:
                        pe.wait_ge(cat_ready, c)
                    for j in range(c + 1):
                        last = mm(po[:, h * AE:(h + 1) * AE], pT[g % 2][:, j * P:(j + 1) * P],
                                  va[:, j, h * AE:(h + 1) * AE], start=j == 0, stop=j == c)
                    last.then_inc(pv_done, 1)

            def turn_cat(c, i):
                pe.wait_ge(ml_ready if i else cat_ready, c + 1)
                o = open_turn(turn_item["cat", c, i])
                for j in range(4):
                    src = om[:, c, :] if i else cat[:]
                    last = nc.tensor.transpose(o[:, j * P:(j + 1) * P], src[:, j * P:(j + 1) * P], ident)
                last.then_inc(pt_done, 1)

            def project_out(c, i):
                pe.wait_ge(pt_copied, turn_item["cat", c, 1] + 1)
                if c == 0:
                    pe.wait_ge(wo_in[i], 16)
                o = open_score(score_item["out", c, i])
                for k in range(KD):
                    last = mm(o[:], catT[:, k, :], wo[i][:, k, :], start=k == 0, stop=k == KD - 1)
                last.then_inc(ps_done, 1)

            def turn_h1(c, i):
                pe.wait_ge(h1_ready, 2 * c + i + 1)
                o = open_turn(turn_item["h1T", c, i])
                for j in range(4):
                    k = 4 * i + j
                    last = nc.tensor.transpose(o[:, j * P:(j + 1) * P], h1[:, c, k * P:(k + 1) * P], ident)
                last.then_inc(pt_done, 1)

            for kind, c, i in order:
                if kind == "ml":
                    mlstm(c, i)
                elif kind == "om" and i == 0:
                    project_gate(c)
                elif kind == "head":
                    head(c, i)
                elif kind == "cat":
                    turn_cat(c, i)
                elif kind == "out":
                    project_out(c, i)
                elif kind == "h1T":
                    turn_h1(c, i)

            pe.wait_ge(pt_copied, turn_items)
            pe.wait_ge(h1T_split, 2 * NB)
            pe.wait_ge(ps_read, score_items)

            def query_head(h, q):
                pe.wait_ge(wq_lo_ready, h + 1)
                for side in range(2):
                    pe.wait_ge(qry_copied, h * 2 + (side + 1))
                    for k in range(KD):
                        cs = slice(side * P, (side + 1) * P)
                        mm(pj[side][:], wq_hi[q][:, k, cs], h1T_hi[:, k, :], start=k == 0, stop=False)
                        mm(pj[side][:], wq_hi[q][:, k, cs], h1T_lo[:, k, :], start=False, stop=False)
                        last = mm(pj[side][:], wq_lo[q][:, k, cs], h1T_hi[:, k, :],
                                  start=False, stop=k == KD - 1)
                    last.then_inc(qry_done, 1)

            def key_scores(h, q):
                pe.wait_ge(qry_copied, h * 2 + 4)
                for half in range(2):
                    pe.wait_ge(sc_copied, h * 2 + (half + 1))
                    for b in range(2):
                        for side in range(2):
                            blk = 2 * half + b
                            keys = (sk[:, h * 2 + side, :] if isinstance(h, int) else
                                    sk[:, bass.ds(h * 2 + side, 1), :].rearrange("p a n -> p (a n)"))
                            last = mm(ps[half][:, (2 * b + side) * P:(2 * b + side + 1) * P],
                                      qry[q][:, side, blk * P:(blk + 1) * P], keys, start=True, stop=True)
                    last.then_inc(sc_done, 1)

            query_head(0, 0)
            pe.wait_ge(sk_in, 16)
            with pe.Fori(0, PH // 2 - 1, 1) as pair:
                query_head(pair * 2 + 1, 1)
                key_scores(pair * 2, 0)
                query_head(pair * 2 + 2, 0)
                key_scores(pair * 2 + 1, 1)
            query_head(PH - 1, 1)
            key_scores(PH - 2, 0)
            key_scores(PH - 1, 1)

            pe.wait_ge(sc_copied, 2 + 2 * PH)

            def step(s, first=False, gates=True, select=True, tiles=TPS, half=0, quarter=0, block=0,
                     store=True, lone=None):
                for j in range(TPS):
                    if j < tiles:
                        pe.wait_ge(wd_lo_ready, s * TPS + (j + 1))
                        pe.wait_ge(gelu_done, s * TPS + (j + 1))
                        o = down_banks[j]
                        for k in range(KD):
                            mm(o, wd_hi[j][:, k, :], h1T_hi[:, k, :], start=k == 0, stop=False)
                            mm(o, wd_hi[j][:, k, :], h1T_lo[:, k, :], start=False, stop=False)
                            last = mm(o, wd_lo[j][:, k, :], h1T_hi[:, k, :], start=False, stop=k == KD - 1)
                        last.then_inc(down_done, 1)
                    for group in ((0,), (1,), (2, 3))[j] if gates else ():
                        m = (s - PH) * GPS + group
                        pe.wait_ge(hot_ready, m + 1)
                        pe.wait_ge(gmat_staged, m + 1)
                        for r in range(TOK):
                            last = mm(ps[group % 2][:, r * P:(r + 1) * P], hot2[:, group % 2, r, :],
                                      hot1[:, group % 2, r, :], start=True, stop=True)
                        last.then_inc(gmat_done, 1)

            def turn_picks(g):
                pe.wait_ge(picks_ready, (g + 1) * PH)
                for i in range(3):
                    last = nc.tensor.transpose(pt[0][:, i * P:(i + 1) * P], picks[:, i, :], ident)
                last.then_inc(turned_ready, 1)

            down_steps(pe, step, after_group=turn_picks)

            banks = [[pj[0], pj[1]], [ps[0], ps[1]], [pt[0], pt[1]], [py[:, 0, :], py[:, 1, :]]]
            pe.wait_ge(gmat_staged, 2 + GROUPS)
            pe.wait_ge(gelu_done, TPS + TILES)
            pe.wait_ge(picksT_ready, NB)

            def up_ready(n):
                pe.wait_ge(wu_lo_ready, n + 3)
                pe.wait_ge(ga_lo_ready, n + 1)

            def up_block(b, q, first=False):
                t = slice(b * P, (b + 1) * P)
                for ga_part, wu_part in ((ga_hi, wu_hi), (ga_hi, wu_lo), (ga_lo, wu_hi)):
                    for i in range(2):
                        last = mm(banks[b][i][:, 0:512], ga_part[q][:, t], wu_part[q][:, i * 512:(i + 1) * 512],
                                  start=first and (ga_part, wu_part) == (ga_hi, wu_hi), stop=False,
                                  skip_group_check=True)
                return last

            def up(n, q, first=False):
                up_ready(n)
                for b in range(NB):
                    last = up_block(b, q, first)
                last.then_inc(up_done, 1)

            for q in range(2):
                up(q, q, first=q == 0)
            with pe.Fori(1, TILES // 2 - 1, 1) as pair:
                for q in range(2):
                    up(pair * 2 + q, q)
            up_ready(TILES - 2)
            up_block(0, 0)
            up_block(1, 0)
            up_ready(TILES - 1)
            for b in range(NB):
                up_block(b, 1).then_inc(block_done, 1)
                if b + 2 < NB:
                    up_block(b + 2, 0)

        @block.scalar
        def _(act):
            run = nc.scalar.activation
            steps = [0]

            def dep(ins):
                steps[0] += 1
                ins.then_inc(act_step, 1)
                act.wait_ge(act_step, steps[0])

            def take(n, dst, scale=1.0):
                act.wait_ge(proj_done, n + 1)
                src = pj[n % 2][:, 0:dst.free_size()]
                if len(dst.shape) == 3:
                    src = src.rearrange("p (a b) -> p a b", a=dst.shape[1])
                run(dst, src, ACT.Copy, scale=scale).then_inc(proj_copied, 1)
                split_between(n)

            def split_piece(n, part):
                act.wait_ge(wp_in[n % 4], 16 * (n // 4 + 1))
                if n >= 2:
                    act.wait_ge(proj_done, piece_used[n - 2])
                k = slice(part * KD // 2, (part + 1) * KD // 2)
                ins = run(wp_hi[n % 2][:, k, :], wp[n % 4][:, k, :], ACT.Copy)
                if part == 1:
                    ins.then_inc(wp_hi_ready, 1)

            def split_between(item):
                for n, used in enumerate(piece_used):
                    if item == used - 1:
                        split_piece(n + 2, 0)
                    if item == used or used == PROJ_ITEMS == item + 1:
                        split_piece(n + 2, 1)

            for i in range(4):
                act.wait_ge(xT_in[i], 16)
                run(x_hi[:, 2 * i:2 * i + 2, :], xT_sb[:, 2 * i:2 * i + 2, :], ACT.Copy).then_inc(x_hi_ready, 1)
                if i == 0:
                    act.wait_ge(first_in, 16)
                    run(wp_hi[0][:, :, 0:P], wp[0][:, :, 0:P], ACT.Copy).then_inc(first_hi_ready, 1)
            act.wait_ge(wp_in[0], 16)
            run(wp_hi[0][:, :, P:HW], wp[0][:, :, P:HW], ACT.Copy).then_inc(wp_hi_ready, 1)
            split_piece(1, 0)
            split_piece(1, 1)
            act.wait_ge(wg_in, 16)
            run(wg_hi[:], wg_sb[:], ACT.Copy).then_inc(wg_hi_ready, 1)

            def silu_exp(h):
                act.wait_ge(conv_done, h + 1)
                run(xc[:, h, :], kmT[:, h, :], ACT.Exp, scale=-1.0).then_inc(conv_exp, 1)

            for h in range(MH):
                act.wait_ge(pads_zero, 1)
                take(XM + h, xm[:, h, TAPS - 1:TAPS - 1 + S])
            act.wait_ge(proj_done, GATES + 1)
            run(gT[0:2 * MH, :], pj[GATES % 2][0:2 * MH, :], ACT.Copy).then_inc(proj_copied, 1)
            split_between(GATES)
            for i in range(2):
                for c in range(NB):
                    take(VM + 4 * i + c, vm[:, c, i * HW:(i + 1) * HW])
                    if i == 0:
                        silu_exp(c)
            take(GATES_TURNED, gt[:])
            act.wait_ge(gate_pre, 1)
            dep(run(lexp, mn, ACT.Exp))
            act.wait_ge(const_in, 16)
            run(lg, lexp, ACT.Ln, bias=ones[:, 0:1]).then_inc(gate_ln, 1)
            for i in range(4):
                take(QA + i, qa[:, i, :])
            act.wait_ge(xc_ready, MH)
            for h in range(MH):
                take(MQ + h, qm[:, h, :], scale=float(ME) ** -0.5)
            for h in range(MH):
                take(MK + h, kmT[:, h, :])
            for h in range(MH):
                take(KM + h, km[:, :, h, :])
            act.wait_ge(r_ready, 1)
            for i in range(4):
                for k in range(i * MH, (i + 1) * MH):
                    run(diag_r[:, i, k % MH, :], ident, ACT.Copy, scale=rr[:, k:k + 1]).then_inc(diag_ready, 1)
                take(KA + i, ka[:, i, :])
            for i in range(2):
                for c in range(NB):
                    take(VA + 4 * i + c, va[:, c, i * HW:(i + 1) * HW])
                    if (i, c) == (1, 2):
                        act.wait_ge(args_ready, 1)
                        run(ew[:].rearrange("p a b -> p (a b)"), ew[:].rearrange("p a b -> p (a b)"),
                            ACT.Exp).then_inc(weights_ready, 1)
            act.wait_ge(weights_ready, 1)

            def turned(n, dst):
                act.wait_ge(pt_done, n + 1)
                src = pt[n % 2][:, 0:dst.free_size()]
                if len(dst.shape) == 3:
                    src = src.rearrange("p (a b) -> p a b", a=dst.shape[1])
                run(dst, src, ACT.Copy).then_inc(pt_copied, 1)

            def decay(c):
                for h in range(MH):
                    k = 4 * c + h
                    last = run(swm[:, h, :], rm[:, c, h, :], ACT.Exp, bias=nmx[:, k:k + 1])
                last.then_inc(mexp_done, 1)
                if c < NB - 1:
                    for h in range(MH):
                        last = run(kw[:, h, :], km[:, c, h, :], ACT.Copy, scale=w_k[:, 4 * c + h:4 * c + h + 1])
                    last.then_inc(kw_ready, 1)

            def mlstm(c, part):
                if (c, part) == (0, 0):
                    act.wait_ge(proj_done, KA)
                    decay(0)
                elif part == 2 and c < NB - 1:
                    decay(c + 1)
                elif part == 1:
                    act.wait_ge(upd_done, c + 1)
                    if c >= 1:
                        act.wait_ge(ml_ready, c)
                    for h in range(MH):
                        last = run(inter[:, h, :], pi[:, h * P:(h + 1) * P], ACT.Copy,
                                   scale=w_inter[:, 4 * c + h:4 * c + h + 1])
                    last.then_inc(inter_scaled, 1)
                    if c >= 1:
                        act.wait_ge(mpv_done, c)
                    turned(turn_item["ml", c, 1], pTm)
                elif part == 3:
                    act.wait_ge(var_ready, c + 1)
                    run(sd[:], mv[:, :, 1], ACT.Sqrt, bias=eps).then_inc(sd_ready, 1)

            def head(c, i):
                if i < AH:
                    g = AH * c + i
                    act.wait_ge(ps_read, score_item["head", c, i] + 1)
                    v = sw[g % 3][:, 0:(c + 1) * P]
                    run(v, v, ACT.Exp, scale=-1.0, bias=hv[:, 0, i:i + 1]).then_inc(aexp_done, 1)
                if 2 <= i <= AH + 1:
                    g = AH * c + i - 2
                    if g >= 2:
                        act.wait_ge(pv_done, g - 1)
                    turned(turn_item["head", c, i - 2], pT[g % 2][:, 0:(c + 1) * P])

            def split_query(q, n):
                act.wait_ge(wq_in[q], n * 16)
                run(wq_hi[q][:], wq[q][:], ACT.Copy).then_inc(wq_hi_ready, 1)

            for kind, c, i in order:
                if kind == "ml":
                    mlstm(c, i)
                elif kind == "om" and i == 0:
                    act.wait_ge(ps_read, score_item["om", c, 0] + 1)
                    dep(run(om[:, c, :], om[:, c, :], ACT.Exp, scale=-1.0))
                    run(om[:, c, :], om[:, c, :], ACT.Identity, bias=ones[:, 0:1]).then_inc(ogate_exp, 1)
                elif kind == "wq":
                    split_query(i, 1)
                elif kind == "head":
                    head(c, i)
                elif kind == "cat":
                    if c >= 1:
                        act.wait_ge(ps_done, score_item["out", c - 1, 1] + 1)
                    turned(turn_item["cat", c, i], catT[:, 4 * i:4 * i + 4, :])
                elif kind == "ln" and i == 0:
                    act.wait_ge(ln_var_ready, c + 1)
                    run(ln_sd[:, 0:1], ln_mv[:, 1:2], ACT.Sqrt, bias=eps).then_inc(ln_sd_ready, 1)
                elif kind == "ln" and i == 1:
                    act.wait_ge(ln_rstd_ready, c + 1)
                    for part in range(2):
                        hh = h1[:, c, part * 512:(part + 1) * 512]
                        run(hh, hh, ACT.Identity, scale=ln_sd[:, 1:2], bias=ln_sd[:, 2:3]).then_inc(ln_norm_ready, 1)
                elif kind == "h1T":
                    turned(turn_item["h1T", c, i], h1T_hi[:, 4 * i:4 * i + 4, c * P:(c + 1) * P])

            act.sem_inc(qry_copied, 2)

            def high_part(j, s):
                act.wait_ge(wd_in[j], s * 16 + 16)
                run(wd_hi[j][:], wd[j][:], ACT.Copy).then_inc(wd_hi_ready, 1)

            def take_query(h, q):
                for side in range(2):
                    act.wait_ge(qry_done, h * 2 + (side + 1))
                    run(qry[q][:, side, :], pj[side][:], ACT.Copy).then_inc(qry_copied, 1)

            with act.Fori(0, PH // 2 - 1, 1) as pair:
                for q in range(2):
                    take_query(pair * 2 + q, q)
                    split_query(q, pair + 2)
            high_part(0, 0)
            for q in range(2):
                take_query(PH - 2 + q, q)

            act.sem_inc(gelu_done, TPS)
            act.sem_inc(gmat_staged, 2)
            act.sem_inc(up_done, 2)
            for q in range(TPS):
                act.sem_inc(act_out[q], 16)
            for q in range(2):
                act.sem_inc(stage_out[q], 16)

            def gelu(s, j):
                n = s * TPS + j
                act.wait_ge(down_done, n + (TPS + 1))
                act.wait_ge(act_out[j], (s + 1) * 16)
                run(gel[j][:], down_banks[j], ACT.Gelu).then_inc(gelu_done, 1)
                act.wait_ge(gelu_done, n + (TPS + 1))
                act.dma_start(act_dram[:, n, :] if isinstance(n, int) else
                              act_dram[:, bass.ds(n, 1), :].rearrange("p a t -> p (a t)"),
                              gel[j][:]).then_inc(act_out[j], 16)

            def step(s, first=False, gates=True, select=True, tiles=TPS, half=0, quarter=0, block=0,
                     store=True, lone=None):
                for j in range(GPS):
                    if j < tiles:
                        if tiles == TPS or j + 1 < tiles:
                            high_part((j + 1) % TPS, s + (j + 1) // TPS)
                        if select and j == 1:
                            act.wait_ge(shifted_ready, s + 1)
                            run(gate_exp[:], shifted[:], ACT.Exp, accum_out=gate_sum[:]).then_inc(gates_ready, 1)
                        if j:
                            gelu(s, j - 1)
                        elif not first:
                            gelu(s - 1, TPS - 1)
                        if j == 1 and gates and store:
                            store_gates(1 - half, (block - 1) * 2 + (half - 1), quarter,
                                        (block - 1) * (PH * GPS) + (half * (PH // 2 * GPS) + 2))
                        if j < 2 and lone is not None:
                            store_gates(1, 2 * NB - 1, lone * 2 + j, GROUPS + 2)
                    if gates:
                        m = (s - PH) * GPS + j
                        act.wait_ge(gmat_done, m + 3)
                        if j == 0:
                            act.wait_ge(stage_out[half], block * 64 - 48)
                        run(stage[half][:, :, bass.ds(quarter * 16 + TOK * j, TOK)],
                            ps[j % 2][:].rearrange("p (t i) -> p i t", t=TOK), ACT.Copy).then_inc(gmat_staged, 1)

            def store_gates(buffer, n, piece, staged):
                act.wait_ge(gmat_staged, staged)
                half_block = (gates_dram[:, n, :] if isinstance(n, int) else
                              gates_dram[:, bass.ds(n, 1), :].rearrange("p a t -> p (a t)"))
                act.dma_start(half_block[:, bass.ds(piece * (PIECE * HALF), PIECE * HALF)],
                              stage[buffer][:].rearrange("p i t -> p (i t)")[
                                  :, bass.ds(piece * (PIECE * HALF), PIECE * HALF)]).then_inc(stage_out[buffer], 16)

            act.wait_ge(sc_copied, 2 + 2 * PH)
            down_steps(act, step)

            def high_parts_up(pair, q):
                act.wait_ge(wu_in[q], pair * 16 + 16)
                act.wait_ge(up_done, pair * 2 + (q + 1))
                run(wu_hi[q][:], wu[q][:], ACT.Copy).then_inc(wu_hi_ready, 1)
                act.wait_ge(ga_ready, pair * 2 + (q + 9))
                run(ga_hi[q][:], ga[q][:], ACT.Copy).then_inc(ga_hi_ready, 1)

            high_parts_up(0, 0)
            gelu(TILES // TPS, REST - 1)
            high_parts_up(0, 1)
            with act.Fori(1, TILES // 2, 1) as pair:
                for q in range(2):
                    high_parts_up(pair, q)
            for b in range(NB):
                act.wait_ge(var2_ready, b + 1)
                run(sd[:, b:b + 1], mv[:, b, 1:2], ACT.Sqrt, bias=eps).then_inc(sd2_ready, 1)
                act.wait_ge(rstd2_ready, b + 1)
                for half in range(2):
                    hh = h1[:, b, half * 512:(half + 1) * 512]
                    run(hh, hh, ACT.Identity, scale=rstd[:, b:b + 1], bias=shift[:, b:b + 1]).then_inc(norm_ready, 1)

        @block.vector
        def _(dve):
            v = nc.vector
            steps = [0]

            def dep(ins):
                steps[0] += 1
                ins.then_inc(dve_step, 1)
                dve.wait_ge(dve_step, steps[0])

            def spread(col, n):
                return col.unsqueeze(2).to_broadcast([P, col.shape[1], n])

            def blocks(ap, n=MH):
                return ap.rearrange("p (a b) -> p a b", a=n)

            def split_x(i):
                dve.wait_ge(x_hi_ready, i + 1)
                part = (slice(None), slice(2 * i, 2 * i + 2), slice(None))
                v.tensor_tensor(x_lo[part], xT_sb[part], x_hi[part].bitcast(F32), ALU.subtract).then_inc(x_lo_ready, 1)

            split_x(0)
            dve.wait_ge(first_hi_ready, 1)
            v.tensor_tensor(wp_lo[0][:, :, 0:P], wp[0][:, :, 0:P], wp_hi[0][:, :, 0:P].bitcast(F32),
                            ALU.subtract).then_inc(first_lo_ready, 1)
            for i in range(1, 4):
                split_x(i)
            dve.wait_ge(wp_hi_ready, 1)
            v.tensor_tensor(wp_lo[0][:, :, P:HW], wp[0][:, :, P:HW], wp_hi[0][:, :, P:HW].bitcast(F32),
                            ALU.subtract).then_inc(wp_lo_ready, 1)
            dve.wait_ge(wg_hi_ready, 1)
            v.tensor_tensor(wg_lo[:], wg_sb[:], wg_hi[:].bitcast(F32), ALU.subtract).then_inc(wg_split, 1)
            dve.wait_ge(small_in, 16 * 7)

            def conv_head(h):
                dve.wait_ge(proj_copied, XM + h + 1)
                y = kmT[:, h, :]
                dep(v.tensor_scalar(y, xm[:, h, 0:S], conv_sb[:, h, 0:1], conv_sb[:, h, TAPS:TAPS + 1],
                                    ALU.mult, ALU.add))
                for j in range(1, TAPS):
                    ins = v.scalar_tensor_tensor(y, xm[:, h, j:j + S], conv_sb[:, h, j:j + 1], y,
                                                 ALU.mult, ALU.add)
                    if j < TAPS - 1:
                        dep(ins)
                ins.then_inc(conv_done, 1)

            def silu(h):
                dve.wait_ge(conv_exp, h + 1)
                dve.wait_ge(conv_done, h + 1)
                dep(v.tensor_scalar(xc[:, h, :], xc[:, h, :], 1.0, None, ALU.add))
                dep(v.reciprocal(xc[:, h, :], xc[:, h, :]))
                v.tensor_tensor(xc[:, h, :], xc[:, h, :], kmT[:, h, :], ALU.mult).then_inc(xc_ready, 1)

            for h in range(MH):
                conv_head(h)
            for h in range(MH):
                silu(h)
            dve.wait_ge(proj_copied, GATES_TURNED + 1)
            g3 = gt[:]
            v.tensor_tensor(ip.rearrange("p (c h) -> p c h", c=NB), g3[:, :, 0:MH],
                            gbias[:, 0:MH].unsqueeze(1).to_broadcast([P, NB, MH]), ALU.add)
            dep(v.tensor_tensor(ff.rearrange("p (c h) -> p c h", c=NB), g3[:, :, MH:2 * MH],
                                gbias[:, MH:2 * MH].unsqueeze(1).to_broadcast([P, NB, MH]), ALU.add))
            dep(v.tensor_scalar(nf, ff, -1.0, None, ALU.mult))
            v.tensor_tensor(mn, nf, ff, ALU.min).then_inc(gate_pre, 1)
            dve.wait_ge(gate_ln, 1)
            dep(v.tensor_scalar(ff, ff, 0.0, None, ALU.min))
            v.tensor_tensor(logf, ff, lg, ALU.subtract).then_inc(logf_ready, 1)
            dve.wait_ge(gate_sums, 1)
            v.tensor_copy(bl, pi[:, 16:32])
            dep(v.tensor_copy(bc, pi[:, 0:16]))
            v.tensor_tensor(rr, ip, bc, ALU.subtract).then_inc(r_ready, 1)
            for c in range(NB):
                dve.wait_ge(ps_done, c + 1)
                if c == 0:
                    dve.wait_ge(proj_done, KA)
                    dve.wait_ge(const_in, 16)
                v.tensor_reduce(rmax[:, 4 * c:4 * c + 4], blocks(ps[c % 2][:]), X, ALU.max)
                dep(v.tensor_tensor(rm[:, c], blocks(ps[c % 2][:]),
                                    tril_bias.unsqueeze(1).to_broadcast([P, MH, P]), ALU.add))
                v.tensor_reduce(mmax[:, 4 * c:4 * c + 4], rm[:, c], X, ALU.max).then_inc(ps_read, 1)
            dep(v.memset(mprev[:, 0:4], 0.0))
            for c in range(NB):
                g = slice(4 * c, 4 * c + 4)
                dep(v.tensor_tensor(mxl[:, g], mprev[:, g], rmax[:, g], ALU.max))
                dep(v.tensor_tensor(mprev[:, 4 * c + 4:4 * c + 8], mxl[:, g], bl[:, g], ALU.add))
            dve.wait_ge(ps_read, NB)
            dep(v.tensor_tensor(mx, mprev[:, 0:16], mmax, ALU.max))
            v.tensor_scalar(nmx, mx, -1.0, None, ALU.mult)
            v.tensor_tensor(w_inter, mprev[:, 0:16], mx, ALU.subtract)
            v.tensor_tensor(a_dec, mprev[:, 0:16], mxl, ALU.subtract)
            v.tensor_tensor(w_k, rr, mxl, ALU.subtract)
            dep(v.tensor_tensor(e_mt, bc, mx, ALU.add))
            v.tensor_scalar(e_mt, e_mt, -1.0, None, ALU.mult).then_inc(args_ready, 1)
            v.memset(ct[:], 0.0)
            v.memset(nst[:], 0.0).then_inc(state_ready, 1)
            dve.wait_ge(weights_ready, 1)

            rs_sum, den, nden = hv[:, 1, 0:4], hv[:, 2, 0:4], hv[:, 3, 0:4]

            def mlstm(c, part):
                k0, g = 4 * c, slice(4 * c, 4 * c + 4)
                if part == 0:
                    n = score_item["ml", c, 0]
                    dve.wait_ge(mexp_done, c + 1)
                    dve.wait_ge(ps_done, n + 1)
                    v.tensor_tensor(swm, swm, blocks(ps[n % 2][:]), ALU.mult).then_inc(ps_read, 1)
                    dve.wait_ge(ps_read, n + 1)
                    dep(v.tensor_reduce(rs_sum, swm, X, ALU.add))
                    dve.sem_inc(mp_ready, 1)
                elif part == 1:
                    dve.wait_ge(upd_done, c + 1)
                    dep(v.tensor_tensor(den, w_inter[:, g], pj[1][:, 0:4], ALU.mult))
                    dep(v.tensor_tensor(den, den, rs_sum, ALU.add))
                    dep(v.tensor_scalar(nden, den, -1.0, None, ALU.mult))
                    dep(v.tensor_tensor(den, den, nden, ALU.max))
                    dep(v.tensor_tensor(den, den, e_mt[:, g], ALU.max))
                    dep(v.reciprocal(den, den))
                    if c < NB - 1:
                        for h in range(MH):
                            dep(v.scalar_tensor_tensor(ct[:, h, :], ct[:, h, :], a_dec[:, k0 + h:k0 + h + 1],
                                                       pj[0][:, h * P:(h + 1) * P], ALU.mult, ALU.add))
                        dep(v.tensor_tensor(nst[:], nst[:], a_dec[:, g], ALU.mult))
                        v.tensor_tensor(nst[:], nst[:], pj[1][:, 4:8], ALU.add).then_inc(state_ready, 1)
                elif part == 3:
                    dve.wait_ge(inter_scaled, c + 1)
                    dve.wait_ge(mpv_done, c + 1)
                    v.tensor_tensor(inter, inter, blocks(pi), ALU.add).then_inc(num_done, 1)
                    dve.wait_ge(num_done, c + 1)
                    dep(v.tensor_tensor(inter, inter, spread(den, ME), ALU.mult))
                    for h in range(MH):
                        dep(v.bn_stats(stats[:, h, :], inter[:, h, :]))
                    for h in range(MH):
                        ins = v.bn_aggr(mv[:, h, :], stats[:, h, :])
                    ins.then_inc(var_ready, 1)
                elif part == 4:
                    dve.wait_ge(sd_ready, c + 1)
                    dve.wait_ge(ogate_ready, c + 1)
                    dep(v.reciprocal(rstd[:], sd[:]))
                    for h in range(MH):
                        ins = v.tensor_scalar(inter[:, h, :], inter[:, h, :],
                                              mv[:, h, 0:1], rstd[:, h:h + 1], ALU.subtract, ALU.mult)
                    dep(ins)
                    v.tensor_tensor(blocks(om[:, c, :]), inter, blocks(om[:, c, :]), ALU.mult).then_inc(ml_ready, 1)

            def head(c, i):
                wide = slice(0, (c + 1) * P)
                off = slice((NB - 1 - c) * P, S)
                if i < AH:
                    n, g = score_item["head", c, i], AH * c + i
                    dve.wait_ge(ps_done, n + 1)
                    if g >= 3:
                        before = turn_item["head", (g - 3) // AH, (g - 3) % AH]
                        dve.wait_ge(pt_done, before + 1)
                    s = sw[g % 3][:, wide]
                    v.tensor_tensor_reduce(out=s, in0=ps[n % 2][:, wide], in1=attn_bias[:, off],
                                           scale=-float(AE) ** -0.5, scalar=-LOWEST, op0=ALU.add, op1=ALU.min,
                                           accum_out=hv[:, 0, i:i + 1]).then_inc(ps_read, 1)
                if 1 <= i <= AH:
                    g = AH * c + i - 1
                    dve.wait_ge(aexp_done, g + 1)
                    s = sw[g % 3][:, wide]
                    v.tensor_tensor_reduce(out=s, in0=s, in1=attn_count[:, off], scale=1.0, scalar=0.0,
                                           op0=ALU.mult, op1=ALU.add,
                                           accum_out=hv[:, 5, i - 1:i]).then_inc(ap_ready, 1)
                if i == AH + 2:
                    dve.wait_ge(ap_ready, AH * (c + 1))
                    dep(v.reciprocal(hv[:, 6, :], hv[:, 5, :]))
                    dve.wait_ge(pv_done, AH * (c + 1))
                    if c >= 1:
                        dve.wait_ge(pt_done, turn_item["cat", c - 1, 0] + 1)
                    v.tensor_tensor(blocks(cat[:], AH), blocks(po, AH), spread(hv[:, 6, :], AE),
                                    ALU.mult).then_inc(cat_ready, 1)

            def layer_norm(c, part):
                hb = h1[:, c, :]
                if part == 0:
                    v.bn_aggr(ln_mv[:], ln_stats[:]).then_inc(ln_var_ready, 1)
                elif part == 1:
                    dve.wait_ge(ln_sd_ready, c + 1)
                    dep(v.reciprocal(ln_sd[:, 1:2], ln_sd[:, 0:1]))
                    v.tensor_scalar(ln_sd[:, 2:3], ln_mv[:, 0:1], ln_sd[:, 1:2], -1.0,
                                    ALU.mult, ALU.mult).then_inc(ln_rstd_ready, 1)
                else:
                    for half in range(2):
                        cs = slice(half * 512, (half + 1) * 512)
                        dve.wait_ge(ln_norm_ready, 2 * c + half + 1)
                        ins = v.tensor_tensor(hb[:, cs], hb[:, cs], ln1_sb[:, 0, cs], ALU.mult)
                        if c < NB - 1:
                            ins.then_inc(ln_scaled, 1)
                        else:
                            dep(ins)
                            v.tensor_tensor(hb[:, cs], hb[:, cs], ln1_sb[:, 1, cs], ALU.add).then_inc(h1_ready, 1)

            def split_query(q, n):
                dve.wait_ge(wq_hi_ready, n)
                v.tensor_tensor(wq_lo[q][:], wq[q][:], wq_hi[q][:].bitcast(F32),
                                ALU.subtract).then_inc(wq_lo_ready, 1)

            for kind, c, i in order:
                if kind == "ml":
                    mlstm(c, i)
                elif kind == "head":
                    head(c, i)
                elif kind == "om" and i == 0:
                    n = score_item["om", c, 0]
                    dve.wait_ge(ps_done, n + 1)
                    v.tensor_copy(om[:, c, :], ps[n % 2][:]).then_inc(ps_read, 1)
                elif kind == "om":
                    o = om[:, c, (i - 1) * ME:i * ME]
                    dve.wait_ge(ogate_exp, c + 1)
                    v.reciprocal(o, o).then_inc(sigmoid_ready, 1)
                elif kind == "wq":
                    dve.wait_ge(mpv_done, NB)
                    dve.wait_ge(ps_done, score_item["head", NB - 1, AH - 1] + 1)
                    split_query(i, i + 1)
                elif kind == "out":
                    n = score_item["out", c, i]
                    dve.wait_ge(x_in, 16 * NB)
                    dve.wait_ge(ps_done, n + 1)
                    hh = h1[:, c, i * 512:(i + 1) * 512]
                    v.scalar_tensor_tensor(hh, hh, ALPHA, ps[n % 2][:], ALU.mult, ALU.add).then_inc(ps_read, 1)
                    dve.wait_ge(ps_read, n + 1)
                    dep(v.bn_stats(ln_stats[:, i, :], hh))
                elif kind == "ln":
                    layer_norm(c, i)
                elif kind == "h1T":
                    n = turn_item["h1T", c, i]
                    dve.wait_ge(pt_copied, n + 1)
                    part = (slice(None), slice(4 * i, 4 * i + 4), slice(c * P, (c + 1) * P))
                    v.tensor_tensor(h1T_lo[part], blocks(pt[n % 2][:]), h1T_hi[part].bitcast(F32),
                                    ALU.subtract).then_inc(h1T_split, 1)

            dve.wait_ge(pt_copied, turn_items)
            dve.sem_inc(sc_copied, 2)
            s4 = scores[:].rearrange("p (b h) n -> p b (h n)", b=NB)

            def keep_scores(h):
                for half in range(2):
                    dve.wait_ge(sc_done, h * 2 + (half + 1))
                    v.tensor_copy(s4[:, 2 * half:2 * half + 2, bass.ds(h * (2 * NK), 2 * NK)],
                                  ps[half][:].rearrange("p (b n) -> p b n", b=2)).then_inc(sc_copied, 1)

            dve.sem_inc(down_done, TPS)
            with dve.Fori(0, PH // 2 - 1, 1) as pair:
                for q in range(2):
                    split_query(q, pair * 2 + (q + 3))
                    keep_scores(pair * 2 + q)
            for h in range(PH - 2, PH):
                keep_scores(h)
            dve.wait_ge(sc_copied, 2 + 2 * PH)

            def top16(src, src2, vals, inds, dep):
                dep(v.max(vals[:, 0:8], src))
                dep(v.max_index(inds[:, 0:8], vals[:, 0:8], src))
                dep(v.match_replace(src2, vals[:, 0:8], src, LOWEST))
                dep(v.max(vals[:, 8:16], src2))
                dep(v.max_index(inds[:, 8:16], vals[:, 8:16], src2))

            def stand_alone():
                dve.sem_inc(dve_alone, 1)

            dve.sem_inc(gmat_done, 2)

            ranks = iota16.unsqueeze(1).to_broadcast([P, TOPK, TOPK])

            def step(s, first=False, gates=True, select=True, tiles=TPS, half=0, quarter=0, block=0,
                     store=True, lone=None):
                count = [0]

                def dep(ins):
                    count[0] += 1
                    ins.then_inc(loop_step, 1)
                    dve.wait_ge(loop_step, count[0])

                def select_part(part):
                    if part == 0:
                        dep(v.tensor_copy(sc[:], (scores[:, s, :] if isinstance(s, int) else
                                                  scores[:, bass.ds(s, 1), :].rearrange("p a n -> p (a n)"))
                                          .rearrange("p (s n) -> p s n", s=2)))
                    if part < 2:
                        top16(sc[:, part, :], sc2[:, part, :], top[:, part, :], topi[:, part, :], dep)
                    elif part == 2:
                        dep(v.tensor_tensor(cand[:].rearrange("p (i j) -> p i j", i=TOPK),
                                            top[:, 0, :].unsqueeze(2).to_broadcast([P, TOPK, TOPK]),
                                            top[:, 1, :].unsqueeze(1).to_broadcast([P, TOPK, TOPK]), ALU.add))
                        top16(cand[:], cand2[:], best[:], pos[:], dep)
                        v.tensor_scalar(shifted[:], best[:], best[:, 0:1], None, ALU.subtract).then_inc(shifted_ready, 1)
                    else:
                        v.tensor_scalar(hl[:, 0, :], pos[:], 4, None, ALU.logical_shift_right)
                        dep(v.tensor_scalar(hl[:, 1, :], pos[:], 15, None, ALU.bitwise_and))
                        for side in range(2):
                            ins = v.tensor_tensor(eq[:, side], ranks,
                                                  hl[:, side, :].unsqueeze(2).to_broadcast([P, TOPK, TOPK]),
                                                  ALU.is_equal)
                        dep(ins)
                        for side in range(2):
                            ins = v.tensor_tensor(eq[:, side], eq[:, side],
                                                  topi[:, side, :].unsqueeze(1).to_broadcast([P, TOPK, TOPK]),
                                                  ALU.mult)
                        dep(ins)
                        dep(v.tensor_reduce(e12g[:, 0:2, :], eq[:], X, ALU.add))
                        dve.wait_ge(gates_ready, s + 1)
                        dep(v.reciprocal(gate_rs[:], gate_sum[:]))
                        dep(v.tensor_scalar(e12g[:, 2, :], gate_exp[:], gate_rs[:], None, ALU.mult))
                        head = s if isinstance(s, int) else (s if not gates else quarter + half * (PH // 2))
                        v.tensor_copy(picks[:, :, bass.ds(head * TOPK, TOPK)], e12g[:]).then_inc(picks_ready, 1)

                if gates:
                    dep(v.tensor_copy(cols[:], picksT[:, :, bass.ds(quarter * 16 + half * HALF, 16)]))
                for j in range(TPS):
                    for group in ((0,), (1,), (2, 3))[j] if gates else ():
                        m = (s - PH) * GPS + group
                        dve.wait_ge(gmat_done, m + 1)
                        v.tensor_tensor(hot2[:, group % 2], iota128.unsqueeze(1).to_broadcast([P, TOK, P]),
                                        cols[:, 1, group * TOK:(group + 1) * TOK].unsqueeze(2)
                                        .to_broadcast([P, TOK, P]), ALU.is_equal)
                        for r in range(TOK):
                            t = TOK * group + r
                            last = v.tensor_scalar(hot1[:, group % 2, r, :], iota128, cols[:, 0, t:t + 1],
                                                   cols[:, 2, t:t + 1], ALU.is_equal, ALU.mult)
                        last.then_inc(hot_ready, 1)
                    for part in ((0, 1), (2,), (3,))[j] if select else ():
                        select_part(part)
                if select:
                    dve.wait_ge(picks_ready, s + 1)
                if gates:
                    dve.wait_ge(hot_ready, (s - PH) * GPS + GPS)
                stand_alone()
                dve.sem_clear(loop_step)

            def keep_turned(g):
                dve.wait_ge(turned_ready, g + 1)
                v.tensor_copy(picksT[:], pt[0][:, 0:3 * P].rearrange("p (a b) -> p a b", a=3)).then_inc(picksT_ready, 1)
                dve.wait_ge(picksT_ready, g + 1)
                stand_alone()

            down_steps(dve, step, after_group=keep_turned)

            dve.wait_ge(gmat_done, 2 + GROUPS)
            dve.sem_inc(wu_lo_ready, 2)
            dve.sem_inc(ga_ready, 2 * UTS)
            with dve.Fori(0, TILES // UTS // 2, 1) as pair:
                for q in range(2):
                    for j in range(UTS):
                        n = pair * (2 * UTS) + (q * UTS + j)
                        if j == 0:
                            dve.wait_ge(ga_in[q], pair * 32 + 32)
                        v.tensor_tensor(ga[j % 2][:].rearrange("p (n t) -> p n t", t=HALF),
                                        acts[q][:, j, :].rearrange("p (n t) -> p n t", t=HALF),
                                        gts[q][:, :, j, :], ALU.mult).then_inc(ga_ready, 1)
                        dve.wait_ge(wu_hi_ready, n + 1)
                        v.tensor_tensor(wu_lo[j % 2][:], wu[j % 2][:], wu_hi[j % 2][:].bitcast(F32),
                                        ALU.subtract).then_inc(wu_lo_ready, 1)
                        dve.wait_ge(ga_hi_ready, n + 1)
                        v.tensor_tensor(ga_lo[j % 2][:], ga[j % 2][:], ga_hi[j % 2][:].bitcast(F32),
                                        ALU.subtract).then_inc(ga_lo_ready, 1)

            banks = [[pj[0], pj[1]], [ps[0], ps[1]], [pt[0], pt[1]], [py[:, 0, :], py[:, 1, :]]]
            dve.wait_ge(ln2_in, 32)
            def residual(b):
                dve.wait_ge(block_done, b + 1)
                for i in range(2):
                    hh = h1[:, b, i * 512:(i + 1) * 512]
                    dep(v.scalar_tensor_tensor(hh, hh, ALPHA, banks[b][i][:, 0:512], ALU.mult, ALU.add))
                    dep(v.bn_stats(stats[:, 2 * (b % 2) + i, :], hh))
                v.bn_aggr(mv[:, b, :], stats[:, 2 * (b % 2):2 * (b % 2) + 2, :]).then_inc(var2_ready, 1)

            residual(0)
            for b in range(NB):
                dve.wait_ge(sd2_ready, b + 1)
                dep(v.reciprocal(rstd[:, b:b + 1], sd[:, b:b + 1]))
                v.tensor_scalar(shift[:, b:b + 1], mv[:, b, 0:1], rstd[:, b:b + 1], -1.0,
                                ALU.mult, ALU.mult).then_inc(rstd2_ready, 1)
                if b + 1 < NB:
                    residual(b + 1)
                for half in range(2):
                    cs = slice(half * 512, (half + 1) * 512)
                    dve.wait_ge(norm_ready, 2 * b + half + 1)
                    v.tensor_tensor(h1[:, b, cs], h1[:, b, cs], ln2_sb[:, 0, cs], ALU.mult).then_inc(scaled_ready, 1)

        @block.gpsimd
        def _(pool):
            nc.gpsimd.memset(xm[:, :, 0:TAPS - 1], 0.0).then_inc(pads_zero, 1)
            pool.wait_ge(wp_lo_ready, 1)
            for n in range(1, PIECES):
                pool.wait_ge(wp_hi_ready, n + 1)
                nc.gpsimd.tensor_tensor(wp_lo[n % 4][:], wp[n % 4][:], wp_hi[n % 2][:].bitcast(F32),
                                        ALU.subtract).then_inc(wp_lo_ready, 1)

            pool.wait_ge(small_in, 16 * 7)
            for kind, c, i in order:
                if kind == "om" and i == MH:
                    pool.wait_ge(sigmoid_ready, MH * (c + 1))
                    nc.gpsimd.tensor_tensor(om[:, c, :], om[:, c, :], mhg[:], ALU.mult).then_inc(ogate_ready, 1)
                elif kind == "ln" and i == 2 and c < NB - 1:
                    for half in range(2):
                        cs = slice(half * 512, (half + 1) * 512)
                        pool.wait_ge(ln_scaled, 2 * c + half + 1)
                        nc.gpsimd.tensor_tensor(h1[:, c, cs], h1[:, c, cs], ln1_sb[:, 1, cs],
                                                ALU.add).then_inc(h1_ready, 1)

            def low_part(n, j):
                pool.wait_ge(wd_hi_ready, n + 1)
                nc.gpsimd.tensor_tensor(wd_lo[j][:], wd[j][:], wd_hi[j][:].bitcast(F32),
                                        ALU.subtract).then_inc(wd_lo_ready, 1)

            with pool.Fori(0, TILES // TPS, 1) as s:
                for j in range(TPS):
                    low_part(s * TPS + j, j)
            for j in range(REST):
                low_part(TILES - REST + j, j)
            for n in range(2 * NB):
                b, cs = n // 2, slice(n % 2 * 512, (n % 2 + 1) * 512)
                pool.wait_ge(scaled_ready, n + 1)
                nc.gpsimd.tensor_tensor(h1[:, b, cs], h1[:, b, cs], ln2_sb[:, 1, cs], ALU.add).then_inc(out_ready, 1)


def shape_constants():
    import numpy as np
    t, s = np.arange(P)[:, None], np.arange(P)[None, :]
    dist = t - (np.arange(S)[None, :] - (S - P))
    count = (((dist >= 0) & (dist <= 128)).astype(np.float32)
             + ((dist >= 0) & (dist % 4 == 0) & (dist <= 512)) + ((dist >= 0) & (dist % 16 == 0)))
    tail = np.zeros((P, 32), np.float32)
    tail[:, 0:16] = np.arange(16)
    tail[:, 16] = EPS
    return np.concatenate([np.eye(P), (t <= s), np.ones((P, P)), np.where(s <= t, 0.0, NEG),
                           np.where(count > 0, 0.0, NEG), count, tail,
                           np.broadcast_to(np.arange(P), (P, P))], axis=1).astype(np.float32)


def kernel(**inputs):
    import numpy as _np
    import concourse.bacc as _bacc
    from concourse import mybir as _mybir
    from concourse.bass_utils import run_bass_kernel_spmd as _run

    a = {k: _np.asarray(v) for k, v in inputs.items()}
    x = a["x"][0]
    w_in = a["w_in"][0]
    conv = _np.concatenate([a["conv_w"][0], a["conv_b"]], axis=0)
    laid = {
        "xT": x.T,
        "x": x,
        "w_in": w_in[:, :6 * W],
        "w_gate": w_in[:, 6 * W:].reshape(KD, P, 2 * MH).transpose(1, 0, 2),
        "conv": conv.reshape(TAPS + 1, MH, ME).transpose(2, 1, 0),
        "gate_bias": _np.concatenate([a["b_igate"], a["b_fgate"]], axis=1),
        "w_mq": a["w_mq"][0],
        "w_mk": a["w_mk"][0],
        "mh_g": a["mh_norm_g"],
        "w_out": a["w_out"][0],
        "ln1": _np.concatenate([a["ln1_g"], a["ln1_b"]], axis=0),
        "w_query": a["peer_w_query"][0],
        "sub_keys": a["peer_sub_keys"][0].transpose(3, 0, 1, 2).reshape(P, PH * 2, NK),
        "w_downT": a["peer_w_down"][0].reshape(NK, NK, KD, P).transpose(0, 3, 2, 1).reshape(NK * P, KD * NK),
        "w_up": a["peer_w_up"][0],
        "ln2": _np.concatenate([a["ln2_g"], a["ln2_b"]], axis=0),
        "consts": shape_constants(),
    }
    nc = _bacc.Bacc("TRN2", target_bir_lowering=False, num_devices=1)
    arrays, args = {}, []
    for name, v in laid.items():
        arrays[f"in_{name}"] = _np.ascontiguousarray(v)
        args.append(nc.dram_tensor(f"in_{name}", v.shape, _mybir.dt.from_np(v.dtype), kind="ExternalInput").ap())
    args.append(nc.dram_tensor("gates_dram", (P, 2 * NB, NK * HALF), F32).ap())
    args.append(nc.dram_tensor("act_dram", (P, TILES, S), F32).ap())
    args.append(nc.dram_tensor("out_0", (S, D), F32, kind="ExternalOutput").ap())
    build(nc, *args)
    r = _run(nc, [arrays], core_ids=[0])
    return _np.asarray(r.results[0]["out_0"]).reshape(1, S, D)
```
